# Optimizing a Trainium2 kernel written in Bass

```python
import functools
import jax
import jax.numpy as jnp
from jax import lax
import numpy as np

D_MODEL = 2048
BATCH = 1
SEQ = 256
DEPTH = 1
DEC_BATCH = 8
DEC_SEQ = 4
PAST_LEN = 1024
PAGE_SIZE = 128

GLA_HEADS = 4
GLA_DK = D_MODEL // 16
GLA_DV = D_MODEL // 8
GLA_GATE_RANK = 16
GLA_TAU = 16.0
GLA_CHUNK = 32
FOX_HEADS = 8
FOX_DH = D_MODEL // 16
Q_BLOCK = 128
N_GROUPS = 4
EXPERTS_PER_GROUP = 4
N_EXPERTS = N_GROUPS * EXPERTS_PER_GROUP
TOP_K_IN_GROUP = 2
D_EXPERT = D_MODEL // 4
RMS_EPS = 1e-6

GLA_KW = GLA_HEADS * GLA_DK
GLA_VW = GLA_HEADS * GLA_DV
FOX_W = FOX_HEADS * FOX_DH
IN_SPLIT = (GLA_KW, GLA_KW, GLA_VW, GLA_VW, GLA_GATE_RANK, FOX_W, FOX_W, FOX_W, FOX_HEADS, D_MODEL, D_MODEL)
D_IN = sum(IN_SPLIT)

kernel_name = 'hybrid_gla_fox_hmoe_step'

def rmsnorm(x, g):
    x32 = x.astype(jnp.float32)
    y = x32 * lax.rsqrt(jnp.mean(x32 * x32, axis=-1, keepdims=True) + RMS_EPS)
    return (y * g.astype(jnp.float32)).astype(x.dtype)

def adaln(c, w_ada, b_ada):
    mod = jax.nn.silu(c) @ w_ada + b_ada
    return jnp.split(mod[:, None, :], 6, axis=-1)

def modulate(h, shift, scale):
    return h * (1.0 + scale) + shift

def mixer_inputs(h, w_in, w_a2, b_a, b_f):
    B, L, _ = h.shape
    offs = [int(o) for o in np.cumsum(IN_SPLIT)[:-1]]
    qa, ka, va, ra, lra, qb, kb, vb, fb, ga, gb = jnp.split(h @ w_in, offs, axis=-1)
    qa = qa.reshape(B, L, GLA_HEADS, GLA_DK) * (GLA_DK ** -0.5)
    ka = ka.reshape(B, L, GLA_HEADS, GLA_DK)
    va = va.reshape(B, L, GLA_HEADS, GLA_DV)
    ra = ra.reshape(B, L, GLA_HEADS, GLA_DV)
    log_a = (jax.nn.log_sigmoid((lra @ w_a2 + b_a).astype(jnp.float32)) / GLA_TAU).reshape(B, L, GLA_HEADS, GLA_DK)
    qb = qb.reshape(B, L, FOX_HEADS, FOX_DH)
    kb = kb.reshape(B, L, FOX_HEADS, FOX_DH)
    vb = vb.reshape(B, L, FOX_HEADS, FOX_DH)
    logf = jax.nn.log_sigmoid((fb + b_f).astype(jnp.float32))
    return qa, ka, va, ra, log_a, qb, kb, vb, logf, ga, gb

def gla_chunked(q, k, v, log_a, s0, chunk):
    B, L, H, DK = q.shape
    DV = v.shape[-1]
    n = L // chunk
    f32 = jnp.float32
    qc = q.astype(f32).reshape(B, n, chunk, H, DK)
    kc = k.astype(f32).reshape(B, n, chunk, H, DK)
    vc = v.astype(f32).reshape(B, n, chunk, H, DV)
    cum = jnp.cumsum(log_a.astype(f32).reshape(B, n, chunk, H, DK), axis=2)
    causal = jnp.tril(jnp.ones((chunk, chunk), dtype=bool))[None, None, :, :, None, None]
    rel = jnp.where(causal, cum[:, :, :, None] - cum[:, :, None, :], -jnp.inf)
    scores = jnp.einsum('bnthd,bnshd,bntshd->bntsh', qc, kc, jnp.exp(rel))
    o_intra = jnp.einsum('bntsh,bnshv->bnthv', scores, vc)
    last = cum[:, :, -1]
    upd = jnp.einsum('bnshd,bnshv->bnhdv', kc * jnp.exp(last[:, :, None] - cum), vc)

    def step(s, inp):
        decay, u = inp
        return decay[..., None] * s + u, s

    s_final, s_prev = lax.scan(step, s0.astype(f32),
                               (jnp.moveaxis(jnp.exp(last), 1, 0), jnp.moveaxis(upd, 1, 0)))
    o_inter = jnp.einsum('bnthd,nbhdv->bnthv', qc * jnp.exp(cum), s_prev)
    return (o_intra + o_inter).reshape(B, L, H, DV), s_final

def fox_prompt(q, k, v, logf):
    B, L, H, Dh = q.shape
    nb = L // Q_BLOCK
    Ft = jnp.cumsum(logf.astype(jnp.float32), axis=1).transpose(0, 2, 1)
    q_blocks = jnp.moveaxis(q.reshape(B, nb, Q_BLOCK, H, Dh), 1, 0)
    f_blocks = jnp.moveaxis(Ft.reshape(B, H, nb, Q_BLOCK), 2, 0)
    pos_blocks = jnp.arange(L).reshape(nb, Q_BLOCK)
    key_pos = jnp.arange(L)
    scale = FOX_DH ** -0.5

    def block(args):
        qi, fi, pi = args
        s = jnp.einsum('bqhd,bkhd->bhqk', qi, k).astype(jnp.float32) * scale
        s = s + fi[..., None] - Ft[:, :, None, :]
        s = jnp.where((pi[:, None] >= key_pos[None, :])[None, None], s, -jnp.inf)
        p = jax.nn.softmax(s, axis=-1).astype(v.dtype)
        return jnp.einsum('bhqk,bkhd->bqhd', p, v)

    o = lax.map(block, (q_blocks, f_blocks, pos_blocks))
    return jnp.moveaxis(o, 0, 1).reshape(B, L, H, Dh)

def fox_sample(q, k_new, v_new, logf_new, cache_k, cache_v, cache_logf, page_table):
    DB, T, H, Dh = q.shape
    k_past = cache_k[page_table].reshape(DB, -1, H, Dh)
    v_past = cache_v[page_table].reshape(DB, -1, H, Dh)
    lf_past = cache_logf[page_table].reshape(DB, -1, H).astype(jnp.float32)
    P = k_past.shape[1]
    R = (lax.cumsum(lf_past, axis=1, reverse=True) - lf_past).transpose(0, 2, 1)
    Fn = jnp.cumsum(logf_new.astype(jnp.float32), axis=1).transpose(0, 2, 1)
    scale = FOX_DH ** -0.5
    s_past = jnp.einsum('bqhd,bkhd->bhqk', q, k_past).astype(jnp.float32) * scale
    s_past = s_past + Fn[..., None] + R[:, :, None, :]
    s_new = jnp.einsum('bqhd,bkhd->bhqk', q, k_new).astype(jnp.float32) * scale
    s_new = s_new + Fn[..., :, None] - Fn[..., None, :]
    s_new = jnp.where(jnp.tril(jnp.ones((T, T), dtype=bool))[None, None], s_new, -jnp.inf)
    p = jax.nn.softmax(jnp.concatenate([s_past, s_new], axis=-1), axis=-1).astype(v_new.dtype)
    return (jnp.einsum('bhqk,bkhd->bqhd', p[..., :P], v_past)
            + jnp.einsum('bhqk,bkhd->bqhd', p[..., P:], v_new))

def mixer_output(o_gla, ra, o_fox, ga, gb, g_gla_norm, w_up_a, w_up_b, w_out):
    B, L = o_gla.shape[:2]
    o_gla = rmsnorm(o_gla.astype(ra.dtype), g_gla_norm) * jax.nn.silu(ra)
    u_a = o_gla.reshape(B, L, GLA_VW) @ w_up_a
    u_b = o_fox.reshape(B, L, FOX_W) @ w_up_b
    merged = jax.nn.sigmoid(ga) * u_a + jax.nn.sigmoid(gb) * u_b
    return merged @ w_out

def hier_moe(h, w_grp, b_grp, w_exp, b_exp, w_gate_e, w_up_e, w_down_e):
    B, L, D = h.shape
    t = h.reshape(-1, D)
    g_logits = (t @ w_grp + b_grp).astype(jnp.float32)
    g_prob = jax.nn.softmax(g_logits, axis=-1)
    _, g_idx = lax.top_k(g_logits, 1)
    g_onehot = jax.nn.one_hot(g_idx[:, 0], N_GROUPS, dtype=jnp.float32)
    g_w = jnp.sum(g_prob * g_onehot, axis=-1, keepdims=True)
    e_logits = (t @ w_exp + b_exp).astype(jnp.float32).reshape(-1, N_GROUPS, EXPERTS_PER_GROUP)
    e_in_group = jnp.einsum('tge,tg->te', e_logits, g_onehot)
    top_v, top_i = lax.top_k(e_in_group, TOP_K_IN_GROUP)
    top_w = jax.nn.softmax(top_v, axis=-1) * g_w
    expert_id = g_idx * EXPERTS_PER_GROUP + top_i
    combine = jnp.sum(jax.nn.one_hot(expert_id, N_EXPERTS, dtype=jnp.float32) * top_w[..., None], axis=1)
    a = jnp.einsum('td,edf->tef', t, w_gate_e)
    u = jnp.einsum('td,edf->tef', t, w_up_e)
    hid = jax.nn.silu(a) * u * combine[..., None].astype(t.dtype)
    return jnp.einsum('tef,efd->td', hid, w_down_e).reshape(B, L, D)

def trunk_layer(x, c, gla_s0, gla_chunk, fox_attend, w_ada, b_ada, g_norm1, g_norm2, w_in, w_a2, b_a, b_f,
                g_gla_norm, w_up_a, w_up_b, w_out, w_grp, b_grp, w_exp, b_exp, w_gate_e, w_up_e, w_down_e):
    sh1, sc1, gt1, sh2, sc2, gt2 = adaln(c, w_ada, b_ada)
    h = modulate(rmsnorm(x, g_norm1), sh1, sc1)
    qa, ka, va, ra, log_a, qb, kb, vb, logf, ga, gb = mixer_inputs(h, w_in, w_a2, b_a, b_f)
    o_a, s_new = gla_chunked(qa, ka, va, log_a, gla_s0, gla_chunk)
    o_b = fox_attend(qb, kb, vb, logf)
    x = x + gt1 * mixer_output(o_a, ra, o_b, ga, gb, g_gla_norm, w_up_a, w_up_b, w_out)
    h2 = modulate(rmsnorm(x, g_norm2), sh2, sc2)
    x = x + gt2 * hier_moe(h2, w_grp, b_grp, w_exp, b_exp, w_gate_e, w_up_e, w_down_e)
    return x, kb, vb, logf, s_new

def setup_inputs(seed: int = 0) -> dict:
    key = jax.random.key(seed)
    ks = jax.random.split(key, 40)
    f32 = jnp.float32

    def nrm(i, shape, scale=1.0):
        return scale * jax.random.normal(ks[i], shape, f32)

    n_pages = PAST_LEN // PAGE_SIZE
    n_used = DEC_BATCH * n_pages
    n_pool = n_used + max(1, n_used // 4)
    page_table = jax.random.permutation(ks[0], n_pool)[:n_used].reshape(DEC_BATCH, n_pages).astype(jnp.int32)
    D = D_MODEL
    return {
        'x_prompt': nrm(1, (BATCH, SEQ, D)),
        'x_sample': nrm(2, (DEC_BATCH, DEC_SEQ, D)),
        'cache_k': nrm(3, (DEPTH, n_pool, PAGE_SIZE, FOX_HEADS, FOX_DH)),
        'cache_v': nrm(4, (DEPTH, n_pool, PAGE_SIZE, FOX_HEADS, FOX_DH)),
        'cache_logf': jax.nn.log_sigmoid(6.0 + nrm(5, (DEPTH, n_pool, PAGE_SIZE, FOX_HEADS), 0.5)),
        'state_gla': nrm(6, (DEPTH, DEC_BATCH, GLA_HEADS, GLA_DK, GLA_DV), 2.0),
        'page_table': page_table,
        'c_prompt': nrm(7, (BATCH, D)),
        'c_sample': nrm(8, (DEC_BATCH, D)),
        'w_ada': nrm(9, (DEPTH, D, 6 * D), D ** -0.5),
        'b_ada': nrm(10, (DEPTH, 6 * D), 0.02),
        'g_norm1': 1.0 + nrm(11, (DEPTH, D), 0.02),
        'g_norm2': 1.0 + nrm(12, (DEPTH, D), 0.02),
        'g_final': 1.0 + nrm(13, (D,), 0.02),
        'w_in': nrm(14, (DEPTH, D, D_IN), D ** -0.5),
        'w_a2': nrm(15, (DEPTH, GLA_GATE_RANK, GLA_KW), GLA_GATE_RANK ** -0.5),
        'b_a': nrm(16, (DEPTH, GLA_KW), 0.02),
        'b_f': 5.0 + nrm(17, (DEPTH, FOX_HEADS), 0.1),
        'g_gla_norm': 1.0 + nrm(18, (DEPTH, GLA_DV), 0.02),
        'w_up_a': nrm(19, (DEPTH, GLA_VW, D), GLA_VW ** -0.5),
        'w_up_b': nrm(20, (DEPTH, FOX_W, D), FOX_W ** -0.5),
        'w_out': nrm(21, (DEPTH, D, D), D ** -0.5),
        'w_grp': nrm(22, (DEPTH, D, N_GROUPS), D ** -0.5),
        'b_grp': nrm(23, (DEPTH, N_GROUPS), 0.01),
        'w_exp': nrm(24, (DEPTH, D, N_EXPERTS), D ** -0.5),
        'b_exp': nrm(25, (DEPTH, N_EXPERTS), 0.01),
        'w_gate_e': nrm(26, (DEPTH, N_EXPERTS, D, D_EXPERT), D ** -0.5),
        'w_up_e': nrm(27, (DEPTH, N_EXPERTS, D, D_EXPERT), D ** -0.5),
        'w_down_e': nrm(28, (DEPTH, N_EXPERTS, D_EXPERT, D), D_EXPERT ** -0.5),
    }

def reference(x_prompt, x_sample, cache_k, cache_v, cache_logf, state_gla, page_table, c_prompt, c_sample,
              w_ada, b_ada, g_norm1, g_norm2, g_final, w_in, w_a2, b_a, b_f, g_gla_norm, w_up_a, w_up_b, w_out,
              w_grp, b_grp, w_exp, b_exp, w_gate_e, w_up_e, w_down_e):
    xp, xs = x_prompt, x_sample
    kp_l, vp_l, fp_l, sp_l = [], [], [], []
    ks_l, vs_l, fs_l, ss_l = [], [], [], []
    for l in range(DEPTH):
        weights = (w_ada[l], b_ada[l], g_norm1[l], g_norm2[l], w_in[l], w_a2[l], b_a[l], b_f[l], g_gla_norm[l],
                   w_up_a[l], w_up_b[l], w_out[l], w_grp[l], b_grp[l], w_exp[l], b_exp[l],
                   w_gate_e[l], w_up_e[l], w_down_e[l])
        s0 = jnp.zeros((xp.shape[0], GLA_HEADS, GLA_DK, GLA_DV), jnp.float32)
        xp, kp, vp, fp, sp = trunk_layer(xp, c_prompt, s0, GLA_CHUNK, fox_prompt, *weights)
        attend = functools.partial(fox_sample, cache_k=cache_k[l], cache_v=cache_v[l],
                                   cache_logf=cache_logf[l], page_table=page_table)
        xs, ks_, vs_, fs_, ss_ = trunk_layer(xs, c_sample, state_gla[l], xs.shape[1], attend, *weights)
        kp_l.append(kp); vp_l.append(vp); fp_l.append(fp); sp_l.append(sp)
        ks_l.append(ks_); vs_l.append(vs_); fs_l.append(fs_); ss_l.append(ss_)
    y_prompt = rmsnorm(xp, g_final)
    y_sample = rmsnorm(xs, g_final)
    return (y_prompt, y_sample, jnp.stack(kp_l), jnp.stack(vp_l), jnp.stack(fp_l), jnp.stack(sp_l),
            jnp.stack(ks_l), jnp.stack(vs_l), jnp.stack(fs_l), jnp.stack(ss_l))


_drawn_inputs = setup_inputs


def setup_inputs(seed=0):
    import zlib

    import numpy as np

    out = dict(_drawn_inputs(seed))
    spreads = {}
    factors = {'cache_logf': 64.0,
     'g_norm1': 2.731,
     'g_final': 7.687,
     'b_a': 5.158,
     'g_gla_norm': 22.421,
     'b_grp': 45.536,
     'b_exp': 34.824,
     'g_norm2': 8.0,
     'b_f': 3.238}
    for name, (base, spread) in spreads.items():
        noise = np.random.default_rng([zlib.crc32(name.encode()), seed]).standard_normal(out[name].shape)
        drawn = base * np.exp(spread * noise) if base else spread * noise
        out[name] = jnp.asarray(drawn.astype(out[name].dtype))
    for name, factor in factors.items():
        out[name] = (out[name] * factor).astype(out[name].dtype)
    return out
```

```python
from contextlib import ExitStack

import concourse.bass as bass
from concourse import mybir

ALU = mybir.AluOpType
ACT = mybir.ActivationFunctionType
AX = mybir.AxisListType
F32 = mybir.dt.float32
I32 = mybir.dt.int32

P = 128
D = 2048
KT = D // P
TP = 256
DB, DT = 8, 4
TS = DB * DT
T = TP + TS
NC = 1 + DB
H_A, DV = 4, 256
VB = DV // P
H_B = 8
PAST, PAGE = 1024, 128
NPG = PAST // PAGE
NG, EG = 4, 4
NE = NG * EG
FE = D // 4
TT = 96
NT = T // TT
W = 128
MAXW = NG + T // W
TW = T + W
EPS = 1e-6
SCALE = float(P) ** -0.5
BIG = 1e30
N_SMALL = 10
SLOTS = 6
SLOT = 4096
COL_QB = 2 * 512 + 2 * 1024 + 16
COL_LRA = COL_QB - 16
COL_FB = COL_QB + 3 * 1024
COL_GA = COL_FB + 8
COL_GB = COL_GA + D
LEVELS = (64, 32, 16, 8, 4, 2, 1)

STEPS = {
    "pe_step": (
            "ss1_ready c_turned vec_turned lra_fb_ready za_ready va_turned kt_turned state1_ready "
            "oa_ready update2_ready os_own_ready os_state_ready os_turned ss_a_ready lf_turned "
            "s_new_ready o_all_turned ss2_ready logits_ready rank_ready cs_summed perm_turned "
            "ss3_ready ").split(),
    "act_step": (
            "c_sig_ready root1_ready za_exp zf_exp decay_exp oa_squared root_a_ready "
            "ra_sig root2_ready root3_ready ").split(),
    "dve_step": (
            "ms1_ready c_silu cT_ready lra_copied za_read logf_ready va_copied decay_rel "
            "decayed_ready kt_copied state1_copied oa_copied gla_prompt_ready update2_used os_summed "
            "gla_sample_ready os_turned_copied gla_scratch_free ms_a_ready rs_a_ready oa_final "
            "kv_tok_ready f_ready s_new_copied ob_ready work_free ms2_ready onehot_ready perm_ready "
            "table_ready perm_copied hs_ready ys_ready ms3_ready y_ready ").split(),
}


def ds(i, n):
    return bass.ds(i, n)


def build(nc, io, out):
    with ExitStack() as ctx:
        made = {}

        def sem(name):
            if name not in made:
                made[name] = ctx.enter_context(nc.semaphore(name))
            return made[name]

        reached = {name: 0 for name in STEPS}

        def step(name):
            for engine, names in STEPS.items():
                if name in names:
                    return sem(engine), names.index(name) + 1

        def reach(name):
            s, n = step(name)
            engine = [e for e, names in STEPS.items() if name in names][0]
            assert n == reached[engine] + 1, name
            reached[engine] = n
            return s

        def sb(name, shape, dt=F32):
            return ctx.enter_context(nc.sbuf_tensor(name, shape, dt))

        ring = sb("ring", [P, SLOTS * SLOT])
        xT = sb("xT", [P, KT, T])
        hT = sb("hT", [P, KT, T])
        z = sb("z", [P, 48 * T])
        work2 = sb("work2", [P, 2976])
        ident = sb("ident", [P, P])
        ones = sb("ones", [P, P])
        fox_mask = sb("fox_mask", [P, P])
        new_mask = sb("new_mask", [P, TS])
        own_seq = sb("own_seq", [P, DB])
        ramp = sb("ramp", [P, 4])
        vcol = sb("vcol", [P, 152])
        modT = sb("modT", [P, 6 * KT, NC])
        mod_a = sb("mod_a", [P, KT, NC])
        rstd = sb("rstd", [P, T])
        ms = sb("ms", [P, T])
        brow = sb("brow", [1, 20])
        bfc = sb("bfc", [H_B, 1])
        ptab = sb("ptab", [1, DB * NPG], I32)
        fT = sb("fT", [H_B, T])
        shifted = sb("shifted", [P, TS])
        wtab = sb("wtab", [1, 24], I32)

        ps = ctx.enter_context(nc.psum_tensor("ps", [P, 8, 512], F32))

        def slot(s):
            return ring[:, (s % SLOTS) * SLOT:(s % SLOTS + 1) * SLOT]

        def ztile(i, n=1):
            return z[:, i * T:(i + n) * T].rearrange("p (n t) -> p n t", t=T)

        qa, ka, va, ra = ztile(0, 4), ztile(4, 4), ztile(8, 8), ztile(16, 8)
        qb, kb, vb = ztile(24, 8), ztile(32, 8), ztile(40, 8)
        oaT, obT, mgT = ztile(0, 8), qb, ztile(8, 16)
        vaTok = z[:, 8 * T:8 * T + 2 * 1024].rearrange("p (c n) -> p c n", c=2)
        vbTok = z[:, 40 * T:40 * T + 2 * 1024].rearrange("p (c n) -> p c n", c=2)
        x_in = z[:, 0:3 * D].rearrange("p (c n) -> p c n", c=3)
        sq = z[:, 3 * D:3 * D + KT * T].rearrange("p (k t) -> p k t", t=T)
        c_in = z[:, 11000:11000 + D]
        bada_rows = z[0:96, 13312:13312 + P]
        vec_rows = z[0:54, 13440:13440 + P]
        late = z[:, 48 * T - 2 * D:48 * T].rearrange("p (n d) -> p n d", n=2)
        c_sig = sq[:, 0:8, :].rearrange("p k t -> p (k t)")[:, 0:D]
        cT = work2[:, 0:KT * 32].rearrange("p (k c) -> p k c", c=32)
        mod_row = work2[:, 512:512 + 3 * 512].rearrange("p (j n) -> p j n", j=3)
        w_small = work2[:, 2048:2048 + KT * 40].rearrange("p (k n) -> p k n", n=40)
        lraT = work2[0:16, 2688:2688 + T]
        wk = ring[:, 4 * SLOT:6 * SLOT]
        F4 = H_A * T
        la = wk[:, 0:F4].rearrange("p (h t) -> p h t", t=T)
        buf = [wk[:, (i + 1) * F4:(i + 2) * F4] for i in range(5)]
        buf3 = [b.rearrange("p (h t) -> p h t", t=T) for b in buf]
        cum = buf3[4]
        atP = wk[:, 6 * F4:6 * F4 + 1024].rearrange("p (c h t) -> p c h t", c=2, h=H_A)
        atS = wk[0:TS, 6 * F4 + 1024:6 * F4 + 1152].rearrange("p (h t) -> p h t", h=H_A)
        w4 = ring[:, 2 * SLOT:4 * SLOT]
        ktP = w4[:, 0:1024].rearrange("p (c n) -> p c n", c=2)
        ktS = w4[0:TS, 1024:1536]
        kmS = w4[0:TS, 1536:2048]
        vaS = w4[0:TS, 2048:3072]
        stP = w4[:, 3072:4096].rearrange("p (h v) -> p h v", h=H_A)
        osS = w4[:, 4096:4096 + DV]
        decay = w4[:, 4400:4400 + H_A * 10].rearrange("p (h n) -> p h n", h=H_A)
        level_mask = w4[:, 4480:4480 + len(LEVELS) * P].rearrange("p (n t) -> p n t", t=P)
        wa2 = w4[0:16, 5400:5912]
        fa, fb_, fc = (w4[0:H_B, 6000 + n * T:6000 + (n + 1) * T] for n in range(3))
        state = ring[:, 0:2 * SLOT].rearrange("p (b h v) -> p b h v", b=DB, h=H_A)
        sq8 = wk[:, F4:3 * F4].rearrange("p (n t) -> p n t", t=T)
        rs4 = buf3[2]
        sig8 = wk[:, 4 * F4:6 * F4].rearrange("p (n t) -> p n t", t=T)
        w3 = z[:, 8 * T:24 * T]
        kbTok = w3[:, 0:2048].rearrange("p (c n) -> p c n", c=2)
        prob = w3[:, 2048:2048 + 768].rearrange("p (c n) -> p c n", c=2)
        probT = w3[:, 2816:2816 + 768].rearrange("p (c n) -> p c n", c=2)
        lfTok = w3[:, 3600:3600 + 24].rearrange("p (c n) -> p c n", c=3)
        st_p = w3[:, 3640:3640 + 16]
        kbS = work2[0:TS, 0:1024]
        vbS = work2[0:TS, 1024:2048]
        ktR = wk[:, 0:8 * 512].rearrange("p (n t) -> p n t", n=8)
        pS = wk[:, 4096:4096 + 2 * 1056].rearrange("p (g n) -> p g n", g=2)
        pTS = w3[:, 1280:3328].rearrange("p (g n t) -> p g n t", g=2, n=8)
        pTN = w3[0:TS, 3328:3584].rearrange("p (g t) -> p g t", g=2)
        s_new = w3[:, 4200:4264].rearrange("p (g t) -> p g t", g=2)
        o_all = w3[:, 4300:4556].rearrange("p (g t) -> p g t", g=2)
        fn_r = w3[:, 4560:4562]
        nfT = w3[0:H_B, 3700:3700 + T]
        after = w3[:, 4000:4000 + P]
        lf_in = w3[:, 0:64].rearrange("p (n h) -> p n h", h=H_B)
        lf_a = w3[:, 64:128].rearrange("p (n h) -> p n h", h=H_B)
        lf_b = w3[:, 128:192].rearrange("p (n h) -> p n h", h=H_B)
        rT = w3[0:H_B, 256:256 + PAST]
        st_s = w3[:, 200:232]
        sig_ab = work2[:, 0:8 * T].rearrange("p (n t) -> p n t", t=T)
        hTok = ring[0:TT, 0:NT * D].rearrange("p (c n) -> p c n", c=NT)
        yTok = hTok
        perm = work2[0:TT, 0:NT * T].rearrange("p (c n) -> p c n", c=NT)
        permT = work2[0:TT, NT * T:2 * NT * T].rearrange("p (c n) -> p c n", c=NT)
        rt = work2[0:TT, 1728:2300]
        cw = work2[0:NE, 2300:2300 + W]
        selw = work2[0:NE, 2428:2432]
        rrow = work2[0:1, 2432:2480]
        prow = work2[0:TT, 2300 + 672:2300 + 676]
        wrt = work2[:, 2480:2480 + KT * 20].rearrange("p (k n) -> p k n", n=20)
        iota_pos = z[:, 13312:13312 + T]
        before = z[0:TT, 13600:13600 + TT]
        hs = z[:, 0:KT * TW].rearrange("p (k t) -> p k t", t=TW)
        ys = z[:, KT * TW:2 * KT * TW].rearrange("p (k t) -> p k t", t=TW)
        hflat = hT[:, :, :].rearrange("p k t -> p (k t)")
        hw = hflat[:, 0:KT * W].rearrange("p (k t) -> p k t", t=W)
        comb_b = hflat[:, 2048:2560].rearrange("p (j t) -> p j t", j=EG)
        sg = hflat[:, 2560:3072]
        hid = hflat[:, 3072:4096].rearrange("p (b n) -> p b n", b=2)
        cs = hflat[0:NE, 4096:4096 + TW]
        out_tok = ring[:, 2 * SLOT:2 * SLOT + 3 * D].rearrange("p (c n) -> p c n", c=3)
        sq2 = z[:, 24 * T:(24 + KT) * T].rearrange("p (k t) -> p k t", t=T)

        V_G1, V_G2, V_GF, V_BA, V_GG = 96, 112, 128, 144, 148

        ADA, WIN, UP, WOUT = 0, 24, 48, 72
        MOE = WOUT + 8
        EXTRA = DB

        def freed(n):
            f = n // SLOTS + 1
            return f + (EXTRA if n >= UP and n % SLOTS < 4 else 0)

        def freed_for_pages(s):
            return freed(UP + s) - (EXTRA if s < 4 else 0)

        def filled(n):
            return 16 * (n // SLOTS + 1)

        block = ctx.enter_context(nc.Block())

        @block.sync
        def _(sp):
            sp.dma_start(x_in[:, 0:2, :], io["x_prompt"].rearrange("a (c p) n -> p (a c) n", p=P)).then_inc(sem("x_loaded"), 16)
            sp.dma_start(x_in[0:TS, 2, :], io["x_sample"].rearrange("b t n -> (b t) n")).then_inc(sem("x_loaded"), 16)

            for n in range(ADA, WIN):
                j, q = (n - ADA) // 8, (n - ADA) % 8
                sp.wait_ge(sem(f"ring_free{n % SLOTS}"), freed(n))
                src = io["w_ada"][0, q * 2 * P:(q + 1) * 2 * P, j * D:(j + 1) * D]
                sp.dma_start(slot(n).rearrange("p (k n) -> p k n", k=2),
                             src.rearrange("(k p) n -> p k n", p=P)).then_inc(sem(f"ring_full{n % SLOTS}"), 16)

            for part, col in ((0, 0), (1, COL_QB)):
                with sp.Fori(0, 2) as i:
                    for n in range(SLOTS):
                        j, q = n // 2, n % 2
                        sp.wait_ge(sem(f"ring_free{n}"), i + freed(WIN + 12 * part + n))
                        src = io["w_in"][0, q * 8 * P:(q + 1) * 8 * P, ds(i * 1536 + (col + j * 512), 512)]
                        sp.dma_start(slot(n).rearrange("p (k n) -> p k n", k=8),
                                     src.rearrange("(k p) n -> p k n", p=P)).then_inc(sem(f"ring_full{n}"), 16)

            for s in range(2):
                sp.wait_ge(sem(f"ring_free{s}"), freed_for_pages(s))
            sp.dma_start(state, io["state_gla"][0].rearrange("b h k v -> k b h v")).then_inc(sem("state_loaded"), 16)

            with sp.Fori(0, DB) as b:
                for n in range(NPG):
                    pg = sp.value_load(ptab[0:1, ds(b * NPG + n, 1)], min_val=0, max_val=io["cache_k"].shape[1] - 1)
                    if n == 0:
                        sp.wait_ge(sem("lf_used"), b + 1)
                    sp.dma_start(lf_in[:, n, :], io["cache_logf"][0, ds(pg, 1)].rearrange("a p h -> (a p) h")).then_inc(sem("lf_loaded"), 16)
                for kv, name in ((0, "cache_k"), (1, "cache_v")):
                    for n in range(NPG):
                        s = 2 * kv + n // 4
                        pg = sp.value_load(ptab[0:1, ds(b * NPG + n, 1)], min_val=0, max_val=io["cache_k"].shape[1] - 1)
                        if n % 4 == 0:
                            if s == 0:
                                sp.wait_ge(sem("state_stored"), 16)
                            if s == 2:
                                sp.wait_ge(*step("gla_scratch_free"))
                            sp.wait_ge(sem(f"ring_free{s}"), b + freed_for_pages(s))
                        sp.dma_start(slot(s)[:, (n % 4) * 1024:(n % 4 + 1) * 1024],
                                     io[name][0, ds(pg, 1)].rearrange("a p h d -> (a p) (h d)")).then_inc(sem(f"kv_full{s}"), 16)

            sp.wait_ge(*step("work_free"))
            with sp.Fori(0, 4) as g:
                for n in range(SLOTS):
                    for s in ((n,), (1, 2), (), (n,), (n,), (n,))[n]:
                        sp.wait_ge(sem(f"ring_free{s}"), g + freed(UP + s))
                    part, q = n // 3, n % 3
                    if q < 2:
                        src = io["w_in"][0, q * 8 * P:(q + 1) * 8 * P, ds(g * 512 + (COL_GA, COL_GB)[part], 512)]
                    else:
                        src = io[("w_up_a", "w_up_b")[part]][0, :, ds(g * 512, 512)]
                    sp.dma_start(slot(n).rearrange("p (k n) -> p k n", k=8),
                                 src.rearrange("(k p) n -> p k n", p=P)).then_inc(sem(f"ring_full{n}"), 16)

            for n in range(8):
                j, q = n // 2, n % 2
                sp.wait_ge(sem(f"ring_free{n % SLOTS}"), freed(WOUT + n))
                src = io["w_out"][0, q * 8 * P:(q + 1) * 8 * P, j * 512:(j + 1) * 512]
                sp.dma_start(slot(n).rearrange("p (k n) -> p k n", k=8),
                             src.rearrange("(k p) n -> p k n", p=P)).then_inc(sem(f"ring_full{n % SLOTS}"), 16)

            def gate_up(e, turn):
                for n in range(4):
                    s = (MOE + n) % SLOTS
                    sp.wait_ge(sem(f"ring_free{s}"), turn + freed(MOE + n))
                    src = io[("w_gate_e", "w_up_e")[n // 2]][0, ds(e, 1), (n % 2) * 8 * P:(n % 2 + 1) * 8 * P, :]
                    sp.dma_start(slot(s).rearrange("p (k n) -> p k n", k=8),
                                 src.rearrange("a (k p) n -> p (a k) n", p=P)).then_inc(sem(f"ring_full{s}"), 16)

            def down(e, turn):
                for n in (4, 5):
                    s = (MOE + n) % SLOTS
                    sp.wait_ge(sem(f"ring_free{s}"), turn + freed(MOE + n))
                    src = io["w_down_e"][0, ds(e, 1), :, (n - 4) * 1024:(n - 3) * 1024]
                    sp.dma_start(slot(s).rearrange("p (k n) -> p k n", k=4),
                                 src.rearrange("a (k p) n -> p (a k) n", p=P)).then_inc(sem(f"ring_full{s}"), 16)

            gate_up(0, 0)
            sp.wait_ge(*step("table_ready"))
            sp.wait_ge(*step("hs_ready"))
            last_turn = sp.value_load(wtab[0:1, 1:2], min_val=3, max_val=MAXW - 1)
            with sp.Fori(0, last_turn) as w:
                e = sp.value_load(wtab[0:1, ds(w + 2, 1)], min_val=0, max_val=NE - EG)
                e_next = sp.value_load(wtab[0:1, ds(w + 3, 1)], min_val=0, max_val=NE - EG)
                for j in range(EG):
                    down(e + j, w * EG + j)
                    gate_up(e + (j + 1) if j + 1 < EG else e_next, w * EG + (j + 1))
            e = NE - EG
            for j in range(EG):
                down(e + j, last_turn * EG + j)
                if j + 1 < EG:
                    gate_up(e + (j + 1), last_turn * EG + (j + 1))

        @block.gpsimd
        def _(pool):
            pool.memset(ident[:, :], 0.0)
            pool.memset(ones[:, :], 1.0)
            pool.memset(fox_mask[:, :], 0.0)
            pool.memset(new_mask[:, :], 0.0)
            pool.memset(own_seq[:, :], 1.0)
            pool.memset(w_small[:, :, :], 0.0)
            pool.drain()
            pool.sem_inc(sem("w_small_clear"), 1)
            pool.affine_select(out=ident[:, :], in_=ident[:, :], compare_op=ALU.not_equal, fill=1.0,
                               base=0, pattern=[[-1, P]], channel_multiplier=1).then_inc(sem("ident_ready"), 1)
            pool.affine_select(out=fox_mask[:, :], in_=fox_mask[:, :], compare_op=ALU.is_ge, fill=-BIG, base=0,
                               pattern=[[-1, P]], channel_multiplier=1)
            for h in range(4):
                m = new_mask[32 * h:32 * h + 32, :]
                pool.affine_select(out=m, in_=m, compare_op=ALU.is_ge, fill=-BIG, base=0,
                                   pattern=[[-1, TS]], channel_multiplier=1)
                pool.drain()
                pool.affine_select(out=m.rearrange("p (b j) -> p b j", j=DT), in_=m.rearrange("p (b j) -> p b j", j=DT),
                                   compare_op=ALU.is_ge, fill=-BIG, base=DT - 1,
                                   pattern=[[DT, DB], [0, DT]], channel_multiplier=-1)
                o = own_seq[32 * h:32 * h + 32, :]
                pool.affine_select(out=o, in_=o, compare_op=ALU.is_ge, fill=0.0, base=0,
                                   pattern=[[-DT, DB]], channel_multiplier=1)
                pool.drain()
                pool.affine_select(out=o, in_=o, compare_op=ALU.is_ge, fill=0.0, base=DT - 1,
                                   pattern=[[DT, DB]], channel_multiplier=-1)
                pool.drain()
            pool.iota(ramp[:, :], pattern=[[-1, 4]], base=4, channel_multiplier=0, allow_small_or_imprecise_dtypes=True)
            pool.drain()
            pool.sem_inc(sem("consts_ready"), 1)

            pool.wait_ge(*step("vec_turned"))
            with pool.Fori(0, 3) as i:
                for k in range(KT):
                    pool.wait_ge(sem(f"late_free{k % 2}"), i * 8 + (k // 2 + 1))
                    pool.dma_start(late[:, k % 2, :], io["w_ada"][0, k * P:(k + 1) * P, ds(i * D + 3 * D, D)]).then_inc(sem(f"late_full{k % 2}"), 16)

            pool.wait_ge(*step("lra_fb_ready"))
            pool.memset(level_mask, 0.0)
            pool.drain()
            for n, b in enumerate(LEVELS):
                v = level_mask[:, n, :].rearrange("p (m two t) -> p m two t", two=2, t=b)[:, :, 1, :]
                pool.memset(v, 1.0)
                pool.drain()
                pool.affine_select(out=v, in_=v, compare_op=ALU.is_ge, fill=0.0, base=0,
                                   pattern=[[-2 * b, P // (2 * b)], [0, b]], channel_multiplier=1)
                pool.drain()
                pool.affine_select(out=v, in_=v, compare_op=ALU.is_ge, fill=0.0, base=b - 1,
                                   pattern=[[2 * b, P // (2 * b)], [0, b]], channel_multiplier=-1)
            pool.drain()
            pool.sem_inc(sem("masks_ready"), 1)

            pool.wait_ge(*step("gla_prompt_ready"))
            pool.dma_start(out["gla_prompt"][0, 0].rearrange("h k v -> k h v"), stP).then_inc(sem("gla_prompt_stored"), 16)
            pool.wait_ge(*step("gla_sample_ready"))
            pool.dma_start(out["gla_sample"][0].rearrange("b h k v -> k b h v"), state).then_inc(sem("state_stored"), 16)
            pool.wait_ge(*step("kv_tok_ready"))
            pool.dma_start(out["k_prompt"][0, 0].rearrange("(c p) h d -> p c (h d)", p=P), kbTok).then_inc(sem("kv_stored"), 16)
            pool.dma_start(out["v_prompt"][0, 0].rearrange("(c p) h d -> p c (h d)", p=P), vbTok).then_inc(sem("kv_stored"), 16)
            pool.dma_start(out["k_sample"][0].rearrange("b t h d -> (b t) (h d)"), kbS).then_inc(sem("kv_stored"), 16)
            pool.dma_start(out["v_sample"][0].rearrange("b t h d -> (b t) (h d)"), vbS).then_inc(sem("kv_stored"), 16)
            pool.dma_start(out["logf_prompt"][0, 0].rearrange("(c p) h -> p c h", p=P), lfTok[:, 0:2, :]).then_inc(sem("kv_stored"), 16)
            pool.dma_start(out["logf_sample"][0].rearrange("b t h -> (b t) h"), lfTok[0:TS, 2, :]).then_inc(sem("kv_stored"), 16)
            pool.affine_select(out=after, in_=ones[:, :], compare_op=ALU.is_gt, fill=0.0, base=0,
                               pattern=[[-1, P]], channel_multiplier=1).then_inc(sem("after_ready"), 1)
            pool.wait_ge(*step("ob_ready"))
            pool.iota(iota_pos[:, :], pattern=[[1, T]], base=0, channel_multiplier=0, allow_small_or_imprecise_dtypes=True)
            pool.affine_select(out=before, in_=ones[0:TT, 0:TT], compare_op=ALU.is_gt, fill=0.0, base=0,
                               pattern=[[1, TT]], channel_multiplier=-1)
            pool.drain()
            pool.sem_inc(sem("route_consts_ready"), 1)
            pool.wait_ge(*step("y_ready"))
            pool.dma_start(out["y_prompt"].rearrange("a (c p) n -> p (a c) n", p=P), out_tok[:, 0:2, :]).then_inc(sem("y_stored"), 16)
            pool.dma_start(out["y_sample"].rearrange("b t n -> (b t) n"), out_tok[0:TS, 2, :]).then_inc(sem("y_stored"), 16)
            pool.wait_ge(sem("gla_prompt_stored"), 16)
            pool.wait_ge(sem("state_stored"), 16)
            pool.wait_ge(sem("kv_stored"), 6 * 16)
            pool.wait_ge(sem("y_stored"), 2 * 16)

        @block.tensor
        def _(pe):
            def mm(o, lhsT, rhs, start, stop, free=False):
                return nc.tensor.matmul(o, lhsT, rhs, start=start, stop=stop, skip_group_check=free)

            def release(name, count, *slots):
                pe.wait_ge(sem(name), count)
                for s in slots:
                    pe.sem_inc(sem(f"ring_free{s % SLOTS}"), 1)

            def tr(o, i):
                n = i.shape[0]
                return nc.tensor.transpose(o, i, ident[0:n, 0:n])

            pe.wait_ge(sem("ident_ready"), 1)
            pe.wait_ge(sem("x_loaded"), 32)
            for k in range(KT):
                if k >= 4:
                    pe.wait_ge(sem("xT_copied"), k - 3)
                for c in range(2):
                    tr(ps[:, k % 4, c * P:(c + 1) * P], x_in[:, c, k * P:(k + 1) * P])
                tr(ps[:, k % 4, TP:T], x_in[0:TS, 2, k * P:(k + 1) * P]).then_inc(sem("xT_turned"), 1)
            pe.wait_ge(sem("xT_squared"), KT)
            pe.wait_ge(sem("consts_ready"), 1)
            pe.wait_ge(sem("small_loaded"), 16 * N_SMALL)
            for k in range(KT):
                last = mm(ps[:, 4, 0:T], ones[:, :], sq[:, k, :], k == 0, k == KT - 1)
            last.then_inc(reach("ss1_ready"), 1)
            pe.wait_ge(*step("c_silu"))
            for k in range(KT):
                last = tr(ps[:, 5, k * NC:(k + 1) * NC], c_in[0:NC, k * P:(k + 1) * P])
            last.then_inc(reach("c_turned"), 1)
            pe.wait_ge(sem("small_loaded"), 16 * N_SMALL)
            tr(ps[:, 6, 0:96], bada_rows)
            tr(ps[:, 6, 96:150], vec_rows).then_inc(reach("vec_turned"), 1)

            pe.wait_ge(*step("cT_ready"))
            pe.wait_ge(sem("xT_copied"), KT)
            def turn(section, row, bank):
                pe.wait_ge(sem("mod_row_ready"), section + 1)
                for jt in range(4):
                    last = tr(ps[:, bank, jt * P:(jt + 1) * P], mod_row[:, row, jt * P:(jt + 1) * P])
                last.then_inc(sem("mod_turned"), 1)

            for n in range(ADA, WIN):
                j, q = (n - ADA) // 8, (n - ADA) % 8
                pe.wait_ge(sem(f"ring_full{n % SLOTS}"), filled(n))
                w = slot(n).rearrange("p (k n) -> p k n", k=2)
                for k in range(2):
                    for c in range(4):
                        last = mm(ps[32 * c:32 * c + 32, j, :], cT[:, 2 * q + k, :], w[:, k, c * 512:(c + 1) * 512],
                                  q == 0 and k == 0, q == 7 and k == 1)
                if q < 7:
                    last.then_inc(sem(f"ring_free{n % SLOTS}"), 1)
                    continue
                last.then_inc(sem("mod_summed"), 1)
                release("mod_summed", j + 1, n)
                if j:
                    turn(j - 1, j - 1, 2 + j)
            turn(2, 2, 5)

            pe.wait_ge(sem("h1_ready"), 1)
            pe.wait_ge(sem("mod_ready"), 3)
            def win_round(i, late_too):
                def late_section(first, count):
                    for k in range(first, first + count):
                        if k == 0:
                            pe.wait_ge(sem("mod_row_ready"), i + 3)
                        pe.wait_ge(sem(f"late_full{k % 2}"), i * 128 + 16 * (k // 2 + 1))
                        for c in range(4):
                            last = mm(ps[32 * c:32 * c + 32, 7, :], cT[:, k, :], late[:, k % 2, c * 512:(c + 1) * 512], k == 0, k == KT - 1)
                        if k < KT - 1:
                            last.then_inc(sem(f"late_free{k % 2}"), 1)
                            continue
                        last.then_inc(sem("mod_summed"), 1)
                        pe.wait_ge(sem("mod_summed"), i + 4)
                        pe.sem_inc(sem(f"late_free{k % 2}"), 1)

                for j in range(3):
                    for s in (2 * j, 2 * j + 1):
                        pe.wait_ge(sem(f"ring_full{s}"), i * 16 + filled(WIN + s))
                    wl, wh = (slot(s).rearrange("p (k n) -> p k n", k=8) for s in (2 * j, 2 * j + 1))
                    for t in range(4):
                        n = 4 * j + t
                        pe.wait_ge(sem("win_bank_free%d" % (n % 2)), i * 6 + (n // 2 + 1))
                        for k in range(KT):
                            w = (wl if k < 8 else wh)[:, k % 8, t * P:(t + 1) * P]
                            last = mm(ps[:, n % 6, 0:T], w, hT[:, k, :], k == 0, k == KT - 1)
                        last.then_inc(sem("win_tile"), 1)
                        if late_too and n < 7:
                            late_section(2 * n, 2)
                        elif late_too and n < 9:
                            late_section(7 + n, 1)
                    release("win_tile", i * 12 + 4 * (j + 1), 2 * j, 2 * j + 1)
                if late_too:
                    pe.wait_ge(sem("mod_ready"), i + 3)
                    turn(i + 3, 2, 6)

            with pe.Fori(0, 3) as i:
                win_round(i, True)
            win_round(3, False)
            pe.wait_ge(sem("mod_ready"), 6)
            pe.wait_ge(sem("w_small_loaded"), 32)
            for k in range(KT):
                last = mm(ps[0:40, 6, 0:T], w_small[:, k, :], hT[:, k, :], k == 0, k == KT - 1)
            last.then_inc(reach("lra_fb_ready"), 1)
            pe.wait_ge(*step("lra_copied"))
            pe.wait_ge(sem("wa2_loaded"), 16)
            pe.wait_ge(sem("win_bank_free0"), 24 + 3)
            pe.wait_ge(sem("win_bank_free1"), 24 + 3)
            for h in range(H_A):
                last = mm(ps[:, h, 0:T], wa2[:, h * P:(h + 1) * P], lraT, True, True)
            last.then_inc(reach("za_ready"), 1)

            for c in range(2):
                for n in range(8):
                    last = tr(ps[:, 4 + 2 * c + n // 4, (n % 4) * P:(n % 4 + 1) * P], va[:, n, c * P:(c + 1) * P])
            pe.wait_ge(*step("za_read"))
            for n in range(8):
                last = tr(ps[0:TS, n // 4, (n % 4) * P:(n % 4 + 1) * P], va[:, n, TP:T])
            last.then_inc(reach("va_turned"), 1)
            pe.wait_ge(*step("va_copied"))
            for n in range(len(LEVELS) + 1):
                pe.wait_ge(sem("level_ready"), n + 1)
                if n >= 2:
                    pe.wait_ge(sem("level_read"), n - 1)
                b0 = 3 * (n % 2)
                ql, kl = (buf3[0], buf3[1]) if n < len(LEVELS) else (qa, ka)
                for c in range(2):
                    for h in range(H_A):
                        last = mm(ps[:, b0 + c, h * P:(h + 1) * P], kl[:, h, c * P:(c + 1) * P], ql[:, h, c * P:(c + 1) * P], True, True)
                if n >= len(LEVELS) - 2:
                    for h in range(H_A):
                        last = mm(ps[0:TS, b0 + 2, h * TS:(h + 1) * TS], kl[:, h, TP:T], ql[:, h, TP:T], True, True)
                last.then_inc(sem("level_scored"), 1)
            pe.wait_ge(*step("decayed_ready"))
            for c in range(2):
                for h in range(H_A):
                    last = tr(ps[:, 6 + c, h * P:(h + 1) * P], buf3[3][:, h, c * P:(c + 1) * P])
            pe.wait_ge(sem("level_read"), len(LEVELS))
            for h in range(H_A):
                last = tr(ps[0:TS, 0, h * P:(h + 1) * P], buf3[3][:, h, TP:T])
            last.then_inc(reach("kt_turned"), 1)
            pe.wait_ge(*step("kt_copied"))
            pe.wait_ge(sem("level_read"), len(LEVELS) + 1)
            for h in range(H_A):
                last = mm(ps[:, 4 + h // 2, (h % 2) * DV:(h % 2 + 1) * DV], ktP[:, 0, h * P:(h + 1) * P],
                          vaTok[:, 0, h * DV:(h + 1) * DV], True, True)
            last.then_inc(reach("state1_ready"), 1)
            pe.wait_ge(*step("state1_copied"))
            for n in range(8):
                h, v = n // 2, n % 2
                vs = slice(h * DV + v * P, h * DV + (v + 1) * P)
                o = ps[:, n // 2, (n % 2) * TP:(n % 2 + 1) * TP]
                mm(o[:, 0:P], vaTok[:, 0, vs], atP[:, 0, h, :], True, True)
                mm(o[:, P:TP], vaTok[:, 1, vs], atP[:, 1, h, :], True, False)
                last = mm(o[:, P:TP], stP[:, h, v * P:(v + 1) * P], buf3[2][:, h, P:TP], False, True)
            last.then_inc(reach("oa_ready"), 1)
            for h in range(H_A):
                last = mm(ps[:, 6 + h // 2, (h % 2) * DV:(h % 2 + 1) * DV], ktP[:, 1, h * P:(h + 1) * P],
                          vaTok[:, 1, h * DV:(h + 1) * DV], True, True)
            last.then_inc(reach("update2_ready"), 1)
            pe.wait_ge(*step("oa_copied"))
            for h in range(H_A):
                last = mm(ps[32 * h:32 * h + 32, 4, 0:DV], atS[:, h, :], vaS[:, h * DV:(h + 1) * DV], True, True)
            last.then_inc(reach("os_own_ready"), 1)
            pe.wait_ge(sem("state_loaded"), 16)
            for b in range(DB):
                for h in range(H_A):
                    last = mm(ps[32 * h:32 * h + 32, b // 2, (b % 2) * DV:(b % 2 + 1) * DV], buf3[2][:, h, TP:T], state[:, b, h, :], True, True)
            last.then_inc(reach("os_state_ready"), 1)
            pe.wait_ge(*step("update2_used"))
            for b in range(DB):
                pe.wait_ge(sem("km_ready"), b + 1)
                if b >= 1:
                    pe.wait_ge(sem("state_updated"), b)
                for h in range(H_A):
                    last = mm(ps[:, 6 + h // 2, (h % 2) * DV:(h % 2 + 1) * DV], kmS[:, h * P:(h + 1) * P],
                              vaS[:, h * DV:(h + 1) * DV], True, True)
                last.then_inc(sem("update_ready"), 1)
            pe.wait_ge(*step("os_summed"))
            for v in range(VB):
                last = tr(ps[:, 4, v * P:(v + 1) * P], osS[:, v * P:(v + 1) * P])
            last.then_inc(reach("os_turned"), 1)
            pe.wait_ge(*step("oa_squared"))
            for h in range(H_A):
                for v in range(VB):
                    last = mm(ps[:, h, 0:T], ones[:, :], sq8[:, 2 * h + v, :], v == 0, v == VB - 1)
            last.then_inc(reach("ss_a_ready"), 1)

            pe.wait_ge(*step("os_turned_copied"))
            pe.wait_ge(sem("state_updated"), DB)
            for m, src in ((0, kb), (1, vb)):
                if m:
                    pe.wait_ge(sem("tok_copied"), 1)
                for c in range(2):
                    for h in range(H_B):
                        last = tr(ps[:, 4 + 2 * c + h // 4, (h % 4) * P:(h % 4 + 1) * P], src[:, h, c * P:(c + 1) * P])
                last.then_inc(sem("tok_turned"), 1)
            pe.wait_ge(sem("tok_copied"), 2)
            for m, src in ((0, kb), (1, vb)):
                for h in range(H_B):
                    last = tr(ps[0:TS, 4 + 2 * m + h // 4, (h % 4) * P:(h % 4 + 1) * P], src[:, h, TP:T])
            last.then_inc(sem("tok_turned"), 1)
            pe.wait_ge(*step("rs_a_ready"))
            pe.wait_ge(*step("logf_ready"))
            for c in range(3):
                n = P if c < 2 else TS
                last = tr(ps[0:n, 0, c * H_B:(c + 1) * H_B], fT[:, c * P:c * P + n])
            last.then_inc(reach("lf_turned"), 1)
            pe.wait_ge(*step("f_ready"))
            pe.wait_ge(sem("tok_copied"), 4)
            for i in range(H_B + 1):
                if i < H_B:
                    h = i
                    if h >= 2:
                        pe.wait_ge(sem("fox_exp"), h - 1)
                    sbk = ps[:, 1 + h % 2, :]
                    hot = ident[0:H_B, h:h + 1]
                    for q in range(2):
                        kk = P * (q + 1)
                        o = sbk[:, q * P:q * P + kk]
                        mm(o, qb[:, h, q * P:(q + 1) * P], kb[:, h, 0:kk], True, False)
                        mm(o, hot.to_broadcast([H_B, P]), nfT[:, 0:kk], False, False)
                        last = mm(o, fT[:, q * P:(q + 1) * P], hot.to_broadcast([H_B, kk]), False, True)
                    last.then_inc(sem("fox_scored"), 1)
                if i >= 1:
                    h = i - 1
                    pe.wait_ge(sem("fox_prob"), h + 1)
                    if h >= 1:
                        pe.wait_ge(sem("fox_pt"), h)
                    for n in range(3):
                        last = tr(ps[:, 3, n * P:(n + 1) * P], prob[:, h % 2, n * P:(n + 1) * P])
                    last.then_inc(sem("fox_turned"), 1)
                    pe.wait_ge(sem("fox_pt"), h + 1)
                    if h >= 2:
                        pe.wait_ge(sem("fox_out"), h - 1)
                    o = ps[:, 4 + h % 2, 0:TP]
                    vh = slice(h * P, (h + 1) * P)
                    mm(o[:, 0:P], vbTok[:, 0, vh], probT[:, h % 2, 0:P], True, True)
                    mm(o[:, P:TP], vbTok[:, 0, vh], probT[:, h % 2, P:2 * P], True, False)
                    last = mm(o[:, P:TP], vbTok[:, 1, vh], probT[:, h % 2, 2 * P:3 * P], False, True)
                    last.then_inc(sem("fox_pv"), 1)

            pe.wait_ge(sem("fox_out"), H_B)
            for g in range(2):
                for c in range(4):
                    h = 4 * g + c
                    o = ps[32 * c:32 * c + 32, 0, g * TS:(g + 1) * TS]
                    mm(o, qb[:, h, TP:T], kb[:, h, TP:T], True, False)
                    mm(o, ident[0:H_B, h:h + 1].to_broadcast([H_B, TS]), nfT[:, TP:T], False, False)
                    mm(o, fT[:, TP:T], ident[0:H_B, h:h + 1].to_broadcast([H_B, TS]), False, True)
                    last = mm(ps[32 * c:32 * c + 32, 1, g:g + 1], fT[:, TP:T], ident[0:H_B, h:h + 1], True, True)
            last.then_inc(reach("s_new_ready"), 1)
            pe.wait_ge(*step("s_new_copied"))
            pe.wait_ge(sem("after_ready"), 1)
            with pe.Fori(0, DB) as b:
                pe.wait_ge(sem("lf_summed"), b + 1)
                pe.wait_ge(sem("o_all_ready"), b + 1)
                for n in range(NPG):
                    o = ps[0:H_B, 6 + n // 4, (n % 4) * PAGE:(n % 4 + 1) * PAGE]
                    mm(o, lf_in[:, n, :], after[:, :], True, False)
                    last = mm(o, lf_b[:, n, :], ones[:, :], False, True)
                last.then_inc(sem("r_ready"), 1)
                for r in range(4):
                    g, half = r % 2, r // 2
                    if g == 0:
                        pe.wait_ge(sem(f"kv_full{half}"), (b + 1) * 64)
                    for c in range(4):
                        n = 4 * r + c
                        pe.wait_ge(sem("kt_copied%d" % (c % 2)), b * 8 + (n // 2 + 1))
                        w = slot(half)
                        for pgi in range(4):
                            last = tr(ps[:, 4 + c % 2, pgi * PAGE:(pgi + 1) * PAGE],
                                      w[:, pgi * 1024 + (4 * g + c) * P:pgi * 1024 + (4 * g + c + 1) * P])
                        last.then_inc(sem("kt_turned_s"), 1)
                    if g == 1:
                        release("kt_turned_s", b * 16 + 4 * (r + 1), half)
                    if r == 0:
                        pe.wait_ge(sem("r_copied"), b + 1)
                    pe.wait_ge(sem("kt_copied0"), b * 8 + (2 * (r + 1) + 1))
                    pe.wait_ge(sem("kt_copied1"), b * 8 + (2 * (r + 1) + 1))
                    for c in range(4):
                        mm(ps[32 * c:32 * c + 32, 2 * g + half, :], qb[:, 4 * g + c, TP:T], ktR[:, 4 * (r % 2) + c, :], True, False)
                    for c in range(4):
                        h = 4 * g + c
                        last = mm(ps[32 * c:32 * c + 32, 2 * g + half, :], ident[0:H_B, h:h + 1].to_broadcast([H_B, TS]),
                                  rT[:, half * 512:(half + 1) * 512], False, True)
                    last.then_inc(sem("s_scored"), 1)
                for g in range(2):
                    pe.wait_ge(sem("s_prob"), b * 2 + (g + 1))
                    for q in range(2):
                        if g:
                            pe.wait_ge(sem("pt_copied"), b * 5 + (q + 1))
                        for n in range(4):
                            last = tr(ps[:, 6 + q, n * P:(n + 1) * P], pS[:, g, (4 * q + n) * P:(4 * q + n + 1) * P])
                        last.then_inc(sem("pt_turned"), 1)
                pe.wait_ge(sem("pt_copied"), b * 5 + 3)
                for g in range(2):
                    last = tr(ps[0:TS, 6, g * P:(g + 1) * P], pS[:, g, PAST:PAST + TS])
                last.then_inc(sem("pt_turned"), 1)
                pe.wait_ge(sem("pt_copied"), b * 5 + 5)
                for s in (2, 3):
                    pe.wait_ge(sem(f"kv_full{s}"), (b + 1) * 64)
                pe.wait_ge(sem("kt_copied1"), b * 8 + 9)
                for g in range(2):
                    for n in range(NPG + 1):
                        for c in range(4):
                            h = 4 * g + c
                            o = ps[32 * c:32 * c + 32, 5, g * P:(g + 1) * P]
                            if n < NPG:
                                v = slot(2 + n // 4)[:, (n % 4) * 1024 + h * P:(n % 4) * 1024 + (h + 1) * P]
                                last = mm(o, pTS[:, g, n, 32 * c:32 * c + 32], v, n == 0, False)
                            else:
                                last = mm(o, pTN[:, g, 32 * c:32 * c + 32], vbS[:, h * P:(h + 1) * P], False, True)
                last.then_inc(sem("o_b_ready"), 1)
                release("o_b_ready", b + 1, 2, 3)
            pe.wait_ge(sem("o_all_ready"), DB + 1)
            for g in range(2):
                last = tr(ps[:, 0, g * P:(g + 1) * P], o_all[:, g, :])
            last.then_inc(reach("o_all_turned"), 1)

            pe.wait_ge(*step("ob_ready"))
            pe.wait_ge(*step("oa_final"))
            with pe.Fori(0, 4) as g:
                for n in range(16):
                    kind, t = n // 4, n % 4
                    first, halves = ((0, 2), (2, 1), (3, 2), (5, 1))[kind]
                    if t == 0:
                        for s in range(first, first + halves):
                            pe.wait_ge(sem(f"ring_full{s}"), g * 16 + filled(UP + s))
                    pe.wait_ge(sem("up_bank_free"), g * 16 + (n + 1))
                    src = hT if kind % 2 == 0 else (oaT if kind == 1 else obT)
                    for k in range(8 * halves):
                        w = slot(first + k // 8).rearrange("p (k n) -> p k n", k=8)[:, k % 8, t * P:(t + 1) * P]
                        last = mm(ps[:, n % 8, 0:T], w, src[:, k, :], k == 0, k == 8 * halves - 1)
                    last.then_inc(sem("up_tile"), 1)
                    if t == 3:
                        release("up_tile", g * 16 + (n + 1), *range(first, first + halves))

            pe.wait_ge(sem("merged"), 17)
            for n in range(KT):
                j, t = n // 4, n % 4
                if t == 0:
                    for s in (2 * j, 2 * j + 1):
                        pe.wait_ge(sem(f"ring_full{s % SLOTS}"), filled(WOUT + s))
                pe.wait_ge(sem("up_bank_free"), 64 + n + 1)
                for k in range(KT):
                    w = slot(2 * j + k // 8).rearrange("p (k n) -> p k n", k=8)[:, k % 8, t * P:(t + 1) * P]
                    last = mm(ps[:, n % 8, 0:T], w, mgT[:, k, :], k == 0, k == KT - 1)
                last.then_inc(sem("wout_tile"), 1)
                if t == 3:
                    release("wout_tile", n + 1, 2 * j, 2 * j + 1)

            pe.wait_ge(sem("x2_squared"), KT)
            pe.wait_ge(sem("up_bank_free"), 64 + 16 + 8)
            for k in range(KT):
                last = mm(ps[:, 0, 0:T], ones[:, :], sq2[:, k, :], k == 0, k == KT - 1)
            last.then_inc(reach("ss2_ready"), 1)

            pe.wait_ge(sem("h2_ready"), 1)
            pe.wait_ge(sem("router_loaded"), 32)
            for c in range(NT):
                o = ps[0:TT, 1, c * 20:(c + 1) * 20]
                for k in range(KT):
                    mm(o, hT[:, k, c * TT:(c + 1) * TT], wrt[:, k, :], k == 0, False)
                last = mm(o, ones[0:1, 0:TT], brow[:, :], False, True)
            last.then_inc(reach("logits_ready"), 1)
            for c in range(NT):
                for q in range(4):
                    n = 4 * c + q
                    if n >= 4:
                        pe.wait_ge(sem("htok_copied"), n - 3)
                    for m in range(4):
                        k = 4 * q + m
                        last = tr(ps[0:TT, 2 + n % 4, m * P:(m + 1) * P], hT[:, k, c * TT:(c + 1) * TT])
                    last.then_inc(sem("htok_turned"), 1)
            pe.wait_ge(*step("onehot_ready"))
            for c in range(NT):
                o = ps[0:TT, 6, c * 4:(c + 1) * 4]
                for m in range(c):
                    mm(o, ones[0:TT, 0:TT], rt[:, m * 4:(m + 1) * 4], m == 0, False)
                mm(o, before[:, :], rt[:, c * 4:(c + 1) * 4], c == 0, True)
            for m in range(NT):
                last = mm(ps[0:TT, 6, 16:20], ones[0:TT, 0:TT], rt[:, m * 4:(m + 1) * 4], m == 0, m == NT - 1)
            last.then_inc(reach("rank_ready"), 1)
            pe.wait_ge(*step("perm_ready"))
            for m in range(NT):
                last = mm(ps[0:NE, 7, 0:T], rt[:, 64 + m * NE:64 + (m + 1) * NE], perm[:, m, :], m == 0, m == NT - 1)
            last.then_inc(reach("cs_summed"), 1)
            pe.wait_ge(sem("htok_copied"), 12)
            for k in range(KT):
                if k >= 4:
                    pe.wait_ge(sem("hs_copied"), k - 3)
                for m in range(NT):
                    last = mm(ps[:, 2 + k % 4, 0:T], hTok[:, m, k * P:(k + 1) * P], perm[:, m, :], m == 0, m == NT - 1)
                last.then_inc(sem("hs_summed"), 1)
            for c in range(NT):
                for m in range(NT):
                    last = tr(ps[0:TT, 0 if c < 1 else (1 if c < 2 else 6), m * TT:(m + 1) * TT], perm[:, m, c * TT:(c + 1) * TT])
            last.then_inc(reach("perm_turned"), 1)
            pe.wait_ge(*step("perm_copied"))
            pe.wait_ge(*step("table_ready"))
            pe.wait_ge(*step("hs_ready"))

            windows = pe.value_load(wtab[0:1, 0:1], min_val=NG, max_val=MAXW)
            with pe.Fori(0, windows) as it:
                def wait_slot(j, n):
                    pe.wait_ge(sem(f"ring_full{(MOE + n) % SLOTS}"), it * (16 * EG) + (filled(MOE + n) + 16 * j))

                def project(j, which):
                    if which == 0:
                        pe.wait_ge(sem("gate_read"), it * EG + (j + 1))
                    else:
                        pe.wait_ge(sem("up_read"), it * EG + (j + 1))
                    bank = (4 + j % 2) if which == 0 else 6
                    for n in (2 * which, 2 * which + 1):
                        wait_slot(j, n)
                        for f in range(4):
                            for k in range(8):
                                wt = slot(MOE + n).rearrange("p (k n) -> p k n", k=8)[:, k, f * P:(f + 1) * P]
                                last = mm(ps[:, bank, f * W:(f + 1) * W], wt, hw[:, (n % 2) * 8 + k, :],
                                          n % 2 == 0 and f == 0 and k == 0, n % 2 == 1 and k == 7, free=True)
                        if n % 2 == 0:
                            last.then_inc(sem(f"ring_free{(MOE + n) % SLOTS}"), 1)
                    last.then_inc(sem(("gate_ready", "up_ready")[which]), 1)
                    release(("gate_ready", "up_ready")[which], it * EG + (j + 1), MOE + 2 * which + 1)

                def down(j):
                    pe.wait_ge(sem("hid_ready"), it * EG + (j + 1))
                    for n in (4, 5):
                        wait_slot(j, n)
                        for m in range(8):
                            dt = (n - 4) * 8 + m
                            for f in range(4):
                                wt = slot(MOE + n).rearrange("p (k n) -> p k n", k=4)[:, f, m * P:(m + 1) * P]
                                last = mm(ps[:, dt // 4, (dt % 4) * W:(dt % 4 + 1) * W], wt, hid[:, j % 2, f * W:(f + 1) * W],
                                          j == 0 and f == 0 and dt % 4 == 0, j == EG - 1 and f == 3, free=True)
                        last.then_inc(sem("down_done"), 1)
                        release("down_done", it * (2 * EG) + (2 * j + n - 3), MOE + n)

                pe.wait_ge(sem("window_ready"), it + 1)
                pe.wait_ge(sem("comb_read"), it + 1)
                for j in range(EG):
                    last = mm(ps[:, 7, j * W:(j + 1) * W], selw[:, j:j + 1].to_broadcast([NE, P]), cw, True, True)
                last.then_inc(sem("comb_ready"), 1)
                project(0, 0)
                project(0, 1)
                for j in range(EG):
                    if j + 1 < EG:
                        project(j + 1, 0)
                    if j == 0:
                        pe.wait_ge(sem("y_bank_free"), it + 1)
                    down(j)
                    if j + 1 < EG:
                        project(j + 1, 1)

            pe.wait_ge(*step("ys_ready"))
            for c in range(NT):
                for q in range(4):
                    n = 4 * c + q
                    if n >= 4:
                        pe.wait_ge(sem("ytok_copied"), n - 3)
                    for m in range(4):
                        last = tr(ps[0:TT, 4 + n % 4, m * P:(m + 1) * P], ys[:, 4 * q + m, c * TT:(c + 1) * TT])
                    last.then_inc(sem("ytok_turned"), 1)
            pe.wait_ge(sem("ytok_copied"), 12)
            for k in range(KT):
                if k >= 4:
                    pe.wait_ge(sem("x3_ready"), k - 3)
                for m in range(NT):
                    last = mm(ps[:, k % 4, 0:T], yTok[:, m, k * P:(k + 1) * P], permT[:, m, :], m == 0, m == NT - 1)
                last.then_inc(sem("y_summed"), 1)
            pe.wait_ge(sem("x3_squared"), KT)
            for k in range(KT):
                last = mm(ps[:, 4, 0:T], ones[:, :], sq2[:, k, :], k == 0, k == KT - 1)
            last.then_inc(reach("ss3_ready"), 1)
            for k in range(KT):
                pe.wait_ge(sem("xf_ready"), k + 1)
                if k >= 4:
                    pe.wait_ge(sem("out_copied"), k - 3)
                for c in range(2):
                    tr(ps[:, k % 4, c * P:(c + 1) * P], xT[:, k, c * P:(c + 1) * P])
                tr(ps[0:TS, k % 4, TP:TP + P], xT[:, k, TP:T]).then_inc(sem("out_turned"), 1)

        @block.scalar
        def _(act):
            def f(o, i, func, **kw):
                return nc.scalar.activation(o, i, func, **kw)

            act.dma_start(c_in[0:1, :], io["c_prompt"]).then_inc(sem("c_loaded"), 16)
            act.dma_start(c_in[1:NC, :], io["c_sample"]).then_inc(sem("c_loaded"), 16)

            def load(dst, src):
                act.dma_start(dst, src).then_inc(sem("small_loaded"), 16)

            load(bada_rows, io["b_ada"].rearrange("a (r n) -> (a r) n", n=P))
            for n, name in enumerate(("g_norm1", "g_norm2")):
                load(vec_rows[n * 16:(n + 1) * 16, :], io[name].rearrange("a (r n) -> (a r) n", n=P))
            load(vec_rows[32:48, :], io["g_final"].rearrange("(r n) -> r n", n=P))
            load(vec_rows[48:52, :], io["b_a"].rearrange("a (r n) -> (a r) n", n=P))
            load(vec_rows[52:54, :], io["g_gla_norm"].rearrange("a (r n) -> (a r) n", n=P))
            load(brow[:, 0:4], io["b_grp"])
            load(brow[:, 4:20], io["b_exp"])
            load(bfc[:, :], io["b_f"].rearrange("a (h o) -> (a h) o", o=1))
            load(ptab[:, :], io["page_table"].rearrange("(a b) n -> a (b n)", a=1))
            act.wait_ge(sem("w_small_clear"), 1)
            act.dma_start(w_small[:, :, 0:16], io["w_in"][0, :, COL_LRA:COL_LRA + 16].rearrange("(k p) n -> p k n", p=P)).then_inc(sem("w_small_loaded"), 16)
            act.dma_start(w_small[:, :, 32:40], io["w_in"][0, :, COL_FB:COL_FB + 8].rearrange("(k p) n -> p k n", p=P)).then_inc(sem("w_small_loaded"), 16)

            for k in range(KT):
                act.wait_ge(sem("xT_copied"), k + 1)
                f(sq[:, k, :], xT[:, k, :], ACT.Square).then_inc(sem("xT_squared"), 1)
            act.wait_ge(*step("ss1_ready"))
            act.wait_ge(sem("c_loaded"), 32)
            f(c_sig[0:NC, :], c_in[0:NC, :], ACT.Sigmoid).then_inc(reach("c_sig_ready"), 1)
            act.wait_ge(*step("ms1_ready"))
            f(ms[:, :], ms[:, :], ACT.Sqrt).then_inc(reach("root1_ready"), 1)
            for j in range(3):
                act.wait_ge(sem("mod_summed"), j + 1)
                f(mod_row[:, j, :], ps[:, j, :], ACT.Copy).then_inc(sem("mod_row_ready"), 1)
            for k in range(KT):
                act.wait_ge(sem("h1_scaled"), k + 1)
                f(hT[:, k, 0:TP], hT[:, k, 0:TP], ACT.Identity, bias=modT[:, k, 0:1]).then_inc(sem("h1_shifted"), 1)
            def win_round(i, late_too):
                for n in range(1, 12, 2):
                    act.wait_ge(sem("win_tile"), i * 12 + (n + 1))
                    f(z[:, ds(i * (12 * T) + n * T, T)], ps[:, n % 6, 0:T], ACT.Copy).then_inc(sem("win_bank_free1"), 1)
                    if n == 9 and late_too:
                        act.wait_ge(sem("mod_summed"), i + 4)
                        act.wait_ge(sem("mod_turned"), i + 3)
                        f(mod_row[:, 2, :], ps[:, 7, :], ACT.Copy).then_inc(sem("mod_row_ready"), 1)

            with act.Fori(0, 3) as i:
                win_round(i, True)
            win_round(3, False)
            act.wait_ge(*step("lra_fb_ready"))
            act.dma_start(wa2, io["w_a2"][0]).then_inc(sem("wa2_loaded"), 16)
            act.wait_ge(sem("za_abs"), 1)
            f(buf[0], buf[0], ACT.Exp, scale=-1.0).then_inc(reach("za_exp"), 1)
            act.wait_ge(sem("zf_abs"), 1)
            f(ms[0:H_B, :], ms[0:H_B, :], ACT.Exp, scale=-1.0).then_inc(reach("zf_exp"), 1)
            for n, b in enumerate(LEVELS):
                act.wait_ge(sem("level_rel"), n + 1)
                tt = T if b <= 2 else TP
                for m, half in ((0, 1), (1, 0)):
                    v = buf3[m][:, :, 0:tt].rearrange("p h (n two t) -> p h n two t", two=2, t=b)[:, :, :, half, :]
                    last = f(v, v, ACT.Exp)
                last.then_inc(sem("level_exp"), 1)
            act.wait_ge(*step("decay_rel"))
            f(buf[2], buf[2], ACT.Exp)
            f(buf[3], buf[3], ACT.Exp)
            f(decay, decay, ACT.Exp).then_inc(reach("decay_exp"), 1)
            act.wait_ge(*step("oa_copied"))
            act.wait_ge(*step("os_turned_copied"))
            f(sq8, oaT, ACT.Square).then_inc(reach("oa_squared"), 1)
            act.wait_ge(*step("ms_a_ready"))
            f(rs4, rs4, ACT.Sqrt).then_inc(reach("root_a_ready"), 1)
            act.wait_ge(sem("state_updated"), DB)
            f(sig8, ra, ACT.Sigmoid).then_inc(reach("ra_sig"), 1)
            for h in range(H_B):
                act.wait_ge(sem("fox_max"), h + 1)
                if h >= 2:
                    act.wait_ge(sem("fox_turned"), h - 1)
                for q in range(2):
                    lo, n = q * P, P * (q + 1)
                    last = f(prob[:, h % 2, lo:lo + n], ps[:, 1 + h % 2, lo:lo + n], ACT.Exp,
                             bias=st_p[:, 4 * (h % 2) + q:4 * (h % 2) + q + 1],
                             accum_out=st_p[:, 8 + 4 * (h % 2) + q:8 + 4 * (h % 2) + q + 1])
                last.then_inc(sem("fox_exp"), 1)
            with act.Fori(0, DB) as b:
                for n in range(1, 16, 2):
                    act.wait_ge(sem("kt_turned_s"), b * 16 + (n + 1))
                    if n // 4 >= 2:
                        act.wait_ge(sem("s_scored"), b * 4 + (n // 4 - 1))
                    f(ktR[:, 4 * ((n // 4) % 2) + n % 4, :], ps[:, 5, :], ACT.Copy).then_inc(sem("kt_copied1"), 1)
                for g in range(2):
                    act.wait_ge(sem("s_max"), b * 2 + (g + 1))
                    f(pS[:, g, 0:PAST].rearrange("p (a n) -> p a n", a=2), ps[:, 2 * g:2 * g + 2, :], ACT.Exp,
                      bias=st_s[:, 4 * g:4 * g + 1], accum_out=st_s[:, 4 * g + 1:4 * g + 2])
                    f(pS[:, g, PAST:PAST + TS], s_new[:, g, :], ACT.Exp,
                      bias=st_s[:, 4 * g + 3:4 * g + 4], accum_out=st_s[:, 4 * g + 2:4 * g + 3]).then_inc(sem("s_prob"), 1)
            with act.Fori(0, 4) as g:
                for n in (0, 1, 2, 3, 8, 9, 10, 11):
                    act.wait_ge(sem("up_tile"), g * 16 + (n + 1))
                    m = n if n < 4 else n - 4
                    if n == 0:
                        act.wait_ge(sem("merged"), g * 4 + 1)
                    f(sig_ab[:, m, :], ps[:, n % 8, 0:T], ACT.Sigmoid).then_inc(sem("gate_sig"), 1)
            act.wait_ge(sem("merged"), 17)
            act.dma_start(wrt[:, :, 0:4], io["w_grp"][0].rearrange("(k p) n -> p k n", p=P)).then_inc(sem("router_loaded"), 16)
            act.dma_start(wrt[:, :, 4:20], io["w_exp"][0].rearrange("(k p) n -> p k n", p=P)).then_inc(sem("router_loaded"), 16)
            for k in range(KT):
                act.wait_ge(sem("x2_ready"), k + 1)
                f(sq2[:, k, :], xT[:, k, :], ACT.Square).then_inc(sem("x2_squared"), 1)
            act.wait_ge(*step("ms2_ready"))
            f(ms[:, :], ms[:, :], ACT.Sqrt).then_inc(reach("root2_ready"), 1)
            for k in range(KT):
                act.wait_ge(sem("h2_scaled"), k + 1)
                f(hT[:, k, 0:TP], hT[:, k, 0:TP], ACT.Identity, bias=modT[:, 48 + k, 0:1]).then_inc(sem("h2_shifted"), 1)
            act.wait_ge(sem("rt_shifted"), 1)
            f(rt[:, 400:412], rt[:, 400:412], ACT.Exp).then_inc(sem("rt_exp"), 1)
            act.wait_ge(sem("rt_shifted"), 2)
            f(rt[:, 420:423], rt[:, 420:423], ACT.Exp).then_inc(sem("rt_exp"), 1)
            for n in range(12):
                act.wait_ge(sem("htok_turned"), n + 1)
                f(hTok[:, n // 4, (n % 4) * 512:(n % 4 + 1) * 512], ps[0:TT, 2 + n % 4, :], ACT.Copy).then_inc(sem("htok_copied"), 1)
            act.wait_ge(*step("table_ready"))
            windows = act.value_load(wtab[0:1, 0:1], min_val=NG, max_val=MAXW)
            with act.Fori(0, windows) as it:
                for j in range(EG):
                    act.wait_ge(sem("gate_ready"), it * EG + (j + 1))
                    act.wait_ge(sem("sg_free"), it * EG + (j + 1))
                    f(sg, ps[:, 4 + j % 2, :], ACT.Sigmoid).then_inc(sem("sg_ready"), 1)
            for n in range(12):
                act.wait_ge(sem("ytok_turned"), n + 1)
                f(yTok[:, n // 4, (n % 4) * 512:(n % 4 + 1) * 512], ps[0:TT, 4 + n % 4, :], ACT.Copy).then_inc(sem("ytok_copied"), 1)
            for k in range(KT):
                act.wait_ge(sem("x3_ready"), k + 1)
                f(sq2[:, k, :], xT[:, k, :], ACT.Square).then_inc(sem("x3_squared"), 1)
            act.wait_ge(*step("ms3_ready"))
            f(ms[:, :], ms[:, :], ACT.Sqrt).then_inc(reach("root3_ready"), 1)

        @block.vector
        def _(v):
            def tt(o, a, b, op):
                return nc.vector.tensor_tensor(o, a, b, op)

            def tsc(o, a, s1, s2, op0, op1=None):
                return nc.vector.tensor_scalar(o, a, s1, s2, op0) if op1 is None else nc.vector.tensor_scalar(o, a, s1, s2, op0, op1)

            def stt(o, a, s, b, op0, op1):
                return nc.vector.scalar_tensor_tensor(out=o, in0=a, scalar=s, in1=b, op0=op0, op1=op1)

            def copy(o, a):
                return nc.vector.tensor_copy(o, a)

            for name, n in (("late_free0", 1), ("late_free1", 1), ("win_bank_free0", 3), ("win_bank_free1", 3),
                            ("up_bank_free", 8), ("gate_read", 2),
                            ("merged", 1), ("o_all_ready", 1), ("kt_copied0", 1), ("kt_copied1", 1),
                            *((f"ring_free{s}", 1) for s in range(SLOTS)),
                            ("up_read", 1), ("comb_read", 1), ("y_bank_free", 1), ("sg_free", 1)):
                v.sem_inc(sem(name), n)

            for k in range(KT):
                v.wait_ge(sem("xT_turned"), k + 1)
                copy(xT[:, k, :], ps[:, k % 4, 0:T]).then_inc(sem("xT_copied"), 1)
            v.wait_ge(*step("ss1_ready"))
            tsc(ms[:, :], ps[:, 4, 0:T], 1.0 / D, EPS, ALU.mult, ALU.add).then_inc(reach("ms1_ready"), 1)
            v.wait_ge(*step("c_sig_ready"))
            tt(c_in[0:NC, :], c_in[0:NC, :], c_sig[0:NC, :], ALU.mult).then_inc(reach("c_silu"), 1)
            nc.vector.memset(cT, 0.0)
            v.drain()
            v.wait_ge(*step("c_turned"))
            copy(cT[:, :, 0:NC], ps[:, 5, 0:KT * NC].rearrange("p (k c) -> p k c", c=NC)).then_inc(reach("cT_ready"), 1)
            v.wait_ge(*step("root1_ready"))
            nc.vector.reciprocal(rstd[:, :], ms[:, :])
            v.wait_ge(*step("vec_turned"))
            copy(vcol[:, 0:150], ps[:, 6, 0:150])
            v.drain()

            def add_bias(section, bank):
                v.wait_ge(sem("mod_turned"), section + 1)
                at = section * KT
                at = slice(at, at + KT) if isinstance(section, int) else ds(at, KT)
                o = modT[:, at, :].rearrange("p (c t) n -> p t c n", c=4)
                s = ps[:, bank, :].rearrange("p (t c n) -> p t c n", t=4, c=4)[:, :, :, 0:NC]
                bias = vcol[:, at].rearrange("p (c t) -> p t c", c=4).unsqueeze(3).to_broadcast([P, 4, 4, NC])
                tt(o, s, bias, ALU.add).then_inc(sem("mod_ready"), 1)

            for j in range(3):
                add_bias(j, 3 + j)
            v.wait_ge(sem("mod_ready"), 3)

            def modulate(tag, shift, scale, gain):
                stt(mod_a[:, :, :], modT[:, scale:scale + KT, :], 1.0,
                    vcol[:, gain:gain + KT].unsqueeze(2).to_broadcast([P, KT, NC]), ALU.add, ALU.mult)
                v.drain()
                for k in range(KT):
                    stt(hT[:, k, 0:TP], xT[:, k, 0:TP], mod_a[:, k, 0:1], rstd[:, 0:TP], ALU.mult, ALU.mult).then_inc(sem(f"{tag}_scaled"), 1)
                hsv = hT[:, :, TP:T]
                h4 = hsv.rearrange("p k (b t) -> p k b t", t=DT)
                tt(hsv, xT[:, :, TP:T], rstd[:, TP:T].unsqueeze(1).to_broadcast([P, KT, TS]), ALU.mult)
                v.drain()
                tt(h4, h4, mod_a[:, :, 1:NC].unsqueeze(3).to_broadcast([P, KT, DB, DT]), ALU.mult)
                v.drain()
                tt(h4, h4, modT[:, shift:shift + KT, 1:NC].unsqueeze(3).to_broadcast([P, KT, DB, DT]), ALU.add)
                v.drain()
                v.wait_ge(sem(f"{tag}_shifted"), KT)
                v.sem_inc(sem(f"{tag}_ready"), 1)

            modulate("h1", 0, KT, V_G1)
            def win_round(i, late_too):
                for n in range(0, 12, 2):
                    v.wait_ge(sem("win_tile"), i * 12 + (n + 1))
                    copy(z[:, ds(i * (12 * T) + n * T, T)], ps[:, n % 6, 0:T]).then_inc(sem("win_bank_free0"), 1)
                if late_too:
                    add_bias(i + 3, 6)

            with v.Fori(0, 3) as i:
                win_round(i, True)
            win_round(3, False)
            v.wait_ge(*step("lra_fb_ready"))
            v.wait_ge(sem("small_loaded"), 16 * N_SMALL)
            tsc(fT[:, :], ps[32:40, 6, 0:T], bfc[:, 0:1], None, ALU.add)
            copy(lraT, ps[0:16, 6, 0:T]).then_inc(reach("lra_copied"), 1)
            v.wait_ge(*step("za_ready"))
            for h in range(H_A):
                last = tsc(la[:, h, :], ps[:, h, 0:T], vcol[:, V_BA + h:V_BA + h + 1], None, ALU.add)
            last.then_inc(reach("za_read"), 1)
            v.drain()

            def log_sigmoid(x, e, a, b, c, tag, scale):
                tsc(e, x, -1.0, None, ALU.mult)
                v.drain()
                tt(e, e, x, ALU.max).then_inc(sem(f"{tag}_abs"), 1)
                tsc(x, x, 0.0, None, ALU.min)
                v.wait_ge(*step(f"{tag}_exp"))
                tsc(a, e, 2.0, None, ALU.add)
                v.drain()
                nc.vector.reciprocal(a, a)
                v.drain()
                tt(a, a, e, ALU.mult)
                v.drain()
                tt(b, a, a, ALU.mult)
                v.drain()
                tsc(c, b, 1.0 / 17, None, ALU.mult)
                for n in (15, 13, 11, 9, 7, 5, 3):
                    v.drain()
                    stt(c, c, 1.0 / n, b, ALU.add, ALU.mult)
                v.drain()
                stt(c, c, 1.0, a, ALU.add, ALU.mult)
                v.drain()
                stt(x, c, -2.0, x, ALU.mult, ALU.add)
                v.drain()
                if scale != 1.0:
                    tsc(x, x, scale, None, ALU.mult)
                    v.drain()

            laf = wk[:, 0:F4]
            log_sigmoid(laf, buf[0], buf[1], buf[2], buf[3], "za", 1.0 / 16)
            log_sigmoid(fT[:, :], ms[0:H_B, :], fa, fb_, fc, "zf", 1.0)
            v.sem_inc(reach("logf_ready"), 1)
            for h in range(H_A):
                for c in range(2):
                    nc.vector.tensor_tensor_scan(cum[:, h, c * P:(c + 1) * P], ones[:, :], la[:, h, c * P:(c + 1) * P], 0.0, ALU.mult, ALU.add)
            cs4 = cum[:, :, TP:T].rearrange("p h (b t) -> p h b t", t=DT)
            copy(cum[:, :, TP:T], la[:, :, TP:T])
            tsc(qa, qa, SCALE, None, ALU.mult)
            tsc(qb, qb, SCALE, None, ALU.mult)
            nc.vector.memset(buf[0], 0.0)
            nc.vector.memset(buf[1], 0.0)
            v.drain()
            for t in range(1, DT):
                tt(cs4[:, :, :, t], cs4[:, :, :, t - 1], cs4[:, :, :, t], ALU.add)
                v.drain()
            v.wait_ge(*step("va_turned"))
            for c in range(2):
                copy(vaTok[:, c, :].rearrange("p (a n) -> p a n", a=2), ps[:, 4 + 2 * c:6 + 2 * c, :])
            copy(vaS.rearrange("p (a n) -> p a n", a=2), ps[0:TS, 0:2, :])
            v.drain()
            v.sem_inc(reach("va_copied"), 1)
            v.wait_ge(sem("masks_ready"), 1)
            v.wait_ge(sem("consts_ready"), 1)
            def add_level(n):
                v.wait_ge(sem("level_scored"), n + 1)
                b0 = 3 * (n % 2)
                mask = level_mask[:, n, :] if n < len(LEVELS) else ident[:, :]
                tmp = laf[:, 0:1024].rearrange("p (c h t) -> p c h t", c=2, h=H_A)
                dst = atP if n == 0 else tmp
                for c in range(2):
                    tt(dst[:, c], ps[:, b0 + c, :].rearrange("p (h t) -> p h t", h=H_A),
                       mask.unsqueeze(1).to_broadcast([P, H_A, P]), ALU.mult)
                first_s = len(LEVELS) - 2
                tmps = laf[0:TS, 1024:1152].rearrange("p (h t) -> p h t", h=H_A)
                if n >= first_s:
                    tt(atS if n == first_s else tmps, ps[0:TS, b0 + 2, 0:H_A * TS].rearrange("p (h t) -> p h t", h=H_A),
                       mask[0:TS, 0:TS].unsqueeze(1).to_broadcast([TS, H_A, TS]), ALU.mult)
                v.drain()
                v.sem_inc(sem("level_read"), 1)
                if n:
                    tt(atP, atP, tmp, ALU.add)
                if n > first_s:
                    tt(atS, atS, tmps, ALU.add)
                v.drain()

            for n, b in enumerate(LEVELS):
                tm = T if b <= 2 else TP

                def pairs(a):
                    return a[:, :, 0:tm].rearrange("p h (n two t) -> p h n two t", two=2, t=b)

                np_ = tm // (2 * b)
                cv, qv, kv = pairs(cum), pairs(buf3[0]), pairs(buf3[1])
                if n:
                    v.wait_ge(sem("level_scored"), n)
                for h in range(H_A):
                    ref = cv[:, h, :, 0, b - 1:b].to_broadcast([P, np_, b])
                    tt(qv[:, h, :, 1, :], cv[:, h, :, 1, :], ref, ALU.subtract)
                    last = tt(kv[:, h, :, 0, :], ref, cv[:, h, :, 0, :], ALU.subtract)
                last.then_inc(sem("level_rel"), 1)
                if n:
                    add_level(n - 1)
                v.wait_ge(sem("level_exp"), n + 1)
                for h in range(H_A):
                    tt(qv[:, h, :, 1, :], qv[:, h, :, 1, :], pairs(qa)[:, h, :, 1, :], ALU.mult)
                    last = tt(kv[:, h, :, 0, :], kv[:, h, :, 0, :], pairs(ka)[:, h, :, 0, :], ALU.mult)
                v.drain()
                v.sem_inc(sem("level_ready"), 1)
            v.sem_inc(sem("level_ready"), 1)
            copy(buf3[2], cum)
            for c in range(2):
                e = (c + 1) * P
                tt(buf3[3][:, :, c * P:e], cum[:, :, e - 1:e].to_broadcast([P, H_A, P]), cum[:, :, c * P:e], ALU.subtract)
                copy(decay[:, :, c:c + 1], cum[:, :, e - 1:e])
            for h in range(H_A):
                tt(buf3[3][:, h, TP:T].rearrange("p (b t) -> p b t", t=DT), cs4[:, h, :, DT - 1:DT].to_broadcast([P, DB, DT]),
                   cs4[:, h], ALU.subtract)
            copy(decay[:, :, 2:10], cs4[:, :, :, DT - 1])
            v.drain()
            v.sem_inc(reach("decay_rel"), 1)
            add_level(len(LEVELS) - 1)
            v.wait_ge(*step("decay_exp"))
            tt(buf3[2], buf3[2], qa, ALU.mult)
            tt(buf3[3], buf3[3], ka, ALU.mult)
            v.drain()
            v.sem_inc(reach("decayed_ready"), 1)
            add_level(len(LEVELS))
            v.wait_ge(*step("kt_turned"))
            copy(ktP, ps[:, 6:8, :])
            copy(ktS, ps[0:TS, 0, :])
            v.drain()
            v.sem_inc(reach("kt_copied"), 1)
            v.wait_ge(*step("state1_ready"))
            copy(stP.rearrange("p (a h) v -> p a (h v)", a=2), ps[:, 4:6, :]).then_inc(reach("state1_copied"), 1)
            v.wait_ge(*step("oa_ready"))
            copy(oaT[:, :, 0:TP].rearrange("p (a n) t -> p a n t", a=4), ps[:, 0:4, :].rearrange("p a (n t) -> p a n t", n=2)).then_inc(reach("oa_copied"), 1)
            v.wait_ge(*step("update2_ready"))
            for h in range(H_A):
                last = stt(stP[:, h, :], stP[:, h, :], decay[:, h, 1:2], ps[:, 6 + h // 2, (h % 2) * DV:(h % 2 + 1) * DV], ALU.mult, ALU.add)
            v.drain()
            v.sem_inc(reach("gla_prompt_ready"), 1)
            v.sem_inc(reach("update2_used"), 1)
            v.wait_ge(*step("os_own_ready"))
            copy(osS, ps[:, 4, 0:DV])
            v.wait_ge(*step("os_state_ready"))
            for b in range(DB):
                v.drain()
                stt(osS, ps[:, b // 2, (b % 2) * DV:(b % 2 + 1) * DV], own_seq[:, b:b + 1], osS, ALU.mult, ALU.add)
            v.drain()
            v.sem_inc(reach("os_summed"), 1)
            for b in range(DB):
                if b:
                    v.wait_ge(sem("update_ready"), b)
                tsc(kmS, ktS, own_seq[0:TS, b:b + 1], None, ALU.mult).then_inc(sem("km_ready"), 1)
                v.wait_ge(sem("update_ready"), b + 1)
                for h in range(H_A):
                    last = stt(state[:, b, h, :], state[:, b, h, :], decay[:, h, 2 + b:3 + b],
                               ps[:, 6 + h // 2, (h % 2) * DV:(h % 2 + 1) * DV], ALU.mult, ALU.add)
                last.then_inc(sem("state_updated"), 1)
            v.wait_ge(sem("state_updated"), DB)
            v.sem_inc(reach("gla_sample_ready"), 1)
            v.wait_ge(*step("os_turned"))
            for w in range(VB):
                copy(oaT[:, :, TP:T].rearrange("p (h w) t -> p w h t", w=VB)[:, w], ps[:, 4, w * P:(w + 1) * P].rearrange("p (h t) -> p h t", h=H_A))
            v.drain()
            v.sem_inc(reach("os_turned_copied"), 1)
            v.wait_ge(sem("gla_prompt_stored"), 16)
            v.sem_inc(reach("gla_scratch_free"), 1)
            v.wait_ge(*step("ss_a_ready"))
            tsc(rs4, ps[:, 0:4, 0:T], 1.0 / DV, EPS, ALU.mult, ALU.add)
            v.drain()
            v.sem_inc(reach("ms_a_ready"), 1)
            v.sem_inc(reach("rs_a_ready"), 1)
            v.wait_ge(*step("root_a_ready"))
            nc.vector.reciprocal(rs4, rs4)
            v.wait_ge(*step("ra_sig"))
            tt(ra, ra, sig8, ALU.mult)
            v.drain()
            for n in range(8):
                stt(oaT[:, n, :], oaT[:, n, :], vcol[:, V_GG + n % 2:V_GG + n % 2 + 1], rs4[:, n // 2, :], ALU.mult, ALU.mult)
            v.drain()
            tt(oaT, oaT, ra, ALU.mult)
            v.drain()
            v.sem_inc(reach("oa_final"), 1)

            v.wait_ge(sem("tok_turned"), 1)
            for c in range(2):
                copy(kbTok[:, c, :].rearrange("p (a n) -> p a n", a=2), ps[:, 4 + 2 * c:6 + 2 * c, :])
            v.drain()
            v.sem_inc(sem("tok_copied"), 1)
            v.wait_ge(sem("tok_turned"), 2)
            vtmp = wk[:, 0:2048].rearrange("p (c n) -> p c n", c=2)
            for c in range(2):
                copy(vtmp[:, c, :].rearrange("p (a n) -> p a n", a=2), ps[:, 4 + 2 * c:6 + 2 * c, :])
            v.drain()
            v.sem_inc(sem("tok_copied"), 1)
            v.wait_ge(sem("tok_turned"), 3)
            v.wait_ge(*step("gla_prompt_ready"))
            copy(kbS.rearrange("p (a n) -> p a n", a=2), ps[0:TS, 4:6, :])
            copy(vbS.rearrange("p (a n) -> p a n", a=2), ps[0:TS, 6:8, :])
            copy(vbTok, vtmp)
            v.wait_ge(*step("lf_turned"))
            copy(lfTok[:, 0:2, :], ps[:, 0, 0:16].rearrange("p (c h) -> p c h", c=2))
            copy(lfTok[0:TS, 2, :], ps[0:TS, 0, 16:24])
            v.drain()
            v.sem_inc(sem("tok_copied"), 2)
            v.sem_inc(reach("kv_tok_ready"), 1)
            nc.vector.tensor_tensor_scan(nfT[:, 0:TP], ones[0:H_B, 0:1].to_broadcast([H_B, TP]), fT[:, 0:TP], 0.0, ALU.mult, ALU.add)
            f4 = fT[:, TP:T].rearrange("p (b t) -> p b t", t=DT)
            for t in range(1, DT):
                tt(f4[:, :, t], f4[:, :, t - 1], f4[:, :, t], ALU.add)
                v.drain()
            copy(fT[:, 0:TP], nfT[:, 0:TP])
            v.drain()
            tsc(nfT[:, :], fT[:, :], -1.0, None, ALU.mult)
            v.drain()
            v.sem_inc(reach("f_ready"), 1)
            for i in range(H_B + 1):
                if i < H_B:
                    h = i
                    v.wait_ge(sem("fox_scored"), h + 1)
                    diag = ps[:, 1 + h % 2, :].rearrange("p (n q) -> p n q", q=P)[:, 0:3:2, :]
                    tt(diag, diag, fox_mask[:, :].unsqueeze(1).to_broadcast([P, 2, P]), ALU.add)
                    v.drain()
                    for q in range(2):
                        lo, n = q * P, P * (q + 1)
                        nc.vector.tensor_reduce(st_p[:, 4 * (h % 2) + q:4 * (h % 2) + q + 1], ps[:, 1 + h % 2, lo:lo + n], AX.X, ALU.max, negate=True)
                    v.drain()
                    v.sem_inc(sem("fox_max"), 1)
                if 1 <= i <= H_B:
                    h = i - 1
                    v.wait_ge(sem("fox_exp"), h + 1)
                    den = st_p[:, 8 + 4 * (h % 2):10 + 4 * (h % 2)]
                    nc.vector.reciprocal(den, den)
                    v.drain()
                    for q in range(2):
                        lo, n = q * P, P * (q + 1)
                        tsc(prob[:, h % 2, lo:lo + n], prob[:, h % 2, lo:lo + n], den[:, q:q + 1], None, ALU.mult)
                    v.drain()
                    v.sem_inc(sem("fox_prob"), 1)
                    v.wait_ge(sem("fox_turned"), h + 1)
                    if h >= 2:
                        v.wait_ge(sem("fox_pv"), h - 1)
                    copy(probT[:, h % 2, :], ps[:, 3, 0:3 * P]).then_inc(sem("fox_pt"), 1)
                    v.wait_ge(sem("fox_pv"), h + 1)
                    copy(obT[:, h, 0:TP], ps[:, 4 + h % 2, 0:TP]).then_inc(sem("fox_out"), 1)

            v.wait_ge(sem("kv_stored"), 6 * 16)
            v.sem_inc(sem("lf_used"), 1)
            v.wait_ge(*step("s_new_ready"))
            tt(s_new, ps[:, 0, 0:2 * TS].rearrange("p (g t) -> p g t", g=2), new_mask[:, :].unsqueeze(1).to_broadcast([P, 2, TS]), ALU.add)
            copy(fn_r, ps[:, 1, 0:2])
            nc.vector.memset(o_all, 0.0)
            v.drain()
            v.sem_inc(reach("s_new_copied"), 1)
            with v.Fori(0, DB) as b:
                v.wait_ge(sem("lf_loaded"), b * (16 * NPG) + 16 * NPG)
                nc.vector.memset(lf_b[:, NPG - 1:NPG, :], 0.0)
                v.drain()
                for n in range(NPG - 2, -1, -1):
                    tt(lf_b[:, n, :], lf_b[:, n + 1, :], lf_in[:, n + 1, :], ALU.add)
                    v.drain()
                v.sem_inc(sem("lf_summed"), 1)
                v.wait_ge(sem("r_ready"), b + 1)
                copy(rT.rearrange("p (a n) -> p a n", a=2), ps[0:H_B, 6:8, :]).then_inc(sem("r_copied"), 1)
                v.sem_inc(sem("lf_used"), 1)
                for n in range(0, 16, 2):
                    v.wait_ge(sem("kt_turned_s"), b * 16 + (n + 1))
                    if n // 4 >= 2:
                        v.wait_ge(sem("s_scored"), b * 4 + (n // 4 - 1))
                    copy(ktR[:, 4 * ((n // 4) % 2) + n % 4, :], ps[:, 4, :]).then_inc(sem("kt_copied0"), 1)
                for g in range(2):
                    m = st_s[:, 4 * g:4 * g + 1]
                    v.wait_ge(sem("s_scored"), b * 4 + (3 + g))
                    nc.vector.tensor_reduce(st_s[:, 16 + 4 * g:17 + 4 * g], ps[:, 2 * g:2 * g + 2, :], AX.XY, ALU.max)
                    nc.vector.tensor_reduce(st_s[:, 17 + 4 * g:18 + 4 * g], s_new[:, g, :], AX.X, ALU.max)
                    v.drain()
                    tt(st_s[:, 16 + 4 * g:17 + 4 * g], st_s[:, 16 + 4 * g:17 + 4 * g], fn_r[:, g:g + 1], ALU.add)
                    v.drain()
                    tt(st_s[:, 18 + 4 * g:19 + 4 * g], st_s[:, 16 + 4 * g:17 + 4 * g], st_s[:, 17 + 4 * g:18 + 4 * g], ALU.max)
                    v.drain()
                    tsc(st_s[:, 4 * g + 3:4 * g + 4], st_s[:, 18 + 4 * g:19 + 4 * g], -1.0, None, ALU.mult)
                    tt(m, fn_r[:, g:g + 1], st_s[:, 18 + 4 * g:19 + 4 * g], ALU.subtract)
                    v.drain()
                    v.sem_inc(sem("s_max"), 1)
                for n in range(5):
                    v.wait_ge(sem("pt_turned"), b * 5 + (n + 1))
                    if n < 4:
                        last = copy(pTS[:, n // 2, 4 * (n % 2):4 * (n % 2) + 4, :], ps[:, 6 + n % 2, :].rearrange("p (n t) -> p n t", n=4))
                    else:
                        last = copy(pTN, ps[0:TS, 6, 0:2 * P].rearrange("p (g t) -> p g t", g=2))
                    last.then_inc(sem("pt_copied"), 1)
                for g in range(2):
                    tt(st_s[:, 24 + g:25 + g], st_s[:, 4 * g + 1:4 * g + 2], st_s[:, 4 * g + 2:4 * g + 3], ALU.add)
                v.drain()
                nc.vector.reciprocal(st_s[:, 24:26], st_s[:, 24:26])
                v.drain()
                tsc(st_s[:, 26:28], st_s[:, 24:26], own_seq[:, ds(b, 1)], None, ALU.mult)
                v.drain()
                v.wait_ge(sem("o_b_ready"), b + 1)
                for g in range(2):
                    last = stt(o_all[:, g, :], ps[:, 5, g * P:(g + 1) * P], st_s[:, 26 + g:27 + g], o_all[:, g, :], ALU.mult, ALU.add)
                v.drain()
                v.sem_inc(sem("o_all_ready"), 1)
            v.wait_ge(*step("o_all_turned"))
            copy(obT[:, :, TP:T].rearrange("p (g c) t -> p g c t", g=2), ps[:, 0, 0:2 * P].rearrange("p (g c t) -> p g c t", g=2, c=4))
            v.drain()
            v.sem_inc(reach("ob_ready"), 1)
            v.sem_inc(reach("work_free"), 1)

            with v.Fori(0, 4) as g:
                for half in range(2):
                    for t in range(4):
                        v.wait_ge(sem("gate_sig"), g * 8 + (4 * half + t + 1))
                        v.sem_inc(sem("up_bank_free"), 1)
                    for t in range(4):
                        tile, m = 8 * half + 4 + t, 4 * half + t
                        v.wait_ge(sem("up_tile"), g * 16 + (tile + 1))
                        tt(sig_ab[:, m, :], sig_ab[:, m, :], ps[:, tile % 8, 0:T], ALU.mult)
                        v.drain()
                        v.sem_inc(sem("up_bank_free"), 1)
                        if half:
                            tt(mgT[:, ds(g * 4 + t, 1), :].rearrange("p a t -> p (a t)"), sig_ab[:, t, :], sig_ab[:, m, :], ALU.add)\
                                .then_inc(sem("merged"), 1)

            def gated_add(k, bank, gate):
                stt(xT[:, k, 0:TP], ps[:, bank, 0:TP], modT[:, gate + k, 0:1], xT[:, k, 0:TP], ALU.mult, ALU.add)
                tt(shifted[:, :].rearrange("p (b t) -> p b t", t=DT), ps[:, bank, TP:T].rearrange("p (b t) -> p b t", t=DT),
                   modT[:, gate + k, 1:NC].unsqueeze(2).to_broadcast([P, DB, DT]), ALU.mult)
                v.drain()
                tt(xT[:, k, TP:T], xT[:, k, TP:T], shifted[:, :], ALU.add)
                v.drain()

            for k in range(KT):
                v.wait_ge(sem("wout_tile"), k + 1)
                gated_add(k, k % 8, 2 * KT)
                v.sem_inc(sem("up_bank_free"), 1)
                v.sem_inc(sem("x2_ready"), 1)
            v.wait_ge(*step("ss2_ready"))
            tsc(ms[:, :], ps[:, 0, 0:T], 1.0 / D, EPS, ALU.mult, ALU.add).then_inc(reach("ms2_ready"), 1)
            v.wait_ge(*step("root2_ready"))
            nc.vector.reciprocal(rstd[:, :], ms[:, :])
            v.drain()
            modulate("h2", 3 * KT, 4 * KT, V_G2)

            lg = rt[:, 340:400].rearrange("p (c n) -> p c n", c=NT)
            oh = rt[:, 0:12].rearrange("p (c n) -> p c n", c=NT)
            comb = rt[:, 64:64 + NT * NE].rearrange("p (c g j) -> p c g j", c=NT, g=NG)
            gx = rt[:, 400:412].rearrange("p (c n) -> p c n", c=NT)
            e2 = rt[:, 420:423]
            mx = rt[:, 430:433]
            gw = rt[:, 440:443]
            t4 = rt[:, 450:462].rearrange("p (c n) -> p c n", c=NT)
            ein = rt[:, 470:482].rearrange("p (c n) -> p c n", c=NT)
            oh1 = rt[:, 490:502].rearrange("p (c n) -> p c n", c=NT)
            oh2 = rt[:, 510:522].rearrange("p (c n) -> p c n", c=NT)
            m1, m2, w1 = rt[:, 530:533], rt[:, 540:543], rt[:, 550:553]
            prod = rt[:, 120:168].rearrange("p (c g j) -> p c g j", c=NT, g=NG)

            def spread(a):
                return a.unsqueeze(2).to_broadcast([TT, NT, 4])

            def red(o, i, op):
                return nc.vector.tensor_reduce(o, i, AX.X, op)

            def first_max(o, i, m):
                red(m, i, ALU.max)
                v.drain()
                tt(o, i, spread(m), ALU.is_equal)
                v.drain()
                tt(o, o, ramp[0:TT, :].unsqueeze(1).to_broadcast([TT, NT, 4]), ALU.mult)
                v.drain()
                red(mx, o, ALU.max)
                v.drain()
                tt(o, ramp[0:TT, :].unsqueeze(1).to_broadcast([TT, NT, 4]), spread(mx), ALU.is_equal)
                v.drain()

            v.wait_ge(sem("route_consts_ready"), 1)
            v.wait_ge(*step("logits_ready"))
            copy(lg, ps[0:TT, 1, 0:60].rearrange("p (c n) -> p c n", c=NT))
            v.drain()
            gl = lg[:, :, 0:4]
            first_max(oh, gl, m1)
            v.sem_inc(reach("onehot_ready"), 1)
            tt(gx, gl, spread(m1), ALU.subtract).then_inc(sem("rt_shifted"), 1)
            el = lg[:, :, 4:20]
            for c in range(NT):
                tt(prod[:, c], el[:, c, :].rearrange("p (g j) -> p g j", g=NG), oh[:, c, :].unsqueeze(2).to_broadcast([TT, NG, EG]), ALU.mult)
            v.drain()
            for c in range(NT):
                red(ein[:, c, :], prod[:, c].rearrange("p g j -> p j g"), ALU.add)
            v.wait_ge(sem("rt_exp"), 1)
            red(gw, gx, ALU.add)
            v.drain()
            nc.vector.reciprocal(gw, gw)
            first_max(oh1, ein, m1)
            stt(t4, oh1, -BIG, ein, ALU.mult, ALU.add)
            v.drain()
            first_max(oh2, t4, m2)
            tt(e2, m2, m1, ALU.subtract).then_inc(sem("rt_shifted"), 1)
            v.wait_ge(sem("rt_exp"), 2)
            tsc(w1, e2, 1.0, None, ALU.add)
            v.drain()
            nc.vector.reciprocal(w1, w1)
            v.drain()
            tt(w1, w1, gw, ALU.mult)
            v.drain()
            tt(e2, e2, w1, ALU.mult)
            tt(oh1, oh1, spread(w1), ALU.mult)
            v.drain()
            tt(oh2, oh2, spread(e2), ALU.mult)
            v.drain()
            tt(oh1, oh1, oh2, ALU.add)
            v.drain()
            for c in range(NT):
                tt(comb[:, c], oh1[:, c, :].unsqueeze(1).to_broadcast([TT, NG, EG]), oh[:, c, :].unsqueeze(2).to_broadcast([TT, NG, EG]), ALU.mult)
            v.wait_ge(*step("rank_ready"))
            size, start = rt[:, 560:564], rt[:, 565:569]
            copy(size, ps[0:TT, 6, 16:20])
            nc.vector.memset(start, 0.0)
            v.drain()
            for g in range(1, NG):
                tt(start[:, g:g + 1], start[:, g - 1:g], size[:, g - 1:g], ALU.add)
                v.drain()
            tt(t4, ps[0:TT, 6, 0:12].rearrange("p (c n) -> p c n", c=NT), start.unsqueeze(1).to_broadcast([TT, NT, 4]), ALU.add)
            v.drain()
            tt(t4, t4, oh, ALU.mult)
            v.drain()
            red(prow[:, 0:3], t4, ALU.add)
            v.drain()
            for c in range(NT):
                tt(perm[:, c, :], iota_pos[0:TT, :], prow[:, c:c + 1].to_broadcast([TT, T]), ALU.is_equal)
            v.drain()
            v.sem_inc(reach("perm_ready"), 1)
            nw, more, first, base, dbase = (rrow[:, 4 * n:4 * n + 4] for n in range(5))
            begun, tab_e, tab_at = rrow[:, 20:28], rrow[:, 32:40], rrow[:, 40:48]
            tsc(nw, size[0:1, :], float(W), None, ALU.is_gt)
            tsc(more, size[0:1, :], float(2 * W), None, ALU.is_gt)
            v.drain()
            tt(nw, nw, more, ALU.add)
            v.drain()
            tsc(nw, nw, 1.0, None, ALU.add)
            nc.vector.memset(first, 0.0)
            v.drain()
            for g in range(1, NG):
                tt(first[:, g:g + 1], first[:, g - 1:g], nw[:, g - 1:g], ALU.add)
                v.drain()
            stt(base, first, -float(W), start[0:1, :], ALU.mult, ALU.add)
            nc.vector.memset(tab_e, -float(EG))
            tsc(tab_at, iota_pos[0:1, 0:8], float(W), None, ALU.mult)
            v.drain()
            copy(dbase[:, 0:1], base[:, 0:1])
            tt(dbase[:, 1:4], base[:, 1:4], base[:, 0:3], ALU.subtract)
            for g in range(NG):
                v.drain()
                tsc(begun, iota_pos[0:1, 0:8], first[:, g:g + 1], None, ALU.is_ge)
                v.drain()
                stt(tab_e, begun, float(EG), tab_e, ALU.mult, ALU.add)
                stt(tab_at, begun, dbase[:, g:g + 1], tab_at, ALU.mult, ALU.add)
            v.drain()
            tsc(tab_at, tab_at, float(T), None, ALU.min)
            tt(more[:, 0:1], first[:, 3:4], nw[:, 3:4], ALU.add)
            v.drain()
            tsc(more[:, 1:2], more[:, 0:1], -1.0, None, ALU.add)
            v.drain()
            copy(wtab[:, 0:2], more[:, 0:2])
            copy(wtab[:, 2:10], tab_e)
            copy(wtab[:, 12:20], tab_at)
            v.drain()
            v.sem_inc(reach("table_ready"), 1)
            v.wait_ge(sem("htok_copied"), 12)
            nc.vector.memset(cs, 0.0)
            nc.vector.memset(hs[:, :, T:TW], 0.0)
            nc.vector.memset(ys, 0.0)
            v.drain()
            v.wait_ge(*step("cs_summed"))
            copy(cs[:, 0:T], ps[0:NE, 7, 0:T])
            for k in range(KT):
                v.wait_ge(sem("hs_summed"), k + 1)
                copy(hs[:, k, 0:T], ps[:, 2 + k % 4, 0:T]).then_inc(sem("hs_copied"), 1)
            v.wait_ge(*step("perm_turned"))
            for c, bank in enumerate((0, 1, 6)):
                copy(permT[:, c, :], ps[0:TT, bank, 0:T])
            v.drain()
            v.sem_inc(reach("perm_copied"), 1)
            v.sem_inc(reach("hs_ready"), 1)

            def position(w):
                at = v.value_load(wtab[0:1, ds(w + 12, 1)], min_val=0, max_val=T)
                return at

            def window(w):
                e = v.value_load(wtab[0:1, ds(w + 2, 1)], min_val=0, max_val=NE - EG)
                at = position(w)
                copy(hw, hs[:, :, ds(at, W)])
                copy(cw, cs[:, ds(at, W)])
                copy(selw, ident[0:NE, ds(e, EG)])
                v.drain()
                v.sem_inc(sem("window_ready"), 1)

            windows = v.value_load(wtab[0:1, 0:1], min_val=NG, max_val=MAXW)
            window(0)
            with v.Fori(0, windows) as it:
                v.wait_ge(sem("comb_ready"), it + 1)
                copy(comb_b, ps[:, 7, :].rearrange("p (j t) -> p j t", j=EG)).then_inc(sem("comb_copied"), 1)
                v.wait_ge(sem("comb_copied"), it + 1)
                v.sem_inc(sem("comb_read"), 1)
                for j in range(EG):
                    v.wait_ge(sem("sg_ready"), it * EG + (j + 1))
                    hj = hid[:, j % 2, :]
                    if j >= 2:
                        v.wait_ge(sem("down_done"), it * (2 * EG) + (2 * (j - 1)))
                    tt(hj, sg, ps[:, 4 + j % 2, :], ALU.mult)
                    v.drain()
                    v.sem_inc(sem("gate_read"), 1)
                    v.sem_inc(sem("sg_free"), 1)
                    tt(hj.rearrange("p (f t) -> p f t", f=4), hj.rearrange("p (f t) -> p f t", f=4),
                       comb_b[:, j, :].unsqueeze(1).to_broadcast([P, 4, W]), ALU.mult)
                    v.drain()
                    v.wait_ge(sem("up_ready"), it * EG + (j + 1))
                    tt(hj, hj, ps[:, 6, :], ALU.mult)
                    v.drain()
                    v.sem_inc(sem("up_read"), 1)
                    v.sem_inc(sem("hid_ready"), 1)
                window(it + 1)
                v.wait_ge(sem("down_done"), it * (2 * EG) + 2 * EG)
                yw = ys[:, :, ds(position(it), W)]
                tt(yw, yw, ps[:, 0:4, :].rearrange("p a (n t) -> p (a n) t", t=W), ALU.add)
                v.drain()
                v.sem_inc(sem("y_bank_free"), 1)
            v.sem_inc(reach("ys_ready"), 1)

            for k in range(KT):
                v.wait_ge(sem("y_summed"), k + 1)
                gated_add(k, k % 4, 5 * KT)
                v.sem_inc(sem("x3_ready"), 1)
            v.wait_ge(*step("ss3_ready"))
            tsc(ms[:, :], ps[:, 4, 0:T], 1.0 / D, EPS, ALU.mult, ALU.add).then_inc(reach("ms3_ready"), 1)
            v.wait_ge(*step("root3_ready"))
            nc.vector.reciprocal(rstd[:, :], ms[:, :])
            v.drain()
            for k in range(KT):
                stt(xT[:, k, :], xT[:, k, :], vcol[:, V_GF + k:V_GF + k + 1], rstd[:, :], ALU.mult, ALU.mult).then_inc(sem("xf_ready"), 1)
            for k in range(KT):
                v.wait_ge(sem("out_turned"), k + 1)
                copy(out_tok[:, 0:2, k * P:(k + 1) * P], ps[:, k % 4, 0:TP].rearrange("p (c n) -> p c n", c=2))
                copy(out_tok[0:TS, 2, k * P:(k + 1) * P], ps[0:TS, k % 4, TP:TP + P]).then_inc(sem("out_copied"), 1)
            v.wait_ge(sem("out_copied"), KT)
            v.sem_inc(reach("y_ready"), 1)


_INS = ["x_prompt", "x_sample", "cache_k", "cache_v", "cache_logf", "state_gla", "page_table", "c_prompt", "c_sample",
        "w_ada", "b_ada", "g_norm1", "g_norm2", "g_final", "w_in", "w_a2", "b_a", "b_f", "g_gla_norm", "w_up_a",
        "w_up_b", "w_out", "w_grp", "b_grp", "w_exp", "b_exp", "w_gate_e", "w_up_e", "w_down_e"]
_OUTS = [("y_prompt", (1, TP, D)), ("y_sample", (DB, DT, D)), ("k_prompt", (1, 1, TP, H_B, P)), ("v_prompt", (1, 1, TP, H_B, P)),
         ("logf_prompt", (1, 1, TP, H_B)), ("gla_prompt", (1, 1, H_A, P, DV)), ("k_sample", (1, DB, DT, H_B, P)),
         ("v_sample", (1, DB, DT, H_B, P)), ("logf_sample", (1, DB, DT, H_B)), ("gla_sample", (1, DB, H_A, P, DV))]


def kernel(**inputs):
    import numpy as _np
    import concourse.bacc as _bacc
    from concourse import mybir as _mybir
    from concourse.bass_utils import run_bass_kernel_spmd as _run

    nc = _bacc.Bacc("TRN2", target_bir_lowering=False, num_devices=1)
    arrays, io, out = {}, {}, {}
    for name in _INS:
        a = _np.ascontiguousarray(inputs[name])
        arrays[f"in_{name}_dram"] = a
        io[name] = nc.dram_tensor(f"in_{name}_dram", a.shape, _mybir.dt.from_np(a.dtype), kind="ExternalInput").ap()
    for name, shape in _OUTS:
        out[name] = nc.dram_tensor(f"out_{name}_dram", shape, _mybir.dt.float32, kind="ExternalOutput").ap()
    build(nc, io, out)
    r = _run(nc, [arrays], core_ids=[0])
    return tuple(r.results[0][f"out_{name}_dram"] for name, _ in _OUTS)
```

```python
from contextlib import ExitStack

import concourse.bass as bass
from concourse import mybir

ALU = mybir.AluOpType
ACT = mybir.ActivationFunctionType
AX = mybir.AxisListType
F32 = mybir.dt.float32
I32 = mybir.dt.int32

P = 128
D = 2048
KT = D // P
TP = 256
DB, DT = 8, 4
TS = DB * DT
T = TP + TS
NC = 1 + DB
H_A, DV = 4, 256
VB = DV // P
H_B = 8
PAST, PAGE = 1024, 128
NPG = PAST // PAGE
NG, EG = 4, 4
NE = NG * EG
FE = D // 4
TT = 96
NT = T // TT
W = 128
MAXW = NG + T // W
TW = T + W
EPS = 1e-6
SCALE = float(P) ** -0.5
BIG = 1e30
N_SMALL = 10
SLOTS = 6
SLOT = 4096
COL_QB = 2 * 512 + 2 * 1024 + 16
COL_LRA = COL_QB - 16
COL_FB = COL_QB + 3 * 1024
COL_GA = COL_FB + 8
COL_GB = COL_GA + D
LEVELS = (64, 32, 16, 8, 4, 2, 1)

STEPS = {
    "pe_step": (
        "c_turned ss1_ready vec_turned lra_fb_ready za_ready va_turned kt_turned state1_ready "
        "oa_ready update2_ready os_own_ready os_state_ready os_turned ss_a_ready lf_turned "
        "s_new_ready o_all_turned ss2_ready logits_ready rank_ready cs_summed perm_turned "
        "ss3_ready").split(),
    "act_step": (
        "c_sig_ready root1_ready za_exp zf_exp q_scaled decay_exp oa_squared root_a_ready "
        "ra_sig root2_ready root3_ready").split(),
    "dve_step": (
        "c_silu cT_ready ms1_ready lra_copied za_read logf_ready va_copied decay_rel "
        "decayed_ready kt_copied state1_copied oa_copied gla_prompt_ready update2_used os_summed "
        "gla_sample_ready os_turned_copied gla_scratch_free ms_a_ready rs_a_ready rs_a_inverted "
        "kv_tok_ready f_ready s_new_copied ob_ready work_free ms2_ready onehot_ready perm_ready "
        "table_ready perm_copied hs_ready ys_ready ms3_ready").split(),
}


def ds(i, n):
    return bass.ds(i, n)


def build(nc, io, out):
    with ExitStack() as ctx:
        made = {}

        def sem(name):
            if name not in made:
                made[name] = ctx.enter_context(nc.semaphore(name))
            return made[name]

        reached = {name: 0 for name in STEPS}

        def step(name):
            for engine, names in STEPS.items():
                if name in names:
                    return sem(engine), names.index(name) + 1

        def reach(name):
            s, n = step(name)
            engine = [e for e, names in STEPS.items() if name in names][0]
            assert n == reached[engine] + 1, name
            reached[engine] = n
            return s

        def sb(name, shape, dt=F32):
            return ctx.enter_context(nc.sbuf_tensor(name, shape, dt))

        ring = sb("ring", [P, SLOTS * SLOT])
        xT = sb("xT", [P, KT, T])
        hT = sb("hT", [P, KT, T])
        z = sb("z", [P, 48 * T])
        work2 = sb("work2", [P, 2976])
        ident = sb("ident", [P, P])
        ones = sb("ones", [P, P])
        fox_mask = sb("fox_mask", [P, P])
        new_mask = sb("new_mask", [P, TS])
        own_seq = sb("own_seq", [P, DB])
        ramp = sb("ramp", [P, 4])
        vcol = sb("vcol", [P, 152])
        modT = sb("modT", [P, 6 * KT, NC])
        mod_a = sb("mod_a", [P, KT, NC])
        rstd = sb("rstd", [P, T])
        ms = sb("ms", [P, T])
        brow = sb("brow", [1, 20])
        bfc = sb("bfc", [H_B, 1])
        ptab = sb("ptab", [1, DB * NPG], I32)
        fT = sb("fT", [H_B, T])
        shifted = sb("shifted", [P, TS])
        wtab = sb("wtab", [1, 24], I32)

        ps = ctx.enter_context(nc.psum_tensor("ps", [P, 8, 512], F32))

        def slot(s):
            return ring[:, (s % SLOTS) * SLOT:(s % SLOTS + 1) * SLOT]

        def ztile(i, n=1):
            return z[:, i * T:(i + n) * T].rearrange("p (n t) -> p n t", t=T)

        qa, ka, va, ra = ztile(0, 4), ztile(4, 4), ztile(8, 8), ztile(16, 8)
        qb, kb, vb = ztile(24, 8), ztile(32, 8), ztile(40, 8)
        oaT, obT, mgT = ztile(0, 8), qb, ztile(8, 16)
        vaTok = z[:, 8 * T:8 * T + 2 * 1024].rearrange("p (c n) -> p c n", c=2)
        vbTok = z[:, 40 * T:40 * T + 2 * 1024].rearrange("p (c n) -> p c n", c=2)
        x_in = z[:, 0:3 * D].rearrange("p (c n) -> p c n", c=3)
        sq = z[:, 3 * D:3 * D + KT * T].rearrange("p (k t) -> p k t", t=T)
        c_in = z[:, 11000:11000 + D]
        bada_rows = z[0:96, 13312:13312 + P]
        vec_rows = z[0:54, 13440:13440 + P]
        late = z[:, 48 * T - 2 * D:48 * T].rearrange("p (n d) -> p n d", n=2)
        c_sig = hT[:, 0:8, :].rearrange("p k t -> p (k t)")[:, 0:D]
        cT = work2[:, 0:KT * 32].rearrange("p (k c) -> p k c", c=32)
        mod_row = work2[:, 512:512 + 3 * 512].rearrange("p (j n) -> p j n", j=3)
        w_small = work2[:, 2048:2048 + KT * 40].rearrange("p (k n) -> p k n", n=40)
        lraT = work2[0:16, 2688:2688 + T]
        wk = ring[:, 4 * SLOT:6 * SLOT]
        F4 = H_A * T
        la = wk[:, 0:F4].rearrange("p (h t) -> p h t", t=T)
        buf = [wk[:, (i + 1) * F4:(i + 2) * F4] for i in range(5)]
        buf3 = [b.rearrange("p (h t) -> p h t", t=T) for b in buf]
        cum = buf3[4]

        def level_pair(n):
            return buf3[2 * (n % 2)], buf3[2 * (n % 2) + 1]

        atP = wk[:, 6 * F4:6 * F4 + 1024].rearrange("p (c h t) -> p c h t", c=2, h=H_A)
        atS = wk[0:TS, 6 * F4 + 1024:6 * F4 + 1152].rearrange("p (h t) -> p h t", h=H_A)
        w4 = ring[:, 2 * SLOT:4 * SLOT]
        ktP = w4[:, 0:1024].rearrange("p (c n) -> p c n", c=2)
        ktS = w4[0:TS, 1024:1536]
        kmS = w4[0:TS, 1536:2048]
        kms = (kmS, w4[0:TS, 5400:5912])
        vaS = w4[0:TS, 2048:3072]
        stP = w4[:, 3072:4096].rearrange("p (h v) -> p h v", h=H_A)
        osS = w4[:, 4096:4096 + DV]
        decay = w4[:, 4400:4400 + H_A * 10].rearrange("p (h n) -> p h n", h=H_A)
        level_mask = w4[:, 4480:4480 + len(LEVELS) * P].rearrange("p (n t) -> p n t", t=P)
        wa2 = w4[0:16, 5400:5912]
        fa, fb_, fc = (w4[0:H_B, 6000 + n * T:6000 + (n + 1) * T] for n in range(3))
        state = ring[:, 0:2 * SLOT].rearrange("p (b h v) -> p b h v", b=DB, h=H_A)
        sq8 = wk[:, F4:3 * F4].rearrange("p (n t) -> p n t", t=T)
        rs4 = buf3[2]
        sig8 = wk[:, 4 * F4:6 * F4].rearrange("p (n t) -> p n t", t=T)
        w3 = z[:, 8 * T:24 * T]
        kbTok = w3[:, 0:2048].rearrange("p (c n) -> p c n", c=2)
        prob = w3[:, 2048:2048 + 768].rearrange("p (c n) -> p c n", c=2)
        probT = w3[:, 2816:2816 + 768].rearrange("p (c n) -> p c n", c=2)
        lfTok = w3[:, 3600:3600 + 24].rearrange("p (c n) -> p c n", c=3)
        st_p = w3[:, 3640:3640 + 16]
        kbS = work2[0:TS, 0:1024]
        vbS = work2[0:TS, 1024:2048]
        ktR = wk[:, 0:8 * 512].rearrange("p (n t) -> p n t", n=8)
        pS = wk[:, 4096:4096 + 2 * 1056].rearrange("p (g n) -> p g n", g=2)
        pTS = w3[:, 1280:3328].rearrange("p (g n t) -> p g n t", g=2, n=8)
        pTN = w3[0:TS, 3328:3584].rearrange("p (g t) -> p g t", g=2)
        s_new = w3[:, 4200:4264].rearrange("p (g t) -> p g t", g=2)
        o_all = w3[:, 4300:4556].rearrange("p (g t) -> p g t", g=2)
        fn_r = w3[:, 4560:4562]
        nfT = w3[0:H_B, 3700:3700 + T]
        after = w3[:, 4000:4000 + P]
        lf_in = w3[:, 0:64].rearrange("p (n h) -> p n h", h=H_B)
        lf_a = w3[:, 64:128].rearrange("p (n h) -> p n h", h=H_B)
        lf_b = w3[:, 128:192].rearrange("p (n h) -> p n h", h=H_B)
        rT = w3[0:H_B, 256:256 + PAST]
        st_s = w3[:, 200:232]
        sig_ab = work2[:, 0:8 * T].rearrange("p (n t) -> p n t", t=T)
        hTok = ring[0:TT, 0:NT * D].rearrange("p (c n) -> p c n", c=NT)
        yTok = hTok
        perm = work2[0:TT, 0:NT * T].rearrange("p (c n) -> p c n", c=NT)
        permT = work2[0:TT, NT * T:2 * NT * T].rearrange("p (c n) -> p c n", c=NT)
        rt = work2[0:TT, 1728:2300]
        cw = work2[0:NE, 2300:2300 + W]
        selw = work2[0:NE, 2428:2432]
        rrow = work2[0:1, 2432:2480]
        prow = work2[0:TT, 2300 + 672:2300 + 676]
        wrt = work2[:, 2480:2480 + KT * 20].rearrange("p (k n) -> p k n", n=20)
        iota_pos = z[:, 13312:13312 + T]
        before = z[0:TT, 13600:13600 + TT]
        hs = z[:, 0:KT * TW].rearrange("p (k t) -> p k t", t=TW)
        ys = z[:, KT * TW:2 * KT * TW].rearrange("p (k t) -> p k t", t=TW)
        hflat = hT[:, :, :].rearrange("p k t -> p (k t)")
        hw = hflat[:, 0:KT * W].rearrange("p (k t) -> p k t", t=W)
        comb_b = hflat[:, 2048:2560].rearrange("p (j t) -> p j t", j=EG)
        sg = hflat[:, 2560:3072]
        hid = hflat[:, 3072:4096].rearrange("p (b n) -> p b n", b=2)
        cs = hflat[0:NE, 4096:4096 + TW]
        out_tok = ring[:, 2 * SLOT:2 * SLOT + 3 * D].rearrange("p (c n) -> p c n", c=3)
        sq2 = z[:, 24 * T:(24 + KT) * T].rearrange("p (k t) -> p k t", t=T)

        V_G1, V_G2, V_GF, V_BA, V_GG = 96, 112, 128, 144, 148

        ADA, WIN, UP, WOUT = 2, 18, 42, 66
        MOE = WOUT + 8
        EXTRA = DB
        LATER = 8

        def place(n):
            later = LATER if n >= UP and n % SLOTS < 2 else 0
            return n // SLOTS - (1 if n % SLOTS < 2 else 0) + later

        def freed(n):
            return place(n) + 1 + (EXTRA if n >= UP and n % SLOTS < 4 else 0)

        def freed_for_pages(s):
            return place(UP + s) + 1

        def filled(n):
            return 16 * (place(n) + 1)

        def later_place(m):
            return place(UP + m % 2) - LATER + m // 2

        block = ctx.enter_context(nc.Block())

        @block.sync
        def _(sp):
            sp.dma_start(c_in[0:1, :], io["c_prompt"]).then_inc(sem("c_loaded"), 16)
            sp.dma_start(c_in[1:NC, :], io["c_sample"]).then_inc(sem("c_loaded"), 16)

            def load(dst, src):
                sp.dma_start(dst, src).then_inc(sem("small_loaded"), 16)

            load(bada_rows, io["b_ada"].rearrange("a (r n) -> (a r) n", n=P))
            for n, name in enumerate(("g_norm1", "g_norm2")):
                load(vec_rows[n * 16:(n + 1) * 16, :], io[name].rearrange("a (r n) -> (a r) n", n=P))
            load(vec_rows[32:48, :], io["g_final"].rearrange("(r n) -> r n", n=P))
            load(vec_rows[48:52, :], io["b_a"].rearrange("a (r n) -> (a r) n", n=P))
            load(vec_rows[52:54, :], io["g_gla_norm"].rearrange("a (r n) -> (a r) n", n=P))
            load(brow[:, 0:4], io["b_grp"])
            load(brow[:, 4:20], io["b_exp"])
            load(bfc[:, :], io["b_f"].rearrange("a (h o) -> (a h) o", o=1))
            load(ptab[:, :], io["page_table"].rearrange("(a b) n -> a (b n)", a=1))
            sp.dma_start(x_in[:, 0:2, :], io["x_prompt"].rearrange("a (c p) n -> p (a c) n", p=P)).then_inc(sem("x_loaded"), 16)
            sp.dma_start(x_in[0:TS, 2, :], io["x_sample"].rearrange("b t n -> (b t) n")).then_inc(sem("x_loaded"), 16)

            for n in range(ADA, WIN):
                j, q = (n - ADA) // 8, (n - ADA) % 8
                sp.wait_ge(sem(f"ring_free{n % SLOTS}"), freed(n))
                src = io["w_ada"][0, q * 2 * P:(q + 1) * 2 * P, j * D:(j + 1) * D]
                sp.dma_start(slot(n).rearrange("p (k n) -> p k n", k=2),
                             src.rearrange("(k p) n -> p k n", p=P)).then_inc(sem(f"ring_full{n % SLOTS}"), 16)

            for part, col in ((0, 0), (1, COL_QB)):
                with sp.Fori(0, 2) as i:
                    for n in range(SLOTS):
                        j, q = n // 2, n % 2
                        for s in ((0, 1), (), (2,), (3,), (4,), (5,))[n]:
                            sp.wait_ge(sem(f"ring_free{s}"), i + freed(WIN + 12 * part + s))
                        src = io["w_in"][0, q * 8 * P:(q + 1) * 8 * P, ds(i * 1536 + (col + j * 512), 512)]
                        sp.dma_start(slot(n).rearrange("p (k n) -> p k n", k=8),
                                     src.rearrange("(k p) n -> p k n", p=P)).then_inc(sem(f"ring_full{n}"), 16)

            for m in range(16):
                sec, q = 4 + m // 8, m % 8
                sp.wait_ge(sem(f"ring_free{m % 2}"), later_place(m) + 1)
                src = io["w_ada"][0, q * 2 * P:(q + 1) * 2 * P, sec * D:(sec + 1) * D]
                sp.dma_start(slot(m % 2).rearrange("p (k n) -> p k n", k=2),
                             src.rearrange("(k p) n -> p k n", p=P)).then_inc(sem(f"ring_full{m % 2}"), 16)

            for s in range(2):
                sp.wait_ge(sem(f"ring_free{s}"), freed_for_pages(s))
            sp.dma_start(state, io["state_gla"][0].rearrange("b h k v -> k b h v")).then_inc(sem("state_loaded"), 16)

            def pages(b, s):
                name = ("cache_k", "cache_v")[s // 2]
                for n in range(4):
                    pg = sp.value_load(ptab[0:1, ds(b * NPG + (s % 2 * 4 + n), 1)], min_val=0, max_val=io["cache_k"].shape[1] - 1)
                    if n == 0:
                        if s == 0:
                            sp.wait_ge(sem("state_stored"), 16)
                        if s == 2:
                            sp.wait_ge(*step("gla_scratch_free"))
                        sp.wait_ge(sem(f"ring_free{s}"), b + freed_for_pages(s))
                    sp.dma_start(slot(s)[:, n * 1024:(n + 1) * 1024],
                                 io[name][0, ds(pg, 1)].rearrange("a p h d -> (a p) (h d)")).then_inc(sem(f"kv_full{s}"), 16)

            pages(0, 0)
            pages(0, 1)
            with sp.Fori(0, DB - 1) as b:
                pages(b + 1, 0)
                pages(b, 2)
                pages(b, 3)
                pages(b + 1, 1)
            pages(DB - 1, 2)
            pages(DB - 1, 3)

            with sp.Fori(0, 4) as g:
                for n in range(SLOTS):
                    if n == 4:
                        sp.wait_ge(*step("work_free"))
                    for s in ((0,), (2, 1), (), (3,), (4,), (5,))[n]:
                        sp.wait_ge(sem(f"ring_free{s}"), g + freed(UP + s))
                    part, q = n // 3, n % 3
                    if q < 2:
                        src = io["w_in"][0, q * 8 * P:(q + 1) * 8 * P, ds(g * 512 + (COL_GA, COL_GB)[part], 512)]
                    else:
                        src = io[("w_up_a", "w_up_b")[part]][0, :, ds(g * 512, 512)]
                    sp.dma_start(slot(n).rearrange("p (k n) -> p k n", k=8),
                                 src.rearrange("(k p) n -> p k n", p=P)).then_inc(sem(f"ring_full{n}"), 16)

            for n in range(8):
                j, q = n // 2, n % 2
                sp.wait_ge(sem(f"ring_free{n % SLOTS}"), freed(WOUT + n))
                src = io["w_out"][0, q * 8 * P:(q + 1) * 8 * P, j * 512:(j + 1) * 512]
                sp.dma_start(slot(n).rearrange("p (k n) -> p k n", k=8),
                             src.rearrange("(k p) n -> p k n", p=P)).then_inc(sem(f"ring_full{n % SLOTS}"), 16)

            def gate_up(e, turn):
                for n in range(4):
                    s = (MOE + n) % SLOTS
                    sp.wait_ge(sem(f"ring_free{s}"), turn + freed(MOE + n))
                    src = io[("w_gate_e", "w_up_e")[n // 2]][0, ds(e, 1), (n % 2) * 8 * P:(n % 2 + 1) * 8 * P, :]
                    sp.dma_start(slot(s).rearrange("p (k n) -> p k n", k=8),
                                 src.rearrange("a (k p) n -> p (a k) n", p=P)).then_inc(sem(f"ring_full{s}"), 16)

            def down(e, turn):
                for n in (4, 5):
                    s = (MOE + n) % SLOTS
                    sp.wait_ge(sem(f"ring_free{s}"), turn + freed(MOE + n))
                    src = io["w_down_e"][0, ds(e, 1), :, (n - 4) * 1024:(n - 3) * 1024]
                    sp.dma_start(slot(s).rearrange("p (k n) -> p k n", k=4),
                                 src.rearrange("a (k p) n -> p (a k) n", p=P)).then_inc(sem(f"ring_full{s}"), 16)

            gate_up(0, 0)
            sp.wait_ge(*step("table_ready"))
            sp.wait_ge(*step("hs_ready"))
            last_turn = sp.value_load(wtab[0:1, 1:2], min_val=3, max_val=MAXW - 1)
            with sp.Fori(0, last_turn) as w:
                e = sp.value_load(wtab[0:1, ds(w + 2, 1)], min_val=0, max_val=NE - EG)
                e_next = sp.value_load(wtab[0:1, ds(w + 3, 1)], min_val=0, max_val=NE - EG)
                for j in range(EG):
                    down(e + j, w * EG + j)
                    gate_up(e + (j + 1) if j + 1 < EG else e_next, w * EG + (j + 1))
            e = NE - EG
            for j in range(EG):
                down(e + j, last_turn * EG + j)
                if j + 1 < EG:
                    gate_up(e + (j + 1), last_turn * EG + (j + 1))

        @block.gpsimd
        def _(pool):
            pool.memset(ident[:, :], 0.0)
            pool.memset(ones[:, :], 1.0)
            pool.memset(fox_mask[:, :], 0.0)
            pool.memset(new_mask[:, :], 0.0)
            pool.memset(own_seq[:, :], 1.0)
            pool.memset(w_small[:, :, :], 0.0)
            pool.drain()
            pool.sem_inc(sem("w_small_clear"), 1)
            pool.affine_select(out=ident[:, :], in_=ident[:, :], compare_op=ALU.not_equal, fill=1.0,
                               base=0, pattern=[[-1, P]], channel_multiplier=1).then_inc(sem("ident_ready"), 1)
            pool.affine_select(out=fox_mask[:, :], in_=fox_mask[:, :], compare_op=ALU.is_ge, fill=-BIG, base=0,
                               pattern=[[-1, P]], channel_multiplier=1)
            for h in range(4):
                m = new_mask[32 * h:32 * h + 32, :]
                pool.affine_select(out=m, in_=m, compare_op=ALU.is_ge, fill=-BIG, base=0,
                                   pattern=[[-1, TS]], channel_multiplier=1)
                pool.drain()
                pool.affine_select(out=m.rearrange("p (b j) -> p b j", j=DT), in_=m.rearrange("p (b j) -> p b j", j=DT),
                                   compare_op=ALU.is_ge, fill=-BIG, base=DT - 1,
                                   pattern=[[DT, DB], [0, DT]], channel_multiplier=-1)
                o = own_seq[32 * h:32 * h + 32, :]
                pool.affine_select(out=o, in_=o, compare_op=ALU.is_ge, fill=0.0, base=0,
                                   pattern=[[-DT, DB]], channel_multiplier=1)
                pool.drain()
                pool.affine_select(out=o, in_=o, compare_op=ALU.is_ge, fill=0.0, base=DT - 1,
                                   pattern=[[DT, DB]], channel_multiplier=-1)
                pool.drain()
            pool.iota(ramp[:, :], pattern=[[-1, 4]], base=4, channel_multiplier=0, allow_small_or_imprecise_dtypes=True)
            pool.drain()
            pool.sem_inc(sem("consts_ready"), 1)

            pool.wait_ge(*step("vec_turned"))
            with pool.Fori(0, 2) as i:
                for k in range(KT):
                    pool.wait_ge(sem(f"late_free{k % 2}"), i * 8 + (k // 2 + 1))
                    pool.dma_start(late[:, k % 2, :], io["w_ada"][0, k * P:(k + 1) * P, ds(i * D + 2 * D, D)]).then_inc(sem(f"late_full{k % 2}"), 16)

            pool.wait_ge(*step("lra_fb_ready"))
            pool.memset(level_mask, 0.0)
            pool.drain()
            for n, b in enumerate(LEVELS):
                v = level_mask[:, n, :].rearrange("p (m two t) -> p m two t", two=2, t=b)[:, :, 1, :]
                pool.memset(v, 1.0)
                pool.drain()
                pool.affine_select(out=v, in_=v, compare_op=ALU.is_ge, fill=0.0, base=0,
                                   pattern=[[-2 * b, P // (2 * b)], [0, b]], channel_multiplier=1)
                pool.drain()
                pool.affine_select(out=v, in_=v, compare_op=ALU.is_ge, fill=0.0, base=b - 1,
                                   pattern=[[2 * b, P // (2 * b)], [0, b]], channel_multiplier=-1)
            pool.drain()
            pool.sem_inc(sem("masks_ready"), 1)

            pool.wait_ge(*step("gla_prompt_ready"))
            pool.dma_start(out["gla_prompt"][0, 0].rearrange("h k v -> k h v"), stP).then_inc(sem("gla_prompt_stored"), 16)
            pool.wait_ge(*step("gla_sample_ready"))
            pool.dma_start(out["gla_sample"][0].rearrange("b h k v -> k b h v"), state).then_inc(sem("state_stored"), 16)
            pool.wait_ge(*step("ra_sig"))
            pool.tensor_tensor(sig8, ra, sig8, ALU.mult).then_inc(sem("gate_a_ready"), 1)
            pool.wait_ge(*step("kv_tok_ready"))
            pool.dma_start(out["k_prompt"][0, 0].rearrange("(c p) h d -> p c (h d)", p=P), kbTok).then_inc(sem("kv_stored"), 16)
            pool.dma_start(out["v_prompt"][0, 0].rearrange("(c p) h d -> p c (h d)", p=P), vbTok).then_inc(sem("kv_stored"), 16)
            pool.dma_start(out["k_sample"][0].rearrange("b t h d -> (b t) (h d)"), kbS).then_inc(sem("kv_stored"), 16)
            pool.dma_start(out["v_sample"][0].rearrange("b t h d -> (b t) (h d)"), vbS).then_inc(sem("kv_stored"), 16)
            pool.dma_start(out["logf_prompt"][0, 0].rearrange("(c p) h -> p c h", p=P), lfTok[:, 0:2, :]).then_inc(sem("kv_stored"), 16)
            pool.dma_start(out["logf_sample"][0].rearrange("b t h -> (b t) h"), lfTok[0:TS, 2, :]).then_inc(sem("kv_stored"), 16)
            pool.affine_select(out=after, in_=ones[:, :], compare_op=ALU.is_gt, fill=0.0, base=0,
                               pattern=[[-1, P]], channel_multiplier=1).then_inc(sem("after_ready"), 1)
            pool.wait_ge(*step("rs_a_inverted"))
            for n in range(8):
                pool.tensor_tensor(oaT[:, n, :], oaT[:, n, :], rs4[:, n // 2, :], ALU.mult)
                pool.drain()
                pool.tensor_scalar(oaT[:, n, :], oaT[:, n, :], vcol[:, V_GG + n % 2:V_GG + n % 2 + 1], None, ALU.mult)
            pool.drain()
            pool.tensor_tensor(oaT, oaT, sig8, ALU.mult)
            pool.drain()
            pool.sem_inc(sem("oa_final"), 1)
            pool.wait_ge(sem("small_loaded"), 16 * N_SMALL)
            with pool.Fori(0, DB) as b:
                for n in range(NPG):
                    pg = pool.value_load(ptab[0:1, ds(b * NPG + n, 1)], min_val=0, max_val=io["cache_k"].shape[1] - 1)
                    if n == 0:
                        pool.wait_ge(sem("lf_used"), b + 1)
                    pool.dma_start(lf_in[:, n, :], io["cache_logf"][0, ds(pg, 1)].rearrange("a p h -> (a p) h")).then_inc(sem("lf_loaded"), 16)
            pool.wait_ge(*step("ob_ready"))
            pool.iota(iota_pos[:, :], pattern=[[1, T]], base=0, channel_multiplier=0, allow_small_or_imprecise_dtypes=True)
            pool.affine_select(out=before, in_=ones[0:TT, 0:TT], compare_op=ALU.is_gt, fill=0.0, base=0,
                               pattern=[[1, TT]], channel_multiplier=-1)
            pool.drain()
            pool.sem_inc(sem("route_consts_ready"), 1)
            for q in range(4):
                pool.wait_ge(sem("out_copied"), 4 * (q + 1))
                at = slice(q * 512, (q + 1) * 512)
                pool.dma_start(out["y_prompt"].rearrange("a (c p) n -> p (a c) n", p=P)[:, :, at], out_tok[:, 0:2, at]).then_inc(sem("y_stored"), 16)
                pool.dma_start(out["y_sample"].rearrange("b t n -> (b t) n")[:, at], out_tok[0:TS, 2, at]).then_inc(sem("y_stored"), 16)
            pool.wait_ge(sem("gla_prompt_stored"), 16)
            pool.wait_ge(sem("state_stored"), 16)
            pool.wait_ge(sem("kv_stored"), 6 * 16)
            pool.wait_ge(sem("y_stored"), 8 * 16)

        @block.tensor
        def _(pe):
            def mm(o, lhsT, rhs, start, stop, free=False):
                return nc.tensor.matmul(o, lhsT, rhs, start=start, stop=stop, skip_group_check=free)

            def release(name, count, *slots):
                pe.wait_ge(sem(name), count)
                for s in slots:
                    pe.sem_inc(sem(f"ring_free{s % SLOTS}"), 1)

            def tr(o, i):
                n = i.shape[0]
                return nc.tensor.transpose(o, i, ident[0:n, 0:n])

            pe.wait_ge(sem("ident_ready"), 1)
            pe.wait_ge(*step("c_silu"))
            for k in range(KT):
                last = tr(ps[:, 5, k * NC:(k + 1) * NC], c_in[0:NC, k * P:(k + 1) * P])
            last.then_inc(reach("c_turned"), 1)

            pe.wait_ge(sem("x_loaded"), 32)
            for k in range(KT):
                if k >= 4:
                    pe.wait_ge(sem("xT_copied"), k - 3)
                for c in range(2):
                    tr(ps[:, k % 4, c * P:(c + 1) * P], x_in[:, c, k * P:(k + 1) * P])
                tr(ps[:, k % 4, TP:T], x_in[0:TS, 2, k * P:(k + 1) * P]).then_inc(sem("xT_turned"), 1)
            pe.wait_ge(sem("xT_squared"), KT)
            pe.wait_ge(sem("consts_ready"), 1)
            for k in range(KT):
                last = mm(ps[:, 4, 0:T], ones[:, :], sq[:, k, :], k == 0, k == KT - 1)
            last.then_inc(reach("ss1_ready"), 1)
            pe.wait_ge(sem("small_loaded"), 16 * N_SMALL)
            tr(ps[:, 6, 0:96], bada_rows)
            tr(ps[:, 6, 96:150], vec_rows).then_inc(reach("vec_turned"), 1)
            pe.wait_ge(*step("cT_ready"))
            pe.wait_ge(sem("xT_copied"), KT)
            def turn(section, row, bank):
                pe.wait_ge(sem("mod_row_ready"), section + 1)
                for jt in range(4):
                    last = tr(ps[:, bank, jt * P:(jt + 1) * P], mod_row[:, row, jt * P:(jt + 1) * P])
                last.then_inc(sem("mod_turned"), 1)

            for n in range(ADA, WIN):
                j, q = (n - ADA) // 8, (n - ADA) % 8
                pe.wait_ge(sem(f"ring_full{n % SLOTS}"), filled(n))
                w = slot(n).rearrange("p (k n) -> p k n", k=2)
                for k in range(2):
                    for c in range(4):
                        last = mm(ps[32 * c:32 * c + 32, j, :], cT[:, 2 * q + k, :], w[:, k, c * 512:(c + 1) * 512],
                                  q == 0 and k == 0, q == 7 and k == 1)
                if q < 7:
                    last.then_inc(sem(f"ring_free{n % SLOTS}"), 1)
                    continue
                last.then_inc(sem("mod_summed"), 1)
                release("mod_summed", j + 1, n)
                if j:
                    turn(j - 1, j - 1, 2 + j)
            turn(1, 1, 4)

            pe.wait_ge(sem("h1_ready"), 1)
            pe.wait_ge(sem("mod_ready"), 2)
            def win_round(i, late_too):
                def late_section(first, count):
                    for k in range(first, first + count):
                        if k == 0:
                            pe.wait_ge(sem("mod_row_ready"), i + 2)
                        pe.wait_ge(sem(f"late_full{k % 2}"), i * 128 + 16 * (k // 2 + 1))
                        for c in range(4):
                            last = mm(ps[32 * c:32 * c + 32, 7, :], cT[:, k, :], late[:, k % 2, c * 512:(c + 1) * 512], k == 0, k == KT - 1)
                        if k < KT - 1:
                            last.then_inc(sem(f"late_free{k % 2}"), 1)
                            continue
                        last.then_inc(sem("mod_summed"), 1)
                        pe.wait_ge(sem("mod_summed"), i + 3)
                        pe.sem_inc(sem(f"late_free{k % 2}"), 1)

                for j in range(3):
                    for s in (2 * j, 2 * j + 1):
                        pe.wait_ge(sem(f"ring_full{s}"), i * 16 + filled(WIN + s))
                    wl, wh = (slot(s).rearrange("p (k n) -> p k n", k=8) for s in (2 * j, 2 * j + 1))
                    for t in range(4):
                        n = 4 * j + t
                        pe.wait_ge(sem("win_bank_free%d" % (n % 2)), i * 6 + (n // 2 + 1))
                        for k in range(KT):
                            if n == 0:
                                pe.wait_ge(sem("h1_shifted"), k + 1)
                            w = (wl if k < 8 else wh)[:, k % 8, t * P:(t + 1) * P]
                            last = mm(ps[:, n % 6, 0:T], w, hT[:, k, :], k == 0, k == KT - 1)
                        last.then_inc(sem("win_tile"), 1)
                        if late_too and n < 5:
                            late_section(2 * n, 2)
                        elif late_too and n < 11:
                            late_section(5 + n, 1)
                    release("win_tile", i * 12 + 4 * (j + 1), 2 * j, 2 * j + 1)
                if late_too:
                    pe.wait_ge(sem("mod_ready"), i + 2)
                    turn(i + 2, 2, 6)

            with pe.Fori(0, 2) as i:
                win_round(i, True)
            with pe.Fori(2, 4) as i:
                win_round(i, False)
            pe.wait_ge(sem("mod_ready"), 4)
            pe.wait_ge(sem("w_small_loaded"), 32)
            for k in range(KT):
                last = mm(ps[0:40, 6, 0:T], w_small[:, k, :], hT[:, k, :], k == 0, k == KT - 1)
            last.then_inc(reach("lra_fb_ready"), 1)
            pe.wait_ge(*step("lra_copied"))
            pe.wait_ge(sem("wa2_loaded"), 16)
            pe.wait_ge(sem("win_bank_free0"), 24 + 3)
            pe.wait_ge(sem("win_bank_free1"), 24 + 3)
            for h in range(H_A):
                last = mm(ps[:, h, 0:T], wa2[:, h * P:(h + 1) * P], lraT, True, True)
            last.then_inc(reach("za_ready"), 1)

            def later_half_block(m):
                sec, q = 4 + m // 8, m % 8
                pe.wait_ge(sem(f"ring_full{m % 2}"), 16 * (later_place(m) + 1))
                w = slot(m % 2).rearrange("p (k n) -> p k n", k=2)
                for k in range(2):
                    for c in range(4):
                        last = mm(ps[32 * c:32 * c + 32, 7, :], cT[:, 2 * q + k, :], w[:, k, c * 512:(c + 1) * 512],
                                  q == 0 and k == 0, q == 7 and k == 1)
                if q < 7:
                    last.then_inc(sem(f"ring_free{m % 2}"), 1)
                else:
                    last.then_inc(sem("mod_summed"), 1)
                    release("mod_summed", sec + 1, m % 2)

            for m in range(8):
                later_half_block(m)
            turn(4, 2, 6)
            pe.wait_ge(sem("mod_ready"), 5)

            for c in range(2):
                for n in range(8):
                    last = tr(ps[:, 4 + 2 * c + n // 4, (n % 4) * P:(n % 4 + 1) * P], va[:, n, c * P:(c + 1) * P])
            pe.wait_ge(*step("za_read"))
            for n in range(8):
                last = tr(ps[0:TS, n // 4, (n % 4) * P:(n % 4 + 1) * P], va[:, n, TP:T])
            last.then_inc(reach("va_turned"), 1)
            pe.wait_ge(*step("va_copied"))
            for n in range(len(LEVELS) + 1):
                pe.wait_ge(sem("level_ready"), n + 1)
                if n >= 2:
                    pe.wait_ge(sem("level_read"), n - 1)
                b0 = 3 * (n % 2)
                ql, kl = level_pair(n) if n < len(LEVELS) else (qa, ka)
                for c in range(2):
                    for h in range(H_A):
                        last = mm(ps[:, b0 + c, h * P:(h + 1) * P], kl[:, h, c * P:(c + 1) * P], ql[:, h, c * P:(c + 1) * P], True, True)
                if n >= len(LEVELS) - 2:
                    for h in range(H_A):
                        last = mm(ps[0:TS, b0 + 2, h * TS:(h + 1) * TS], kl[:, h, TP:T], ql[:, h, TP:T], True, True)
                last.then_inc(sem("level_scored"), 1)
                later_half_block(8 + n)
            pe.wait_ge(sem("level_read"), len(LEVELS))
            turn(5, 2, 2)
            pe.wait_ge(*step("decayed_ready"))
            for c in range(2):
                for h in range(H_A):
                    last = tr(ps[:, 6 + c, h * P:(h + 1) * P], buf3[3][:, h, c * P:(c + 1) * P])
            pe.wait_ge(sem("level_read"), len(LEVELS))
            for h in range(H_A):
                last = tr(ps[0:TS, 0, h * P:(h + 1) * P], buf3[3][:, h, TP:T])
            last.then_inc(reach("kt_turned"), 1)
            pe.wait_ge(*step("kt_copied"))
            pe.wait_ge(sem("level_read"), len(LEVELS) + 1)
            for h in range(H_A):
                last = mm(ps[:, 4 + h // 2, (h % 2) * DV:(h % 2 + 1) * DV], ktP[:, 0, h * P:(h + 1) * P],
                          vaTok[:, 0, h * DV:(h + 1) * DV], True, True)
            last.then_inc(reach("state1_ready"), 1)
            pe.wait_ge(*step("state1_copied"))
            for n in range(8):
                h, v = n // 2, n % 2
                vs = slice(h * DV + v * P, h * DV + (v + 1) * P)
                o = ps[:, n // 2, (n % 2) * TP:(n % 2 + 1) * TP]
                mm(o[:, 0:P], vaTok[:, 0, vs], atP[:, 0, h, :], True, True)
                mm(o[:, P:TP], vaTok[:, 1, vs], atP[:, 1, h, :], True, False)
                last = mm(o[:, P:TP], stP[:, h, v * P:(v + 1) * P], buf3[2][:, h, P:TP], False, True)
            last.then_inc(reach("oa_ready"), 1)
            for h in range(H_A):
                last = mm(ps[:, 6 + h // 2, (h % 2) * DV:(h % 2 + 1) * DV], ktP[:, 1, h * P:(h + 1) * P],
                          vaTok[:, 1, h * DV:(h + 1) * DV], True, True)
            last.then_inc(reach("update2_ready"), 1)
            pe.wait_ge(*step("oa_copied"))
            for h in range(H_A):
                last = mm(ps[32 * h:32 * h + 32, 4, 0:DV], atS[:, h, :], vaS[:, h * DV:(h + 1) * DV], True, True)
            last.then_inc(reach("os_own_ready"), 1)
            pe.wait_ge(sem("state_loaded"), 16)
            for b in range(DB):
                for h in range(H_A):
                    last = mm(ps[32 * h:32 * h + 32, b // 2, (b % 2) * DV:(b % 2 + 1) * DV], buf3[2][:, h, TP:T], state[:, b, h, :], True, True)
            last.then_inc(reach("os_state_ready"), 1)
            pe.wait_ge(*step("update2_used"))
            for b in range(DB):
                pe.wait_ge(sem("km_ready"), b + 1)
                if b >= 2:
                    pe.wait_ge(sem("state_updated"), b - 1)
                bank = 6 if b % 2 == 0 else 2
                for h in range(H_A):
                    last = mm(ps[:, bank + h // 2, (h % 2) * DV:(h % 2 + 1) * DV], kms[b % 2][:, h * P:(h + 1) * P],
                              vaS[:, h * DV:(h + 1) * DV], True, True)
                last.then_inc(sem("update_ready"), 1)
            pe.wait_ge(*step("os_summed"))
            for v in range(VB):
                last = tr(ps[:, 4, v * P:(v + 1) * P], osS[:, v * P:(v + 1) * P])
            last.then_inc(reach("os_turned"), 1)
            pe.wait_ge(*step("oa_squared"))
            pe.wait_ge(sem("state_updated"), DB)
            for h in range(H_A):
                for v in range(VB):
                    last = mm(ps[:, h, 0:T], ones[:, :], sq8[:, 2 * h + v, :], v == 0, v == VB - 1)
            last.then_inc(reach("ss_a_ready"), 1)

            pe.wait_ge(*step("os_turned_copied"))
            pe.wait_ge(sem("state_updated"), DB)
            for m, src in ((0, kb), (1, vb)):
                if m:
                    pe.wait_ge(sem("tok_copied"), 1)
                for c in range(2):
                    for h in range(H_B):
                        last = tr(ps[:, 4 + 2 * c + h // 4, (h % 4) * P:(h % 4 + 1) * P], src[:, h, c * P:(c + 1) * P])
                last.then_inc(sem("tok_turned"), 1)
            pe.wait_ge(sem("tok_copied"), 2)
            for m, src in ((0, kb), (1, vb)):
                for h in range(H_B):
                    last = tr(ps[0:TS, 4 + 2 * m + h // 4, (h % 4) * P:(h % 4 + 1) * P], src[:, h, TP:T])
            last.then_inc(sem("tok_turned"), 1)
            pe.wait_ge(*step("rs_a_ready"))
            pe.wait_ge(*step("logf_ready"))
            for c in range(3):
                n = P if c < 2 else TS
                last = tr(ps[0:n, 0, c * H_B:(c + 1) * H_B], fT[:, c * P:c * P + n])
            last.then_inc(reach("lf_turned"), 1)
            pe.wait_ge(*step("f_ready"))
            pe.wait_ge(sem("tok_copied"), 4)
            for i in range(H_B + 1):
                if i < H_B:
                    h = i
                    if h >= 2:
                        pe.wait_ge(sem("fox_exp"), h - 1)
                    sbk = ps[:, 1 + h % 2, :]
                    hot = ident[0:H_B, h:h + 1]
                    for q in range(2):
                        kk = P * (q + 1)
                        o = sbk[:, q * P:q * P + kk]
                        mm(o, qb[:, h, q * P:(q + 1) * P], kb[:, h, 0:kk], True, False)
                        mm(o, hot.to_broadcast([H_B, P]), nfT[:, 0:kk], False, False)
                        last = mm(o, fT[:, q * P:(q + 1) * P], hot.to_broadcast([H_B, kk]), False, True)
                    last.then_inc(sem("fox_scored"), 1)
                if i >= 1:
                    h = i - 1
                    pe.wait_ge(sem("fox_prob"), h + 1)
                    if h >= 1:
                        pe.wait_ge(sem("fox_pt"), h)
                    for n in range(3):
                        last = tr(ps[:, 3, n * P:(n + 1) * P], prob[:, h % 2, n * P:(n + 1) * P])
                    last.then_inc(sem("fox_turned"), 1)
                    pe.wait_ge(sem("fox_pt"), h + 1)
                    if h >= 2:
                        pe.wait_ge(sem("fox_out"), h - 1)
                    o = ps[:, 4 + h % 2, 0:TP]
                    vh = slice(h * P, (h + 1) * P)
                    mm(o[:, 0:P], vbTok[:, 0, vh], probT[:, h % 2, 0:P], True, True)
                    mm(o[:, P:TP], vbTok[:, 0, vh], probT[:, h % 2, P:2 * P], True, False)
                    last = mm(o[:, P:TP], vbTok[:, 1, vh], probT[:, h % 2, 2 * P:3 * P], False, True)
                    last.then_inc(sem("fox_pv"), 1)

            pe.wait_ge(sem("fox_out"), H_B)
            for g in range(2):
                for c in range(4):
                    h = 4 * g + c
                    o = ps[32 * c:32 * c + 32, 0, g * TS:(g + 1) * TS]
                    mm(o, qb[:, h, TP:T], kb[:, h, TP:T], True, False)
                    mm(o, ident[0:H_B, h:h + 1].to_broadcast([H_B, TS]), nfT[:, TP:T], False, False)
                    mm(o, fT[:, TP:T], ident[0:H_B, h:h + 1].to_broadcast([H_B, TS]), False, True)
                    last = mm(ps[32 * c:32 * c + 32, 1, g:g + 1], fT[:, TP:T], ident[0:H_B, h:h + 1], True, True)
            last.then_inc(reach("s_new_ready"), 1)
            pe.wait_ge(*step("s_new_copied"))
            pe.wait_ge(sem("after_ready"), 1)
            def past_forgets(b):
                pe.wait_ge(sem("lf_summed"), b + 1)
                for n in range(NPG):
                    o = ps[0:H_B, 6 + n // 4, (n % 4) * PAGE:(n % 4 + 1) * PAGE]
                    mm(o, lf_in[:, n, :], after[:, :], True, False)
                    last = mm(o, lf_b[:, n, :], ones[:, :], False, True)
                last.then_inc(sem("r_ready"), 1)

            def turn_keys(b, r):
                g, half = r % 2, r // 2
                if g == 0:
                    pe.wait_ge(sem(f"kv_full{half}"), b * 64 + 64)
                for c in range(4):
                    n = 4 * r + c
                    pe.wait_ge(sem("kt_copied%d" % (c % 2)), b * 8 + (n // 2 + 1))
                    w = slot(half)
                    for pgi in range(4):
                        last = tr(ps[:, 4 + c % 2, pgi * PAGE:(pgi + 1) * PAGE],
                                  w[:, pgi * 1024 + (4 * g + c) * P:pgi * 1024 + (4 * g + c + 1) * P])
                    last.then_inc(sem("kt_turned_s"), 1)
                if g == 1:
                    release("kt_turned_s", b * 16 + 4 * (r + 1), half)

            def score(b, r):
                g, half = r % 2, r // 2
                pe.wait_ge(sem("kt_copied0"), b * 8 + (2 * (r + 1) + 1))
                pe.wait_ge(sem("kt_copied1"), b * 8 + (2 * (r + 1) + 1))
                for c in range(4):
                    mm(ps[32 * c:32 * c + 32, 2 * g + half, :], qb[:, 4 * g + c, TP:T], ktR[:, 4 * (r % 2) + c, :], True, False)
                for c in range(4):
                    h = 4 * g + c
                    last = mm(ps[32 * c:32 * c + 32, 2 * g + half, :], ident[0:H_B, h:h + 1].to_broadcast([H_B, TS]),
                              rT[:, half * 512:(half + 1) * 512], False, True)
                last.then_inc(sem("s_scored"), 1)

            def sample_sequence(b, more):
                pe.wait_ge(sem("r_copied"), b + 1)
                score(b, 0)
                pe.wait_ge(sem("o_all_ready"), b + 1)
                turn_keys(b, 2)
                score(b, 1)
                turn_keys(b, 3)
                score(b, 2)
                score(b, 3)
                if more:
                    turn_keys(b + 1, 0)
                    turn_keys(b + 1, 1)
                for g in range(2):
                    pe.wait_ge(sem("s_prob"), b * 2 + (g + 1))
                    for q in range(2):
                        if g:
                            pe.wait_ge(sem("pt_copied"), b * 5 + (q + 1))
                        for n in range(4):
                            last = tr(ps[:, 6 + q, n * P:(n + 1) * P], pS[:, g, (4 * q + n) * P:(4 * q + n + 1) * P])
                        last.then_inc(sem("pt_turned"), 1)
                pe.wait_ge(sem("pt_copied"), b * 5 + 3)
                for g in range(2):
                    last = tr(ps[0:TS, 6, g * P:(g + 1) * P], pS[:, g, PAST:PAST + TS])
                last.then_inc(sem("pt_turned"), 1)
                pe.wait_ge(sem("pt_copied"), b * 5 + 5)
                if more:
                    past_forgets(b + 1)
                for s in (2, 3):
                    pe.wait_ge(sem(f"kv_full{s}"), b * 64 + 64)
                pe.wait_ge(sem("kt_copied1"), b * 8 + (13 if more else 9))
                for g in range(2):
                    for n in range(NPG + 1):
                        for c in range(4):
                            h = 4 * g + c
                            o = ps[32 * c:32 * c + 32, 5, g * P:(g + 1) * P]
                            if n < NPG:
                                v = slot(2 + n // 4)[:, (n % 4) * 1024 + h * P:(n % 4) * 1024 + (h + 1) * P]
                                last = mm(o, pTS[:, g, n, 32 * c:32 * c + 32], v, n == 0, False)
                            else:
                                last = mm(o, pTN[:, g, 32 * c:32 * c + 32], vbS[:, h * P:(h + 1) * P], False, True)
                last.then_inc(sem("o_b_ready"), 1)
                release("o_b_ready", b + 1, 2, 3)

            past_forgets(0)
            turn_keys(0, 0)
            turn_keys(0, 1)
            with pe.Fori(0, DB - 1) as b:
                sample_sequence(b, True)
            sample_sequence(DB - 1, False)
            pe.wait_ge(sem("o_all_ready"), DB + 1)
            for g in range(2):
                last = tr(ps[:, 0, g * P:(g + 1) * P], o_all[:, g, :])
            last.then_inc(reach("o_all_turned"), 1)

            pe.wait_ge(*step("ob_ready"))
            pe.wait_ge(sem("oa_final"), 1)
            with pe.Fori(0, 4) as g:
                for n in range(16):
                    kind, t = n // 4, n % 4
                    first, halves = ((0, 2), (2, 1), (3, 2), (5, 1))[kind]
                    if t == 0:
                        for s in range(first, first + halves):
                            pe.wait_ge(sem(f"ring_full{s}"), g * 16 + filled(UP + s))
                    pe.wait_ge(sem("up_bank_free"), g * 16 + (n + 1))
                    src = hT if kind % 2 == 0 else (oaT if kind == 1 else obT)
                    for k in range(8 * halves):
                        w = slot(first + k // 8).rearrange("p (k n) -> p k n", k=8)[:, k % 8, t * P:(t + 1) * P]
                        last = mm(ps[:, n % 8, 0:T], w, src[:, k, :], k == 0, k == 8 * halves - 1)
                    last.then_inc(sem("up_tile"), 1)
                    if t == 3:
                        release("up_tile", g * 16 + (n + 1), *range(first, first + halves))

            pe.wait_ge(sem("merged"), 17)
            for n in range(KT):
                j, t = n // 4, n % 4
                if t == 0:
                    for s in (2 * j, 2 * j + 1):
                        pe.wait_ge(sem(f"ring_full{s % SLOTS}"), filled(WOUT + s))
                pe.wait_ge(sem("up_bank_free"), 64 + n + (1 if n < 7 else 2))
                for k in range(KT):
                    w = slot(2 * j + k // 8).rearrange("p (k n) -> p k n", k=8)[:, k % 8, t * P:(t + 1) * P]
                    last = mm(ps[:, n % 7, 0:T], w, mgT[:, k, :], k == 0, k == KT - 1)
                last.then_inc(sem("wout_tile"), 1)
                if t == 3:
                    release("wout_tile", n + 1, 2 * j, 2 * j + 1)
                for k in {8: range(5), KT - 1: range(KT - 5, KT)}.get(n, (n - 4,) if n > 8 else ()):
                    pe.wait_ge(sem("x2_squared"), k + 1)
                    if k == 0:
                        pe.wait_ge(sem("up_bank_free"), 72)
                    last = mm(ps[:, 7, 0:T], ones[:, :], sq2[:, k, :], k == 0, k == KT - 1)
            last.then_inc(reach("ss2_ready"), 1)
            pe.wait_ge(sem("up_bank_free"), 64 + 16 + 8)

            pe.wait_ge(sem("h2_ready"), 1)
            pe.wait_ge(sem("router_loaded"), 32)
            for c in range(NT):
                o = ps[0:TT, 1, c * 20:(c + 1) * 20]
                for k in range(KT):
                    if c == 0:
                        pe.wait_ge(sem("h2_shifted"), k + 1)
                    mm(o, hT[:, k, c * TT:(c + 1) * TT], wrt[:, k, :], k == 0, False)
                last = mm(o, ones[0:1, 0:TT], brow[:, :], False, True)
            last.then_inc(reach("logits_ready"), 1)
            for c in range(NT):
                for q in range(4):
                    n = 4 * c + q
                    if n >= 4:
                        pe.wait_ge(sem("htok_copied"), n - 3)
                    for m in range(4):
                        k = 4 * q + m
                        last = tr(ps[0:TT, 2 + n % 4, m * P:(m + 1) * P], hT[:, k, c * TT:(c + 1) * TT])
                    last.then_inc(sem("htok_turned"), 1)
            pe.wait_ge(*step("onehot_ready"))
            for c in range(NT):
                o = ps[0:TT, 6, c * 4:(c + 1) * 4]
                for m in range(c):
                    mm(o, ones[0:TT, 0:TT], rt[:, m * 4:(m + 1) * 4], m == 0, False)
                mm(o, before[:, :], rt[:, c * 4:(c + 1) * 4], c == 0, True)
            for m in range(NT):
                last = mm(ps[0:TT, 6, 16:20], ones[0:TT, 0:TT], rt[:, m * 4:(m + 1) * 4], m == 0, m == NT - 1)
            last.then_inc(reach("rank_ready"), 1)
            pe.wait_ge(*step("perm_ready"))
            for m in range(NT):
                last = mm(ps[0:NE, 7, 0:T], rt[:, 64 + m * NE:64 + (m + 1) * NE], perm[:, m, :], m == 0, m == NT - 1)
            last.then_inc(reach("cs_summed"), 1)
            pe.wait_ge(sem("htok_copied"), 12)
            for k in range(KT):
                if k >= 4:
                    pe.wait_ge(sem("hs_copied"), k - 3)
                for m in range(NT):
                    last = mm(ps[:, 2 + k % 4, 0:T], hTok[:, m, k * P:(k + 1) * P], perm[:, m, :], m == 0, m == NT - 1)
                last.then_inc(sem("hs_summed"), 1)
            for c in range(NT):
                for m in range(NT):
                    last = tr(ps[0:TT, 0 if c < 1 else (1 if c < 2 else 6), m * TT:(m + 1) * TT], perm[:, m, c * TT:(c + 1) * TT])
            last.then_inc(reach("perm_turned"), 1)
            pe.wait_ge(*step("perm_copied"))
            pe.wait_ge(*step("table_ready"))
            pe.wait_ge(*step("hs_ready"))

            windows = pe.value_load(wtab[0:1, 0:1], min_val=NG, max_val=MAXW)
            with pe.Fori(0, windows) as it:
                def wait_slot(j, n):
                    pe.wait_ge(sem(f"ring_full{(MOE + n) % SLOTS}"), it * (16 * EG) + (filled(MOE + n) + 16 * j))

                def project(j, which):
                    if which == 0:
                        pe.wait_ge(sem("gate_read"), it * EG + (j + 1))
                    else:
                        pe.wait_ge(sem("up_read"), it * EG + (j + 1))
                    bank = (4 + j % 2) if which == 0 else 6
                    for n in (2 * which, 2 * which + 1):
                        wait_slot(j, n)
                        for f in range(4):
                            for k in range(8):
                                wt = slot(MOE + n).rearrange("p (k n) -> p k n", k=8)[:, k, f * P:(f + 1) * P]
                                last = mm(ps[:, bank, f * W:(f + 1) * W], wt, hw[:, (n % 2) * 8 + k, :],
                                          n % 2 == 0 and f == 0 and k == 0, n % 2 == 1 and k == 7, free=True)
                        if n % 2 == 0:
                            last.then_inc(sem(f"ring_free{(MOE + n) % SLOTS}"), 1)
                    last.then_inc(sem(("gate_ready", "up_ready")[which]), 1)
                    release(("gate_ready", "up_ready")[which], it * EG + (j + 1), MOE + 2 * which + 1)

                def down(j):
                    pe.wait_ge(sem("hid_ready"), it * EG + (j + 1))
                    for n in (4, 5):
                        wait_slot(j, n)
                        for m in range(8):
                            dt = (n - 4) * 8 + m
                            for f in range(4):
                                wt = slot(MOE + n).rearrange("p (k n) -> p k n", k=4)[:, f, m * P:(m + 1) * P]
                                last = mm(ps[:, dt // 4, (dt % 4) * W:(dt % 4 + 1) * W], wt, hid[:, j % 2, f * W:(f + 1) * W],
                                          j == 0 and f == 0 and dt % 4 == 0, j == EG - 1 and f == 3, free=True)
                        last.then_inc(sem("down_done"), 1)
                        release("down_done", it * (2 * EG) + (2 * j + n - 3), MOE + n)

                pe.wait_ge(sem("window_ready"), it + 1)
                pe.wait_ge(sem("comb_read"), it + 1)
                for j in range(EG):
                    last = mm(ps[:, 7, j * W:(j + 1) * W], selw[:, j:j + 1].to_broadcast([NE, P]), cw, True, True)
                last.then_inc(sem("comb_ready"), 1)
                project(0, 0)
                project(0, 1)
                for j in range(EG):
                    if j + 1 < EG:
                        project(j + 1, 0)
                    if j == 0:
                        pe.wait_ge(sem("y_bank_free"), it + 1)
                    down(j)
                    if j + 1 < EG:
                        project(j + 1, 1)

            pe.wait_ge(*step("ys_ready"))
            for c in range(NT):
                for q in range(4):
                    n = 4 * c + q
                    if n >= 4:
                        pe.wait_ge(sem("ytok_copied"), n - 3)
                    for m in range(4):
                        last = tr(ps[0:TT, 4 + n % 4, m * P:(m + 1) * P], ys[:, 4 * q + m, c * TT:(c + 1) * TT])
                    last.then_inc(sem("ytok_turned"), 1)
            pe.wait_ge(sem("ytok_copied"), 12)
            for k in range(KT):
                if k >= 4:
                    pe.wait_ge(sem("x3_ready"), k - 3)
                for m in range(NT):
                    last = mm(ps[:, k % 4, 0:T], yTok[:, m, k * P:(k + 1) * P], permT[:, m, :], m == 0, m == NT - 1)
                last.then_inc(sem("y_summed"), 1)
            pe.wait_ge(sem("x3_squared"), KT)
            for k in range(KT):
                last = mm(ps[:, 4, 0:T], ones[:, :], sq2[:, k, :], k == 0, k == KT - 1)
            last.then_inc(reach("ss3_ready"), 1)
            for k in range(KT):
                pe.wait_ge(sem("xf_ready"), k + 1)
                if k >= 4:
                    pe.wait_ge(sem("out_copied"), k - 3)
                for c in range(2):
                    tr(ps[:, k % 4, c * P:(c + 1) * P], xT[:, k, c * P:(c + 1) * P])
                tr(ps[0:TS, k % 4, TP:TP + P], xT[:, k, TP:T]).then_inc(sem("out_turned"), 1)

        @block.scalar
        def _(act):
            def f(o, i, func, **kw):
                return nc.scalar.activation(o, i, func, **kw)

            act.wait_ge(sem("w_small_clear"), 1)
            act.dma_start(w_small[:, :, 0:16], io["w_in"][0, :, COL_LRA:COL_LRA + 16].rearrange("(k p) n -> p k n", p=P)).then_inc(sem("w_small_loaded"), 16)
            act.dma_start(w_small[:, :, 32:40], io["w_in"][0, :, COL_FB:COL_FB + 8].rearrange("(k p) n -> p k n", p=P)).then_inc(sem("w_small_loaded"), 16)

            act.wait_ge(sem("c_loaded"), 32)
            f(c_sig[0:NC, :], c_in[0:NC, :], ACT.Sigmoid).then_inc(reach("c_sig_ready"), 1)
            for k in range(KT):
                act.wait_ge(sem("xT_copied"), k + 1)
                f(sq[:, k, :], xT[:, k, :], ACT.Square).then_inc(sem("xT_squared"), 1)
            act.wait_ge(*step("ms1_ready"))
            f(ms[:, :], ms[:, :], ACT.Sqrt).then_inc(reach("root1_ready"), 1)
            for j in range(2):
                act.wait_ge(sem("mod_summed"), j + 1)
                f(mod_row[:, j, :], ps[:, j, :], ACT.Copy).then_inc(sem("mod_row_ready"), 1)
            for k in range(KT):
                act.wait_ge(sem("h1_scaled"), k + 1)
                f(hT[:, k, 0:TP], hT[:, k, 0:TP], ACT.Identity, bias=modT[:, k, 0:1]).then_inc(sem("h1_shifted"), 1)
            def win_round(i, late_too):
                for n in range(1, 12, 2):
                    act.wait_ge(sem("win_tile"), i * 12 + (n + 1))
                    f(z[:, ds(i * (12 * T) + n * T, T)], ps[:, n % 6, 0:T], ACT.Copy).then_inc(sem("win_bank_free1"), 1)
                    if n == 11 and late_too:
                        act.wait_ge(sem("mod_summed"), i + 3)
                        act.wait_ge(sem("mod_turned"), i + 2)
                        f(mod_row[:, 2, :], ps[:, 7, :], ACT.Copy).then_inc(sem("mod_row_ready"), 1)

            with act.Fori(0, 2) as i:
                win_round(i, True)
            with act.Fori(2, 4) as i:
                win_round(i, False)
            act.wait_ge(*step("lra_fb_ready"))
            act.dma_start(wa2, io["w_a2"][0]).then_inc(sem("wa2_loaded"), 16)
            act.wait_ge(sem("za_abs"), 1)
            f(buf[0], buf[0], ACT.Exp, scale=-1.0).then_inc(reach("za_exp"), 1)
            act.wait_ge(sem("zf_abs"), 1)
            f(ms[0:H_B, :], ms[0:H_B, :], ACT.Exp, scale=-1.0).then_inc(reach("zf_exp"), 1)
            f(qa, qa, ACT.Copy, scale=SCALE)
            f(qb, qb, ACT.Copy, scale=SCALE).then_inc(reach("q_scaled"), 1)
            def copy_mod_row(sec):
                act.wait_ge(sem("mod_summed"), sec + 1)
                act.wait_ge(sem("mod_turned"), sec)
                f(mod_row[:, 2, :], ps[:, 7, :], ACT.Copy).then_inc(sem("mod_row_ready"), 1)

            copy_mod_row(4)
            for n, b in enumerate(LEVELS):
                act.wait_ge(sem("level_rel"), n + 1)
                tt = T if b <= 2 else TP
                for m, half in ((0, 1), (1, 0)):
                    v = level_pair(n)[m][:, :, 0:tt].rearrange("p h (n two t) -> p h n two t", two=2, t=b)[:, :, :, half, :]
                    last = f(v, v, ACT.Exp)
                last.then_inc(sem("level_exp"), 1)
            act.wait_ge(*step("decay_rel"))
            f(buf[2], buf[2], ACT.Exp)
            f(buf[3], buf[3], ACT.Exp)
            f(decay, decay, ACT.Exp).then_inc(reach("decay_exp"), 1)
            copy_mod_row(5)
            act.wait_ge(*step("oa_copied"))
            act.wait_ge(*step("os_turned_copied"))
            f(sq8, oaT, ACT.Square).then_inc(reach("oa_squared"), 1)
            act.wait_ge(*step("ms_a_ready"))
            f(rs4, rs4, ACT.Sqrt).then_inc(reach("root_a_ready"), 1)
            act.wait_ge(sem("state_updated"), DB)
            f(sig8, ra, ACT.Sigmoid).then_inc(reach("ra_sig"), 1)
            for h in range(H_B):
                act.wait_ge(sem("fox_max"), h + 1)
                if h >= 2:
                    act.wait_ge(sem("fox_turned"), h - 1)
                for q in range(2):
                    lo, n = q * P, P * (q + 1)
                    last = f(prob[:, h % 2, lo:lo + n], ps[:, 1 + h % 2, lo:lo + n], ACT.Exp,
                             bias=st_p[:, 4 * (h % 2) + q:4 * (h % 2) + q + 1],
                             accum_out=st_p[:, 8 + 4 * (h % 2) + q:8 + 4 * (h % 2) + q + 1])
                last.then_inc(sem("fox_exp"), 1)
            def copy_keys(b, r, used):
                for n in range(4 * r + 1, 4 * r + 4, 2):
                    act.wait_ge(sem("kt_turned_s"), b * 16 + (n + 1))
                    if used is not None:
                        act.wait_ge(sem("s_scored"), used)
                    f(ktR[:, 4 * (r % 2) + n % 4, :], ps[:, 5, :], ACT.Copy).then_inc(sem("kt_copied1"), 1)

            def sample_sequence(b, more):
                for r in (2, 3):
                    copy_keys(b, r, b * 4 + (r - 1))
                for g in range(2):
                    act.wait_ge(sem("s_max"), b * 2 + (g + 1))
                    f(pS[:, g, 0:PAST].rearrange("p (a n) -> p a n", a=2), ps[:, 2 * g:2 * g + 2, :], ACT.Exp,
                      bias=st_s[:, 4 * g:4 * g + 1], accum_out=st_s[:, 4 * g + 1:4 * g + 2])
                    f(pS[:, g, PAST:PAST + TS], s_new[:, g, :], ACT.Exp,
                      bias=st_s[:, 4 * g + 3:4 * g + 4], accum_out=st_s[:, 4 * g + 2:4 * g + 3]).then_inc(sem("s_prob"), 1)
                if more:
                    for r in (0, 1):
                        copy_keys(b + 1, r, b * 4 + (3 + r))

            act.wait_ge(sem("oa_final"), 1)
            for r in (0, 1):
                copy_keys(0, r, None)
            with act.Fori(0, DB - 1) as b:
                sample_sequence(b, True)
            sample_sequence(DB - 1, False)
            with act.Fori(0, 4) as g:
                for n in (0, 1, 2, 3, 8, 9, 10, 11):
                    act.wait_ge(sem("up_tile"), g * 16 + (n + 1))
                    m = n if n < 4 else n - 4
                    if n == 0:
                        act.wait_ge(sem("merged"), g * 4 + 1)
                    f(sig_ab[:, m, :], ps[:, n % 8, 0:T], ACT.Sigmoid).then_inc(sem("gate_sig"), 1)
            act.wait_ge(sem("merged"), 17)
            act.dma_start(wrt[:, :, 0:4], io["w_grp"][0].rearrange("(k p) n -> p k n", p=P)).then_inc(sem("router_loaded"), 16)
            act.dma_start(wrt[:, :, 4:20], io["w_exp"][0].rearrange("(k p) n -> p k n", p=P)).then_inc(sem("router_loaded"), 16)
            for k in range(KT):
                act.wait_ge(sem("x2_ready"), k + 1)
                f(sq2[:, k, :], xT[:, k, :], ACT.Square).then_inc(sem("x2_squared"), 1)
            act.wait_ge(*step("ms2_ready"))
            f(ms[:, :], ms[:, :], ACT.Sqrt).then_inc(reach("root2_ready"), 1)
            for k in range(KT):
                act.wait_ge(sem("h2_scaled"), k + 1)
                f(hT[:, k, 0:TP], hT[:, k, 0:TP], ACT.Identity, bias=modT[:, 48 + k, 0:1]).then_inc(sem("h2_shifted"), 1)
            act.wait_ge(sem("rt_shifted"), 1)
            f(rt[:, 400:412], rt[:, 400:412], ACT.Exp).then_inc(sem("rt_exp"), 1)
            act.wait_ge(sem("rt_shifted"), 2)
            f(rt[:, 420:423], rt[:, 420:423], ACT.Exp).then_inc(sem("rt_exp"), 1)
            for n in range(12):
                act.wait_ge(sem("htok_turned"), n + 1)
                f(hTok[:, n // 4, (n % 4) * 512:(n % 4 + 1) * 512], ps[0:TT, 2 + n % 4, :], ACT.Copy).then_inc(sem("htok_copied"), 1)
            act.wait_ge(*step("table_ready"))
            windows = act.value_load(wtab[0:1, 0:1], min_val=NG, max_val=MAXW)
            with act.Fori(0, windows) as it:
                for j in range(EG):
                    act.wait_ge(sem("gate_ready"), it * EG + (j + 1))
                    act.wait_ge(sem("sg_free"), it * EG + (j + 1))
                    f(sg, ps[:, 4 + j % 2, :], ACT.Sigmoid).then_inc(sem("sg_ready"), 1)
            for n in range(12):
                act.wait_ge(sem("ytok_turned"), n + 1)
                f(yTok[:, n // 4, (n % 4) * 512:(n % 4 + 1) * 512], ps[0:TT, 4 + n % 4, :], ACT.Copy).then_inc(sem("ytok_copied"), 1)
            for k in range(KT):
                act.wait_ge(sem("x3_ready"), k + 1)
                f(sq2[:, k, :], xT[:, k, :], ACT.Square).then_inc(sem("x3_squared"), 1)
            act.wait_ge(*step("ms3_ready"))
            f(ms[:, :], ms[:, :], ACT.Sqrt).then_inc(reach("root3_ready"), 1)

        @block.vector
        def _(v):
            def tt(o, a, b, op):
                return nc.vector.tensor_tensor(o, a, b, op)

            def tsc(o, a, s1, s2, op0, op1=None):
                return nc.vector.tensor_scalar(o, a, s1, s2, op0) if op1 is None else nc.vector.tensor_scalar(o, a, s1, s2, op0, op1)

            def stt(o, a, s, b, op0, op1):
                return nc.vector.scalar_tensor_tensor(out=o, in0=a, scalar=s, in1=b, op0=op0, op1=op1)

            def copy(o, a):
                return nc.vector.tensor_copy(o, a)

            for name, n in (("late_free0", 1), ("late_free1", 1), ("win_bank_free0", 3), ("win_bank_free1", 3),
                            ("up_bank_free", 8), ("gate_read", 2),
                            ("merged", 1), ("o_all_ready", 1), ("kt_copied0", 1), ("kt_copied1", 1),
                            *((f"ring_free{s}", 1) for s in range(SLOTS)),
                            ("up_read", 1), ("comb_read", 1), ("y_bank_free", 1), ("sg_free", 1)):
                v.sem_inc(sem(name), n)

            v.wait_ge(*step("c_sig_ready"))
            tt(c_in[0:NC, :], c_in[0:NC, :], c_sig[0:NC, :], ALU.mult).then_inc(reach("c_silu"), 1)
            nc.vector.memset(cT, 0.0)
            v.drain()
            v.wait_ge(*step("c_turned"))
            copy(cT[:, :, 0:NC], ps[:, 5, 0:KT * NC].rearrange("p (k c) -> p k c", c=NC)).then_inc(reach("cT_ready"), 1)
            for k in range(KT):
                v.wait_ge(sem("xT_turned"), k + 1)
                copy(xT[:, k, :], ps[:, k % 4, 0:T]).then_inc(sem("xT_copied"), 1)
            v.wait_ge(*step("ss1_ready"))
            tsc(ms[:, :], ps[:, 4, 0:T], 1.0 / D, EPS, ALU.mult, ALU.add).then_inc(reach("ms1_ready"), 1)
            v.wait_ge(*step("root1_ready"))
            nc.vector.reciprocal(rstd[:, :], ms[:, :])
            v.wait_ge(*step("vec_turned"))
            copy(vcol[:, 0:150], ps[:, 6, 0:150])
            v.drain()

            def add_bias(section, bank):
                v.wait_ge(sem("mod_turned"), section + 1)
                at = section * KT
                at = slice(at, at + KT) if isinstance(section, int) else ds(at, KT)
                o = modT[:, at, :].rearrange("p (c t) n -> p t c n", c=4)
                s = ps[:, bank, :].rearrange("p (t c n) -> p t c n", t=4, c=4)[:, :, :, 0:NC]
                bias = vcol[:, at].rearrange("p (c t) -> p t c", c=4).unsqueeze(3).to_broadcast([P, 4, 4, NC])
                tt(o, s, bias, ALU.add).then_inc(sem("mod_ready"), 1)

            for j in range(2):
                add_bias(j, 3 + j)
            v.wait_ge(sem("mod_ready"), 2)

            def modulate(tag, shift, scale, gain):
                stt(mod_a[:, :, :], modT[:, scale:scale + KT, :], 1.0,
                    vcol[:, gain:gain + KT].unsqueeze(2).to_broadcast([P, KT, NC]), ALU.add, ALU.mult)
                v.drain()
                hsv = hT[:, :, TP:T]
                h4 = hsv.rearrange("p k (b t) -> p k b t", t=DT)
                tt(hsv, xT[:, :, TP:T], rstd[:, TP:T].unsqueeze(1).to_broadcast([P, KT, TS]), ALU.mult)
                v.drain()
                tt(h4, h4, mod_a[:, :, 1:NC].unsqueeze(3).to_broadcast([P, KT, DB, DT]), ALU.mult)
                v.drain()
                tt(h4, h4, modT[:, shift:shift + KT, 1:NC].unsqueeze(3).to_broadcast([P, KT, DB, DT]), ALU.add)
                v.drain()
                v.sem_inc(sem(f"{tag}_ready"), 1)
                for k in range(KT):
                    stt(hT[:, k, 0:TP], xT[:, k, 0:TP], mod_a[:, k, 0:1], rstd[:, 0:TP], ALU.mult, ALU.mult).then_inc(sem(f"{tag}_scaled"), 1)

            modulate("h1", 0, KT, V_G1)
            def win_round(i, late_too):
                for n in range(0, 12, 2):
                    v.wait_ge(sem("win_tile"), i * 12 + (n + 1))
                    copy(z[:, ds(i * (12 * T) + n * T, T)], ps[:, n % 6, 0:T]).then_inc(sem("win_bank_free0"), 1)
                if late_too:
                    add_bias(i + 2, 6)

            with v.Fori(0, 2) as i:
                win_round(i, True)
            with v.Fori(2, 4) as i:
                win_round(i, False)
            v.wait_ge(*step("lra_fb_ready"))
            v.wait_ge(sem("small_loaded"), 16 * N_SMALL)
            tsc(fT[:, :], ps[32:40, 6, 0:T], bfc[:, 0:1], None, ALU.add)
            copy(lraT, ps[0:16, 6, 0:T]).then_inc(reach("lra_copied"), 1)
            v.wait_ge(*step("za_ready"))
            for h in range(H_A):
                last = tsc(la[:, h, :], ps[:, h, 0:T], vcol[:, V_BA + h:V_BA + h + 1], None, ALU.add)
            last.then_inc(reach("za_read"), 1)
            v.drain()

            def log_sigmoid(x, e, a, b, c, tag, scale):
                tsc(e, x, -1.0, None, ALU.mult)
                v.drain()
                tt(e, e, x, ALU.max).then_inc(sem(f"{tag}_abs"), 1)
                tsc(x, x, 0.0, None, ALU.min)
                v.wait_ge(*step(f"{tag}_exp"))
                tsc(a, e, 2.0, None, ALU.add)
                v.drain()
                nc.vector.reciprocal(a, a)
                v.drain()
                tt(a, a, e, ALU.mult)
                v.drain()
                tt(b, a, a, ALU.mult)
                v.drain()
                tsc(c, b, 1.0 / 17, None, ALU.mult)
                for n in (15, 13, 11, 9, 7, 5, 3):
                    v.drain()
                    stt(c, c, 1.0 / n, b, ALU.add, ALU.mult)
                v.drain()
                stt(c, c, 1.0, a, ALU.add, ALU.mult)
                v.drain()
                stt(x, c, -2.0, x, ALU.mult, ALU.add)
                v.drain()
                if scale != 1.0:
                    tsc(x, x, scale, None, ALU.mult)
                    v.drain()

            laf = wk[:, 0:F4]
            log_sigmoid(laf, buf[0], buf[1], buf[2], buf[3], "za", 1.0 / 16)
            log_sigmoid(fT[:, :], ms[0:H_B, :], fa, fb_, fc, "zf", 1.0)
            v.sem_inc(reach("logf_ready"), 1)
            for h in range(H_A):
                for c in range(2):
                    nc.vector.tensor_tensor_scan(cum[:, h, c * P:(c + 1) * P], ones[:, :], la[:, h, c * P:(c + 1) * P], 0.0, ALU.mult, ALU.add)
            cs4 = cum[:, :, TP:T].rearrange("p h (b t) -> p h b t", t=DT)
            copy(cum[:, :, TP:T], la[:, :, TP:T])
            v.drain()
            for t in range(1, DT):
                tt(cs4[:, :, :, t], cs4[:, :, :, t - 1], cs4[:, :, :, t], ALU.add)
                v.drain()
            add_bias(4, 6)
            v.wait_ge(*step("va_turned"))
            for c in range(2):
                copy(vaTok[:, c, :].rearrange("p (a n) -> p a n", a=2), ps[:, 4 + 2 * c:6 + 2 * c, :])
            copy(vaS.rearrange("p (a n) -> p a n", a=2), ps[0:TS, 0:2, :])
            v.drain()
            v.sem_inc(reach("va_copied"), 1)
            v.wait_ge(sem("masks_ready"), 1)
            v.wait_ge(sem("consts_ready"), 1)
            def add_level(n):
                v.wait_ge(sem("level_scored"), n + 1)
                b0 = 3 * (n % 2)
                mask = level_mask[:, n, :] if n < len(LEVELS) else ident[:, :]
                tmp = laf[:, 0:1024].rearrange("p (c h t) -> p c h t", c=2, h=H_A)
                dst = atP if n == 0 else tmp
                for c in range(2):
                    tt(dst[:, c], ps[:, b0 + c, :].rearrange("p (h t) -> p h t", h=H_A),
                       mask.unsqueeze(1).to_broadcast([P, H_A, P]), ALU.mult)
                first_s = len(LEVELS) - 2
                tmps = laf[0:TS, 1024:1152].rearrange("p (h t) -> p h t", h=H_A)
                if n >= first_s:
                    tt(atS if n == first_s else tmps, ps[0:TS, b0 + 2, 0:H_A * TS].rearrange("p (h t) -> p h t", h=H_A),
                       mask[0:TS, 0:TS].unsqueeze(1).to_broadcast([TS, H_A, TS]), ALU.mult)
                v.drain()
                v.sem_inc(sem("level_read"), 1)
                if n:
                    tt(atP, atP, tmp, ALU.add)
                if n > first_s:
                    tt(atS, atS, tmps, ALU.add)
                v.drain()

            def halves(n):
                b = LEVELS[n]
                tm = T if b <= 2 else TP
                ql, kl = level_pair(n)
                return [a[:, :, 0:tm].rearrange("p h (n two t) -> p h n two t", two=2, t=b) for a in (cum, ql, kl, qa, ka)]

            def exponents(n):
                b = LEVELS[n]
                cv, qv, kv, _, _ = halves(n)
                if n >= 2:
                    v.wait_ge(sem("level_scored"), n - 1)
                for h in range(H_A):
                    ref = cv[:, h, :, 0, b - 1:b].to_broadcast([P, (T if b <= 2 else TP) // (2 * b), b])
                    tt(qv[:, h, :, 1, :], cv[:, h, :, 1, :], ref, ALU.subtract)
                    last = tt(kv[:, h, :, 0, :], ref, cv[:, h, :, 0, :], ALU.subtract)
                last.then_inc(sem("level_rel"), 1)

            exponents(0)
            v.wait_ge(*step("q_scaled"))
            for n in range(len(LEVELS)):
                if n + 1 < len(LEVELS):
                    exponents(n + 1)
                v.wait_ge(sem("level_exp"), n + 1)
                _, qv, kv, q0, k0 = halves(n)
                for h in range(H_A):
                    tt(qv[:, h, :, 1, :], qv[:, h, :, 1, :], q0[:, h, :, 1, :], ALU.mult)
                    last = tt(kv[:, h, :, 0, :], kv[:, h, :, 0, :], k0[:, h, :, 0, :], ALU.mult)
                v.drain()
                v.sem_inc(sem("level_ready"), 1)
                if n:
                    add_level(n - 1)
            v.sem_inc(sem("level_ready"), 1)
            copy(buf3[2], cum)
            for c in range(2):
                e = (c + 1) * P
                tt(buf3[3][:, :, c * P:e], cum[:, :, e - 1:e].to_broadcast([P, H_A, P]), cum[:, :, c * P:e], ALU.subtract)
                copy(decay[:, :, c:c + 1], cum[:, :, e - 1:e])
            for h in range(H_A):
                tt(buf3[3][:, h, TP:T].rearrange("p (b t) -> p b t", t=DT), cs4[:, h, :, DT - 1:DT].to_broadcast([P, DB, DT]),
                   cs4[:, h], ALU.subtract)
            copy(decay[:, :, 2:10], cs4[:, :, :, DT - 1])
            v.drain()
            v.sem_inc(reach("decay_rel"), 1)
            add_level(len(LEVELS) - 1)
            v.wait_ge(*step("decay_exp"))
            tt(buf3[2], buf3[2], qa, ALU.mult)
            tt(buf3[3], buf3[3], ka, ALU.mult)
            v.drain()
            v.sem_inc(reach("decayed_ready"), 1)
            add_level(len(LEVELS))
            add_bias(5, 2)
            v.wait_ge(*step("kt_turned"))
            copy(ktP, ps[:, 6:8, :])
            copy(ktS, ps[0:TS, 0, :])
            v.drain()
            v.sem_inc(reach("kt_copied"), 1)
            v.wait_ge(*step("state1_ready"))
            copy(stP.rearrange("p (a h) v -> p a (h v)", a=2), ps[:, 4:6, :]).then_inc(reach("state1_copied"), 1)
            v.wait_ge(*step("oa_ready"))
            copy(oaT[:, :, 0:TP].rearrange("p (a n) t -> p a n t", a=4), ps[:, 0:4, :].rearrange("p a (n t) -> p a n t", n=2)).then_inc(reach("oa_copied"), 1)
            v.wait_ge(*step("update2_ready"))
            for h in range(H_A):
                last = stt(stP[:, h, :], stP[:, h, :], decay[:, h, 1:2], ps[:, 6 + h // 2, (h % 2) * DV:(h % 2 + 1) * DV], ALU.mult, ALU.add)
            v.drain()
            v.sem_inc(reach("gla_prompt_ready"), 1)
            v.sem_inc(reach("update2_used"), 1)
            v.wait_ge(*step("os_own_ready"))
            copy(osS, ps[:, 4, 0:DV])
            v.wait_ge(*step("os_state_ready"))
            for b in range(DB):
                v.drain()
                stt(osS, ps[:, b // 2, (b % 2) * DV:(b % 2 + 1) * DV], own_seq[:, b:b + 1], osS, ALU.mult, ALU.add)
            v.drain()
            v.sem_inc(reach("os_summed"), 1)
            def mask_keys(b):
                tsc(kms[b % 2], ktS, own_seq[0:TS, b:b + 1], None, ALU.mult).then_inc(sem("km_ready"), 1)

            mask_keys(0)
            mask_keys(1)
            for b in range(DB):
                v.wait_ge(sem("update_ready"), b + 1)
                bank = 6 if b % 2 == 0 else 2
                for h in range(H_A):
                    last = stt(state[:, b, h, :], state[:, b, h, :], decay[:, h, 2 + b:3 + b],
                               ps[:, bank + h // 2, (h % 2) * DV:(h % 2 + 1) * DV], ALU.mult, ALU.add)
                last.then_inc(sem("state_updated"), 1)
                if b + 2 < DB:
                    mask_keys(b + 2)
            v.wait_ge(sem("state_updated"), DB)
            v.sem_inc(reach("gla_sample_ready"), 1)
            v.wait_ge(*step("os_turned"))
            for w in range(VB):
                copy(oaT[:, :, TP:T].rearrange("p (h w) t -> p w h t", w=VB)[:, w], ps[:, 4, w * P:(w + 1) * P].rearrange("p (h t) -> p h t", h=H_A))
            v.drain()
            v.sem_inc(reach("os_turned_copied"), 1)
            v.wait_ge(sem("gla_prompt_stored"), 16)
            v.sem_inc(reach("gla_scratch_free"), 1)
            v.wait_ge(*step("ss_a_ready"))
            tsc(rs4, ps[:, 0:4, 0:T], 1.0 / DV, EPS, ALU.mult, ALU.add)
            v.drain()
            v.sem_inc(reach("ms_a_ready"), 1)
            v.sem_inc(reach("rs_a_ready"), 1)
            v.wait_ge(*step("root_a_ready"))
            nc.vector.reciprocal(rs4, rs4).then_inc(reach("rs_a_inverted"), 1)

            v.wait_ge(sem("tok_turned"), 1)
            for c in range(2):
                copy(kbTok[:, c, :].rearrange("p (a n) -> p a n", a=2), ps[:, 4 + 2 * c:6 + 2 * c, :])
            v.drain()
            v.sem_inc(sem("tok_copied"), 1)
            v.wait_ge(sem("tok_turned"), 2)
            vtmp = wk[:, 0:2048].rearrange("p (c n) -> p c n", c=2)
            for c in range(2):
                copy(vtmp[:, c, :].rearrange("p (a n) -> p a n", a=2), ps[:, 4 + 2 * c:6 + 2 * c, :])
            v.drain()
            v.sem_inc(sem("tok_copied"), 1)
            v.wait_ge(sem("tok_turned"), 3)
            v.wait_ge(*step("gla_prompt_ready"))
            copy(kbS.rearrange("p (a n) -> p a n", a=2), ps[0:TS, 4:6, :])
            copy(vbS.rearrange("p (a n) -> p a n", a=2), ps[0:TS, 6:8, :])
            copy(vbTok, vtmp)
            v.wait_ge(*step("lf_turned"))
            v.wait_ge(sem("gate_a_ready"), 1)
            copy(lfTok[:, 0:2, :], ps[:, 0, 0:16].rearrange("p (c h) -> p c h", c=2))
            copy(lfTok[0:TS, 2, :], ps[0:TS, 0, 16:24])
            v.drain()
            v.sem_inc(sem("tok_copied"), 2)
            v.sem_inc(reach("kv_tok_ready"), 1)
            nc.vector.tensor_tensor_scan(nfT[:, 0:TP], ones[0:H_B, 0:1].to_broadcast([H_B, TP]), fT[:, 0:TP], 0.0, ALU.mult, ALU.add)
            f4 = fT[:, TP:T].rearrange("p (b t) -> p b t", t=DT)
            for t in range(1, DT):
                tt(f4[:, :, t], f4[:, :, t - 1], f4[:, :, t], ALU.add)
                v.drain()
            copy(fT[:, 0:TP], nfT[:, 0:TP])
            v.drain()
            tsc(nfT[:, :], fT[:, :], -1.0, None, ALU.mult)
            v.drain()
            v.sem_inc(reach("f_ready"), 1)
            for i in range(H_B + 1):
                if i < H_B:
                    h = i
                    v.wait_ge(sem("fox_scored"), h + 1)
                    diag = ps[:, 1 + h % 2, :].rearrange("p (n q) -> p n q", q=P)[:, 0:3:2, :]
                    tt(diag, diag, fox_mask[:, :].unsqueeze(1).to_broadcast([P, 2, P]), ALU.add)
                    v.drain()
                    for q in range(2):
                        lo, n = q * P, P * (q + 1)
                        nc.vector.tensor_reduce(st_p[:, 4 * (h % 2) + q:4 * (h % 2) + q + 1], ps[:, 1 + h % 2, lo:lo + n], AX.X, ALU.max, negate=True)
                    v.drain()
                    v.sem_inc(sem("fox_max"), 1)
                if 1 <= i <= H_B:
                    h = i - 1
                    v.wait_ge(sem("fox_exp"), h + 1)
                    den = st_p[:, 8 + 4 * (h % 2):10 + 4 * (h % 2)]
                    nc.vector.reciprocal(den, den)
                    v.drain()
                    for q in range(2):
                        lo, n = q * P, P * (q + 1)
                        tsc(prob[:, h % 2, lo:lo + n], prob[:, h % 2, lo:lo + n], den[:, q:q + 1], None, ALU.mult)
                    v.drain()
                    v.sem_inc(sem("fox_prob"), 1)
                    v.wait_ge(sem("fox_turned"), h + 1)
                    if h >= 2:
                        v.wait_ge(sem("fox_pv"), h - 1)
                    copy(probT[:, h % 2, :], ps[:, 3, 0:3 * P]).then_inc(sem("fox_pt"), 1)
                    v.wait_ge(sem("fox_pv"), h + 1)
                    copy(obT[:, h, 0:TP], ps[:, 4 + h % 2, 0:TP]).then_inc(sem("fox_out"), 1)

            v.wait_ge(sem("kv_stored"), 6 * 16)
            v.wait_ge(sem("oa_final"), 1)
            v.sem_inc(sem("lf_used"), 1)
            v.wait_ge(*step("s_new_ready"))
            tt(s_new, ps[:, 0, 0:2 * TS].rearrange("p (g t) -> p g t", g=2), new_mask[:, :].unsqueeze(1).to_broadcast([P, 2, TS]), ALU.add)
            copy(fn_r, ps[:, 1, 0:2])
            nc.vector.memset(o_all, 0.0)
            v.drain()
            v.sem_inc(reach("s_new_copied"), 1)
            def sum_forgets(b):
                v.wait_ge(sem("lf_loaded"), b * (16 * NPG) + 16 * NPG)
                nc.vector.memset(lf_b[:, NPG - 1:NPG, :], 0.0)
                v.drain()
                for n in range(NPG - 2, -1, -1):
                    tt(lf_b[:, n, :], lf_b[:, n + 1, :], lf_in[:, n + 1, :], ALU.add)
                    v.drain()
                v.sem_inc(sem("lf_summed"), 1)

            def copy_forgets(b):
                v.wait_ge(sem("r_ready"), b + 1)
                copy(rT.rearrange("p (a n) -> p a n", a=2), ps[0:H_B, 6:8, :]).then_inc(sem("r_copied"), 1)
                v.sem_inc(sem("lf_used"), 1)

            def copy_keys(b, r, used):
                for n in range(4 * r, 4 * r + 4, 2):
                    v.wait_ge(sem("kt_turned_s"), b * 16 + (n + 1))
                    if used is not None:
                        v.wait_ge(sem("s_scored"), used)
                    copy(ktR[:, 4 * (r % 2) + n % 4, :], ps[:, 4, :]).then_inc(sem("kt_copied0"), 1)

            def sample_sequence(b, more):
                for r in (2, 3):
                    copy_keys(b, r, b * 4 + (r - 1))
                for g in range(2):
                    m = st_s[:, 4 * g:4 * g + 1]
                    v.wait_ge(sem("s_scored"), b * 4 + (3 + g))
                    nc.vector.tensor_reduce(st_s[:, 16 + 4 * g:17 + 4 * g], ps[:, 2 * g:2 * g + 2, :], AX.XY, ALU.max)
                    nc.vector.tensor_reduce(st_s[:, 17 + 4 * g:18 + 4 * g], s_new[:, g, :], AX.X, ALU.max)
                    v.drain()
                    tt(st_s[:, 16 + 4 * g:17 + 4 * g], st_s[:, 16 + 4 * g:17 + 4 * g], fn_r[:, g:g + 1], ALU.add)
                    v.drain()
                    tt(st_s[:, 18 + 4 * g:19 + 4 * g], st_s[:, 16 + 4 * g:17 + 4 * g], st_s[:, 17 + 4 * g:18 + 4 * g], ALU.max)
                    v.drain()
                    tsc(st_s[:, 4 * g + 3:4 * g + 4], st_s[:, 18 + 4 * g:19 + 4 * g], -1.0, None, ALU.mult)
                    tt(m, fn_r[:, g:g + 1], st_s[:, 18 + 4 * g:19 + 4 * g], ALU.subtract)
                    v.drain()
                    v.sem_inc(sem("s_max"), 1)
                if more:
                    for r in (0, 1):
                        copy_keys(b + 1, r, b * 4 + (3 + r))
                    sum_forgets(b + 1)
                for n in range(5):
                    v.wait_ge(sem("pt_turned"), b * 5 + (n + 1))
                    if n < 4:
                        last = copy(pTS[:, n // 2, 4 * (n % 2):4 * (n % 2) + 4, :], ps[:, 6 + n % 2, :].rearrange("p (n t) -> p n t", n=4))
                    else:
                        last = copy(pTN, ps[0:TS, 6, 0:2 * P].rearrange("p (g t) -> p g t", g=2))
                    last.then_inc(sem("pt_copied"), 1)
                if more:
                    copy_forgets(b + 1)
                for g in range(2):
                    tt(st_s[:, 24 + g:25 + g], st_s[:, 4 * g + 1:4 * g + 2], st_s[:, 4 * g + 2:4 * g + 3], ALU.add)
                v.drain()
                nc.vector.reciprocal(st_s[:, 24:26], st_s[:, 24:26])
                v.drain()
                tsc(st_s[:, 26:28], st_s[:, 24:26], own_seq[:, ds(b, 1)], None, ALU.mult)
                v.drain()
                v.wait_ge(sem("o_b_ready"), b + 1)
                for g in range(2):
                    last = stt(o_all[:, g, :], ps[:, 5, g * P:(g + 1) * P], st_s[:, 26 + g:27 + g], o_all[:, g, :], ALU.mult, ALU.add)
                v.drain()
                v.sem_inc(sem("o_all_ready"), 1)

            sum_forgets(0)
            copy_forgets(0)
            for r in (0, 1):
                copy_keys(0, r, None)
            with v.Fori(0, DB - 1) as b:
                sample_sequence(b, True)
            sample_sequence(DB - 1, False)
            v.wait_ge(*step("o_all_turned"))
            copy(obT[:, :, TP:T].rearrange("p (g c) t -> p g c t", g=2), ps[:, 0, 0:2 * P].rearrange("p (g c t) -> p g c t", g=2, c=4))
            v.drain()
            v.sem_inc(reach("ob_ready"), 1)
            v.sem_inc(reach("work_free"), 1)

            with v.Fori(0, 4) as g:
                for half in range(2):
                    for t in range(4):
                        v.wait_ge(sem("gate_sig"), g * 8 + (4 * half + t + 1))
                        v.sem_inc(sem("up_bank_free"), 1)
                    for t in range(4):
                        tile, m = 8 * half + 4 + t, 4 * half + t
                        v.wait_ge(sem("up_tile"), g * 16 + (tile + 1))
                        tt(sig_ab[:, m, :], sig_ab[:, m, :], ps[:, tile % 8, 0:T], ALU.mult)
                        v.drain()
                        v.sem_inc(sem("up_bank_free"), 1)
                        if half:
                            tt(mgT[:, ds(g * 4 + t, 1), :].rearrange("p a t -> p (a t)"), sig_ab[:, t, :], sig_ab[:, m, :], ALU.add)\
                                .then_inc(sem("merged"), 1)

            def gated_add(k, bank, gate):
                stt(xT[:, k, 0:TP], ps[:, bank, 0:TP], modT[:, gate + k, 0:1], xT[:, k, 0:TP], ALU.mult, ALU.add)
                tt(shifted[:, :].rearrange("p (b t) -> p b t", t=DT), ps[:, bank, TP:T].rearrange("p (b t) -> p b t", t=DT),
                   modT[:, gate + k, 1:NC].unsqueeze(2).to_broadcast([P, DB, DT]), ALU.mult)
                v.drain()
                tt(xT[:, k, TP:T], xT[:, k, TP:T], shifted[:, :], ALU.add)
                v.drain()

            for k in range(KT):
                v.wait_ge(sem("wout_tile"), k + 1)
                gated_add(k, k % 7, 2 * KT)
                v.sem_inc(sem("up_bank_free"), 1)
                v.sem_inc(sem("x2_ready"), 1)
            v.wait_ge(*step("ss2_ready"))
            tsc(ms[:, :], ps[:, 7, 0:T], 1.0 / D, EPS, ALU.mult, ALU.add).then_inc(reach("ms2_ready"), 1)
            v.wait_ge(*step("root2_ready"))
            nc.vector.reciprocal(rstd[:, :], ms[:, :])
            v.drain()
            modulate("h2", 3 * KT, 4 * KT, V_G2)

            lg = rt[:, 340:400].rearrange("p (c n) -> p c n", c=NT)
            oh = rt[:, 0:12].rearrange("p (c n) -> p c n", c=NT)
            comb = rt[:, 64:64 + NT * NE].rearrange("p (c g j) -> p c g j", c=NT, g=NG)
            gx = rt[:, 400:412].rearrange("p (c n) -> p c n", c=NT)
            e2 = rt[:, 420:423]
            mx = rt[:, 430:433]
            gw = rt[:, 440:443]
            t4 = rt[:, 450:462].rearrange("p (c n) -> p c n", c=NT)
            ein = rt[:, 470:482].rearrange("p (c n) -> p c n", c=NT)
            oh1 = rt[:, 490:502].rearrange("p (c n) -> p c n", c=NT)
            oh2 = rt[:, 510:522].rearrange("p (c n) -> p c n", c=NT)
            m1, m2, w1 = rt[:, 530:533], rt[:, 540:543], rt[:, 550:553]
            prod = rt[:, 120:168].rearrange("p (c g j) -> p c g j", c=NT, g=NG)

            def spread(a):
                return a.unsqueeze(2).to_broadcast([TT, NT, 4])

            def red(o, i, op):
                return nc.vector.tensor_reduce(o, i, AX.X, op)

            def first_max(o, i, m):
                red(m, i, ALU.max)
                v.drain()
                tt(o, i, spread(m), ALU.is_equal)
                v.drain()
                tt(o, o, ramp[0:TT, :].unsqueeze(1).to_broadcast([TT, NT, 4]), ALU.mult)
                v.drain()
                red(mx, o, ALU.max)
                v.drain()
                tt(o, ramp[0:TT, :].unsqueeze(1).to_broadcast([TT, NT, 4]), spread(mx), ALU.is_equal)
                v.drain()

            v.wait_ge(sem("route_consts_ready"), 1)
            v.wait_ge(*step("logits_ready"))
            copy(lg, ps[0:TT, 1, 0:60].rearrange("p (c n) -> p c n", c=NT))
            v.drain()
            gl = lg[:, :, 0:4]
            first_max(oh, gl, m1)
            v.sem_inc(reach("onehot_ready"), 1)
            tt(gx, gl, spread(m1), ALU.subtract).then_inc(sem("rt_shifted"), 1)
            el = lg[:, :, 4:20]
            for c in range(NT):
                tt(prod[:, c], el[:, c, :].rearrange("p (g j) -> p g j", g=NG), oh[:, c, :].unsqueeze(2).to_broadcast([TT, NG, EG]), ALU.mult)
            v.drain()
            for c in range(NT):
                red(ein[:, c, :], prod[:, c].rearrange("p g j -> p j g"), ALU.add)
            v.wait_ge(sem("rt_exp"), 1)
            red(gw, gx, ALU.add)
            v.drain()
            nc.vector.reciprocal(gw, gw)
            first_max(oh1, ein, m1)
            stt(t4, oh1, -BIG, ein, ALU.mult, ALU.add)
            v.drain()
            first_max(oh2, t4, m2)
            tt(e2, m2, m1, ALU.subtract).then_inc(sem("rt_shifted"), 1)
            v.wait_ge(sem("rt_exp"), 2)
            tsc(w1, e2, 1.0, None, ALU.add)
            v.drain()
            nc.vector.reciprocal(w1, w1)
            v.drain()
            tt(w1, w1, gw, ALU.mult)
            v.drain()
            tt(e2, e2, w1, ALU.mult)
            tt(oh1, oh1, spread(w1), ALU.mult)
            v.drain()
            tt(oh2, oh2, spread(e2), ALU.mult)
            v.drain()
            tt(oh1, oh1, oh2, ALU.add)
            v.drain()
            for c in range(NT):
                tt(comb[:, c], oh1[:, c, :].unsqueeze(1).to_broadcast([TT, NG, EG]), oh[:, c, :].unsqueeze(2).to_broadcast([TT, NG, EG]), ALU.mult)
            v.wait_ge(*step("rank_ready"))
            size, start = rt[:, 560:564], rt[:, 565:569]
            copy(size, ps[0:TT, 6, 16:20])
            nc.vector.memset(start, 0.0)
            v.drain()
            for g in range(1, NG):
                tt(start[:, g:g + 1], start[:, g - 1:g], size[:, g - 1:g], ALU.add)
                v.drain()
            tt(t4, ps[0:TT, 6, 0:12].rearrange("p (c n) -> p c n", c=NT), start.unsqueeze(1).to_broadcast([TT, NT, 4]), ALU.add)
            v.drain()
            tt(t4, t4, oh, ALU.mult)
            v.drain()
            red(prow[:, 0:3], t4, ALU.add)
            v.drain()
            for c in range(NT):
                tt(perm[:, c, :], iota_pos[0:TT, :], prow[:, c:c + 1].to_broadcast([TT, T]), ALU.is_equal)
            v.drain()
            v.sem_inc(reach("perm_ready"), 1)
            nw, more, first, base, dbase = (rrow[:, 4 * n:4 * n + 4] for n in range(5))
            begun, tab_e, tab_at = rrow[:, 20:28], rrow[:, 32:40], rrow[:, 40:48]
            tsc(nw, size[0:1, :], float(W), None, ALU.is_gt)
            tsc(more, size[0:1, :], float(2 * W), None, ALU.is_gt)
            v.drain()
            tt(nw, nw, more, ALU.add)
            v.drain()
            tsc(nw, nw, 1.0, None, ALU.add)
            nc.vector.memset(first, 0.0)
            v.drain()
            for g in range(1, NG):
                tt(first[:, g:g + 1], first[:, g - 1:g], nw[:, g - 1:g], ALU.add)
                v.drain()
            stt(base, first, -float(W), start[0:1, :], ALU.mult, ALU.add)
            nc.vector.memset(tab_e, -float(EG))
            tsc(tab_at, iota_pos[0:1, 0:8], float(W), None, ALU.mult)
            v.drain()
            copy(dbase[:, 0:1], base[:, 0:1])
            tt(dbase[:, 1:4], base[:, 1:4], base[:, 0:3], ALU.subtract)
            for g in range(NG):
                v.drain()
                tsc(begun, iota_pos[0:1, 0:8], first[:, g:g + 1], None, ALU.is_ge)
                v.drain()
                stt(tab_e, begun, float(EG), tab_e, ALU.mult, ALU.add)
                stt(tab_at, begun, dbase[:, g:g + 1], tab_at, ALU.mult, ALU.add)
            v.drain()
            tsc(tab_at, tab_at, float(T), None, ALU.min)
            tt(more[:, 0:1], first[:, 3:4], nw[:, 3:4], ALU.add)
            v.drain()
            tsc(more[:, 1:2], more[:, 0:1], -1.0, None, ALU.add)
            v.drain()
            copy(wtab[:, 0:2], more[:, 0:2])
            copy(wtab[:, 2:10], tab_e)
            copy(wtab[:, 12:20], tab_at)
            v.drain()
            v.sem_inc(reach("table_ready"), 1)
            v.wait_ge(sem("htok_copied"), 12)
            nc.vector.memset(cs, 0.0)
            nc.vector.memset(hs[:, :, T:TW], 0.0)
            nc.vector.memset(ys, 0.0)
            v.drain()
            v.wait_ge(*step("cs_summed"))
            copy(cs[:, 0:T], ps[0:NE, 7, 0:T])
            for k in range(KT):
                v.wait_ge(sem("hs_summed"), k + 1)
                copy(hs[:, k, 0:T], ps[:, 2 + k % 4, 0:T]).then_inc(sem("hs_copied"), 1)
            v.wait_ge(*step("perm_turned"))
            for c, bank in enumerate((0, 1, 6)):
                copy(permT[:, c, :], ps[0:TT, bank, 0:T])
            v.drain()
            v.sem_inc(reach("perm_copied"), 1)
            v.sem_inc(reach("hs_ready"), 1)

            def position(w):
                at = v.value_load(wtab[0:1, ds(w + 12, 1)], min_val=0, max_val=T)
                return at

            def window(w):
                e = v.value_load(wtab[0:1, ds(w + 2, 1)], min_val=0, max_val=NE - EG)
                at = position(w)
                copy(hw, hs[:, :, ds(at, W)])
                copy(cw, cs[:, ds(at, W)])
                copy(selw, ident[0:NE, ds(e, EG)])
                v.drain()
                v.sem_inc(sem("window_ready"), 1)

            windows = v.value_load(wtab[0:1, 0:1], min_val=NG, max_val=MAXW)
            window(0)
            with v.Fori(0, windows) as it:
                v.wait_ge(sem("comb_ready"), it + 1)
                copy(comb_b, ps[:, 7, :].rearrange("p (j t) -> p j t", j=EG)).then_inc(sem("comb_copied"), 1)
                v.wait_ge(sem("comb_copied"), it + 1)
                v.sem_inc(sem("comb_read"), 1)
                for j in range(EG):
                    v.wait_ge(sem("sg_ready"), it * EG + (j + 1))
                    hj = hid[:, j % 2, :]
                    if j >= 2:
                        v.wait_ge(sem("down_done"), it * (2 * EG) + (2 * (j - 1)))
                    tt(hj, sg, ps[:, 4 + j % 2, :], ALU.mult)
                    v.drain()
                    v.sem_inc(sem("gate_read"), 1)
                    v.sem_inc(sem("sg_free"), 1)
                    tt(hj.rearrange("p (f t) -> p f t", f=4), hj.rearrange("p (f t) -> p f t", f=4),
                       comb_b[:, j, :].unsqueeze(1).to_broadcast([P, 4, W]), ALU.mult)
                    v.drain()
                    v.wait_ge(sem("up_ready"), it * EG + (j + 1))
                    tt(hj, hj, ps[:, 6, :], ALU.mult)
                    v.drain()
                    v.sem_inc(sem("up_read"), 1)
                    v.sem_inc(sem("hid_ready"), 1)
                window(it + 1)
                v.wait_ge(sem("down_done"), it * (2 * EG) + 2 * EG)
                yw = ys[:, :, ds(position(it), W)]
                tt(yw, yw, ps[:, 0:4, :].rearrange("p a (n t) -> p (a n) t", t=W), ALU.add)
                v.drain()
                v.sem_inc(sem("y_bank_free"), 1)
            v.sem_inc(reach("ys_ready"), 1)

            for k in range(KT):
                v.wait_ge(sem("y_summed"), k + 1)
                gated_add(k, k % 4, 5 * KT)
                v.sem_inc(sem("x3_ready"), 1)
            v.wait_ge(*step("ss3_ready"))
            tsc(ms[:, :], ps[:, 4, 0:T], 1.0 / D, EPS, ALU.mult, ALU.add).then_inc(reach("ms3_ready"), 1)
            v.wait_ge(*step("root3_ready"))
            nc.vector.reciprocal(rstd[:, :], ms[:, :])
            v.drain()
            for k in range(KT):
                stt(xT[:, k, :], xT[:, k, :], vcol[:, V_GF + k:V_GF + k + 1], rstd[:, :], ALU.mult, ALU.mult).then_inc(sem("xf_ready"), 1)
            for k in range(KT):
                v.wait_ge(sem("out_turned"), k + 1)
                copy(out_tok[:, 0:2, k * P:(k + 1) * P], ps[:, k % 4, 0:TP].rearrange("p (c n) -> p c n", c=2))
                copy(out_tok[0:TS, 2, k * P:(k + 1) * P], ps[0:TS, k % 4, TP:TP + P]).then_inc(sem("out_copied"), 1)


_INS = ["x_prompt", "x_sample", "cache_k", "cache_v", "cache_logf", "state_gla", "page_table", "c_prompt", "c_sample",
        "w_ada", "b_ada", "g_norm1", "g_norm2", "g_final", "w_in", "w_a2", "b_a", "b_f", "g_gla_norm", "w_up_a",
        "w_up_b", "w_out", "w_grp", "b_grp", "w_exp", "b_exp", "w_gate_e", "w_up_e", "w_down_e"]
_OUTS = [("y_prompt", (1, TP, D)), ("y_sample", (DB, DT, D)), ("k_prompt", (1, 1, TP, H_B, P)), ("v_prompt", (1, 1, TP, H_B, P)),
         ("logf_prompt", (1, 1, TP, H_B)), ("gla_prompt", (1, 1, H_A, P, DV)), ("k_sample", (1, DB, DT, H_B, P)),
         ("v_sample", (1, DB, DT, H_B, P)), ("logf_sample", (1, DB, DT, H_B)), ("gla_sample", (1, DB, H_A, P, DV))]


def kernel(**inputs):
    import numpy as _np
    import concourse.bacc as _bacc
    from concourse import mybir as _mybir
    from concourse.bass_utils import run_bass_kernel_spmd as _run

    nc = _bacc.Bacc("TRN2", target_bir_lowering=False, num_devices=1)
    arrays, io, out = {}, {}, {}
    for name in _INS:
        a = _np.ascontiguousarray(inputs[name])
        arrays[f"in_{name}_dram"] = a
        io[name] = nc.dram_tensor(f"in_{name}_dram", a.shape, _mybir.dt.from_np(a.dtype), kind="ExternalInput").ap()
    for name, shape in _OUTS:
        out[name] = nc.dram_tensor(f"out_{name}_dram", shape, _mybir.dt.float32, kind="ExternalOutput").ap()
    build(nc, io, out)
    r = _run(nc, [arrays], core_ids=[0])
    return tuple(r.results[0][f"out_{name}_dram"] for name, _ in _OUTS)
```
